# Optimizing a Trainium2 kernel written in Bass

```python
import math
import jax, jax.numpy as jnp
from jax import lax
import numpy as np
import jax
import jax.numpy as jnp

D_MODEL = 1024
BATCH = 1
SEQ = 256
DEPTH = 2

HEAD_DIM = 64
N_HEADS_A = D_MODEL // (2 * HEAD_DIM)
N_HEADS_B = D_MODEL // (2 * HEAD_DIM)
N_HEADS_C = D_MODEL // (2 * HEAD_DIM)
A_WIDTH = N_HEADS_A * HEAD_DIM
B_WIDTH = N_HEADS_B * HEAD_DIM
HYB_IN = 3 * A_WIDTH + 3 * B_WIDTH + N_HEADS_B
DIFF_QK = 2 * N_HEADS_C * HEAD_DIM
DIFF_V = N_HEADS_C * 2 * HEAD_DIM
D_FF = 2816
CONV_WIDTH = 3
ROPE_THETA = 10000.0
DILATED_PATTERNS = ((128, 1), (512, 4), (2048, 16))
BLOCK_Q = 128
NORM_EPS = 1e-6
SUBLN_EPS = 1e-5
N_EVEN = (DEPTH + 1) // 2
N_ODD = DEPTH // 2


def rms_norm(x, g, eps=NORM_EPS):
    xf = x.astype(jnp.float32)
    y = xf * lax.rsqrt(jnp.mean(xf * xf, axis=-1, keepdims=True) + eps)
    return (y * g.astype(jnp.float32)).astype(x.dtype)

def rope_tables(seq):
    inv = 1.0 / (ROPE_THETA ** (jnp.arange(0, HEAD_DIM, 2, dtype=jnp.float32) / HEAD_DIM))
    ang = jnp.arange(seq, dtype=jnp.float32)[:, None] * inv[None, :]
    ang = jnp.concatenate([ang, ang], axis=-1)
    return jnp.cos(ang)[None, :, None, :], jnp.sin(ang)[None, :, None, :]

def apply_rope(x, cos, sin):
    x1, x2 = jnp.split(x, 2, axis=-1)
    rot = jnp.concatenate([-x2, x1], axis=-1)
    return (x.astype(jnp.float32) * cos + rot.astype(jnp.float32) * sin).astype(x.dtype)

def local_window_attention(q, k, v, span):
    n, L, h, dh = q.shape
    nb = -(-L // BLOCK_Q)
    lp = nb * BLOCK_Q
    pad = lp - L
    padt = lambda t: jnp.pad(t, ((0, 0), (0, pad), (0, 0), (0, 0)))
    q, k, v = padt(q), padt(k), padt(v)

    def blocks_with_prev(t):
        te = jnp.pad(t, ((0, 0), (BLOCK_Q, 0), (0, 0), (0, 0)))
        prev = te[:, :lp].reshape(n, nb, BLOCK_Q, h, t.shape[-1])
        cur = te[:, BLOCK_Q:].reshape(n, nb, BLOCK_Q, h, t.shape[-1])
        return jnp.concatenate([prev, cur], axis=2)

    kb, vb = blocks_with_prev(k), blocks_with_prev(v)
    qb = q.reshape(n, nb, BLOCK_Q, h, dh)
    s = jnp.einsum('nbqhd,nbkhd->nbhqk', qb, kb, preferred_element_type=jnp.float32)
    i = jnp.arange(BLOCK_Q)[:, None]
    j = jnp.arange(2 * BLOCK_Q)[None, :]
    delta = i - j + BLOCK_Q
    band = (delta >= 0) & (delta <= span)
    blk = jnp.arange(nb)[:, None, None]
    valid = band[None] & (blk * BLOCK_Q - BLOCK_Q + j[None] >= 0)
    s = jnp.where(valid[None, :, None], s, -jnp.inf)
    m = jnp.max(s, axis=-1, keepdims=True)
    p = jnp.exp(s - m)
    denom = jnp.sum(p, axis=-1, keepdims=True)
    o = jnp.einsum('nbhqk,nbkhd->nbqhd', (p / denom).astype(v.dtype), vb)
    lse = (m + jnp.log(denom))[..., 0]
    lse = jnp.transpose(lse, (0, 1, 3, 2)).reshape(n, lp, h)[:, :L]
    o = o.reshape(n, lp, h, dh)[:, :L]
    return o, lse

def dilated_attention(q, k, v):
    b, s, h, dh = q.shape
    outs, lses = [], []
    for window, dil in DILATED_PATTERNS:
        L = s // dil

        def to_sub(t):
            t = t.reshape(b, L, dil, *t.shape[2:])
            return jnp.swapaxes(t, 1, 2).reshape(b * dil, L, *t.shape[3:])

        def from_sub(t):
            t = t.reshape(b, dil, L, *t.shape[2:])
            return jnp.swapaxes(t, 1, 2).reshape(b, s, *t.shape[3:])

        o, lse = local_window_attention(to_sub(q), to_sub(k), to_sub(v), window // dil)
        outs.append(from_sub(o))
        lses.append(from_sub(lse))
    alpha = jax.nn.softmax(jnp.stack(lses, axis=0), axis=0)
    out = jnp.sum(alpha[..., None] * jnp.stack(outs, axis=0).astype(jnp.float32), axis=0)
    return out.astype(q.dtype)

def to_blocks(t):
    b, s = t.shape[:2]
    return jnp.moveaxis(t.reshape(b, s // BLOCK_Q, BLOCK_Q, *t.shape[2:]), 1, 0)

def from_blocks(t):
    nb, b, bq = t.shape[:3]
    return jnp.moveaxis(t, 0, 1).reshape(b, nb * bq, *t.shape[3:])

def causal_block_probs(qb, k, q_start, bias=None):
    s = jnp.einsum('bqhd,bkhd->bhqk', qb, k, preferred_element_type=jnp.float32)
    if bias is not None:
        s = s + bias
    qpos = q_start + jnp.arange(qb.shape[1])
    kpos = jnp.arange(k.shape[1])
    s = jnp.where(kpos[None, :] <= qpos[:, None], s, -jnp.inf)
    return jax.nn.softmax(s, axis=-1)

def forgetting_attention(q, k, v, logf):
    c = jnp.cumsum(logf, axis=1)
    ck = jnp.transpose(c, (0, 2, 1))
    nb = q.shape[1] // BLOCK_Q

    def step(args):
        start, qb, cb = args
        bias = jnp.transpose(cb, (0, 2, 1))[..., :, None] - ck[:, :, None, :]
        p = causal_block_probs(qb, k, start, bias)
        return jnp.einsum('bhqk,bkhd->bqhd', p.astype(v.dtype), v)

    out = lax.map(step, (jnp.arange(nb) * BLOCK_Q, to_blocks(q), to_blocks(c)))
    return from_blocks(out)

def differential_attention(q1, q2, k1, k2, v, lam):
    nb = q1.shape[1] // BLOCK_Q

    def step(args):
        start, q1b, q2b = args
        a = causal_block_probs(q1b, k1, start) - lam * causal_block_probs(q2b, k2, start)
        return jnp.einsum('bhqk,bkhd->bqhd', a.astype(v.dtype), v)

    out = lax.map(step, (jnp.arange(nb) * BLOCK_Q, to_blocks(q1), to_blocks(q2)))
    return from_blocks(out)

def hybrid_mixer(n, w_in, b_f, w_out, cos, sin):
    b, s, _ = n.shape
    proj = n @ w_in
    cuts = [A_WIDTH, 2 * A_WIDTH, 3 * A_WIDTH,
            3 * A_WIDTH + B_WIDTH, 3 * A_WIDTH + 2 * B_WIDTH, 3 * A_WIDTH + 3 * B_WIDTH]
    qa, ka, va, qb, kb, vb, fb = jnp.split(proj, cuts, axis=-1)
    heads = lambda t: t.reshape(b, s, -1, HEAD_DIM)
    scale = HEAD_DIM ** -0.5
    oa = dilated_attention(apply_rope(heads(qa), cos, sin) * scale,
                           apply_rope(heads(ka), cos, sin), heads(va))
    logf = jax.nn.log_sigmoid((fb + b_f).astype(jnp.float32))
    ob = forgetting_attention(heads(qb) * scale, heads(kb), heads(vb), logf)
    o = jnp.concatenate([oa.reshape(b, s, A_WIDTH), ob.reshape(b, s, B_WIDTH)], axis=-1)
    return o @ w_out

def diff_mixer(n, w_qkv, lam_params, subln_g, w_out, cos, sin, layer_idx):
    b, s, _ = n.shape
    q, k, v = jnp.split(n @ w_qkv, [DIFF_QK, 2 * DIFF_QK], axis=-1)
    scale = HEAD_DIM ** -0.5
    q = (apply_rope(q.reshape(b, s, 2 * N_HEADS_C, HEAD_DIM), cos, sin) * scale).reshape(b, s, N_HEADS_C, 2, HEAD_DIM)
    k = apply_rope(k.reshape(b, s, 2 * N_HEADS_C, HEAD_DIM), cos, sin).reshape(b, s, N_HEADS_C, 2, HEAD_DIM)
    v = v.reshape(b, s, N_HEADS_C, 2 * HEAD_DIM)
    lam_init = 0.8 - 0.6 * math.exp(-0.3 * layer_idx)
    lp = lam_params.astype(jnp.float32)
    lam = jnp.exp(jnp.sum(lp[0] * lp[1])) - jnp.exp(jnp.sum(lp[2] * lp[3])) + lam_init
    o = differential_attention(q[:, :, :, 0], q[:, :, :, 1], k[:, :, :, 0], k[:, :, :, 1], v, lam)
    o = rms_norm(o, subln_g, SUBLN_EPS) * (1.0 - lam_init)
    return o.reshape(b, s, DIFF_V) @ w_out

def conv_glu_ffn(n, w_up, conv_w, conv_b, w_down):
    s = n.shape[1]
    gate, up = jnp.split(n @ w_up, 2, axis=-1)
    gp = jnp.pad(gate, ((0, 0), (CONV_WIDTH - 1, 0), (0, 0)))
    conv = conv_b
    for j in range(CONV_WIDTH):
        conv = conv + gp[:, j:j + s] * conv_w[j]
    return (jax.nn.silu(conv) * up) @ w_down

def first_inputs(seed: int = 0) -> dict:
    key = jax.random.key(seed)
    ks = jax.random.split(key, 20)
    nrm = lambda k, shape, fan_in: jax.random.normal(k, shape, jnp.float32) * fan_in ** -0.5
    return {
        "x": jax.random.normal(ks[0], (BATCH, SEQ, D_MODEL), jnp.float32),
        "attn_norm": 1.0 + 0.02 * jax.random.normal(ks[1], (DEPTH, D_MODEL), jnp.float32),
        "ffn_norm": 1.0 + 0.02 * jax.random.normal(ks[2], (DEPTH, D_MODEL), jnp.float32),
        "final_norm": 1.0 + 0.02 * jax.random.normal(ks[3], (D_MODEL,), jnp.float32),
        "hyb_w_in": nrm(ks[4], (N_EVEN, D_MODEL, HYB_IN), D_MODEL),
        "hyb_b_f": 2.0 + 0.5 * jax.random.normal(ks[5], (N_EVEN, N_HEADS_B), jnp.float32),
        "hyb_w_out": nrm(ks[6], (N_EVEN, A_WIDTH + B_WIDTH, D_MODEL), A_WIDTH + B_WIDTH),
        "diff_w_qkv": nrm(ks[7], (N_ODD, D_MODEL, 2 * DIFF_QK + DIFF_V), D_MODEL),
        "diff_lambda": 0.1 * jax.random.normal(ks[8], (N_ODD, 4, HEAD_DIM), jnp.float32),
        "diff_subln": 1.0 + 0.02 * jax.random.normal(ks[9], (N_ODD, 2 * HEAD_DIM), jnp.float32),
        "diff_w_out": nrm(ks[10], (N_ODD, DIFF_V, D_MODEL), DIFF_V),
        "ffn_w_up": nrm(ks[11], (DEPTH, D_MODEL, 2 * D_FF), D_MODEL),
        "ffn_conv_w": nrm(ks[12], (DEPTH, CONV_WIDTH, D_FF), CONV_WIDTH),
        "ffn_conv_b": 0.01 * jax.random.normal(ks[13], (DEPTH, D_FF), jnp.float32),
        "ffn_w_down": nrm(ks[14], (DEPTH, D_FF, D_MODEL), D_FF),
    }

def first_block(x, attn_norm, ffn_norm, final_norm, hyb_w_in, hyb_b_f, hyb_w_out,
              diff_w_qkv, diff_lambda, diff_subln, diff_w_out,
              ffn_w_up, ffn_conv_w, ffn_conv_b, ffn_w_down):
    cos, sin = rope_tables(x.shape[1])
    h = x
    for l in range(DEPTH):
        n = rms_norm(h, attn_norm[l])
        if l % 2 == 0:
            e = l // 2
            h = h + hybrid_mixer(n, hyb_w_in[e], hyb_b_f[e], hyb_w_out[e], cos, sin)
        else:
            o = l // 2
            h = h + diff_mixer(n, diff_w_qkv[o], diff_lambda[o], diff_subln[o], diff_w_out[o], cos, sin, l)
        h = h + conv_glu_ffn(rms_norm(h, ffn_norm[l]), ffn_w_up[l], ffn_conv_w[l], ffn_conv_b[l], ffn_w_down[l])
    return rms_norm(h, final_norm)


GRID_W = 64
CTX_LEN = 256
N_EVEN_2 = (DEPTH + 1) // 2
N_ODD_2 = DEPTH // 2
BLK = 128
A_HEADS = 4
A_DIM = 128
A_WIDTH_2 = A_HEADS * A_DIM
A_CHUNK = 64
B_HEADS = 8
B_KV = 2
B_WIN = 128
C_HEADS = 8
C_KV = 2
D_HEADS = 8
NA_ROWS = 8
NA_COLS = 16
MIX_WIDTH = A_WIDTH_2 + B_HEADS * HEAD_DIM
EPS = 1e-6
NEG = -1e30
EVEN_SPLITS = (A_WIDTH_2, A_WIDTH_2, A_WIDTH_2, A_WIDTH_2, 4 * A_HEADS, B_HEADS * HEAD_DIM, B_KV * HEAD_DIM, B_KV * HEAD_DIM)
ODD_SPLITS = (C_HEADS * HEAD_DIM, C_KV * HEAD_DIM, C_KV * HEAD_DIM, D_HEADS * HEAD_DIM, D_HEADS * HEAD_DIM, D_HEADS * HEAD_DIM)
EVEN_COLS = sum(EVEN_SPLITS)
ODD_COLS = sum(ODD_SPLITS)


f32 = jnp.float32

def split_cols(u, sizes):
    return jnp.split(u, np.cumsum(sizes)[:-1].tolist(), axis=-1)

def heads(a, n):
    return a.reshape(a.shape[:-1] + (n, a.shape[-1] // n))

def group(q, n_kv):
    return q.reshape(q.shape[:2] + (n_kv, q.shape[2] // n_kv, q.shape[3]))

def rms_norm_2(x, g):
    xf = x.astype(f32)
    y = xf * lax.rsqrt(jnp.mean(xf * xf, axis=-1, keepdims=True) + EPS)
    return (y * g.astype(f32)).astype(x.dtype)

def modulate(x, g, shift, scale):
    return rms_norm_2(x, g) * (1 + scale) + shift

def axial_rope(n):
    t = jnp.arange(n)
    row = (t // GRID_W).astype(f32)
    col = (t % GRID_W).astype(f32)
    half = HEAD_DIM // 2
    freq = ROPE_THETA ** (-jnp.arange(0, half, 2, dtype=f32) / half)
    ang_r = row[:, None] * freq[None, :]
    ang_c = col[:, None] * freq[None, :]
    ang = jnp.concatenate([ang_r, ang_r, ang_c, ang_c], axis=-1)
    return jnp.cos(ang), jnp.sin(ang)

def apply_rope_2(x, cos, sin):
    xr = x.reshape(x.shape[:-1] + (2, 2, HEAD_DIM // 4))
    rot = jnp.stack([-xr[..., 1, :], xr[..., 0, :]], axis=-2).reshape(x.shape)
    return x * cos[:, None, :].astype(x.dtype) + rot * sin[:, None, :].astype(x.dtype)

def qk_prep(a, g, rope, scale=1.0):
    a = rms_norm_2(a, g)
    if rope is not None:
        a = apply_rope_2(a, rope[0], rope[1])
    return a * scale

def joint_softmax(parts):
    sizes = [p.shape[-1] for p in parts]
    logits = jnp.concatenate([p.astype(f32) for p in parts], axis=-1)
    probs = jax.nn.softmax(logits, axis=-1)
    return jnp.split(probs, np.cumsum(sizes)[:-1].tolist(), axis=-1)

def sink_column(sink, scores):
    hkv, g = scores.shape[-4], scores.shape[-3]
    return jnp.broadcast_to(sink.astype(f32).reshape(hkv, g, 1, 1), scores.shape[:-1] + (1,))

def context_attention(q, k, v, sink=None):
    s = jnp.einsum('bqhgd,bkhd->bhgqk', q, k).astype(f32)
    if sink is None:
        p = jax.nn.softmax(s, axis=-1)
    else:
        _, p = joint_softmax([sink_column(sink, s), s])
    o = jnp.einsum('bhgqk,bkhd->bqhgd', p.astype(v.dtype), v)
    return o.reshape(o.shape[:2] + (-1,))

def window_attention(q, k, v, k_ctx, v_ctx, sink):
    B, S, Hkv, G, d = q.shape
    nb = S // BLK
    qb = q.reshape(B, nb, BLK, Hkv, G, d)

    def band(a):
        ap = jnp.pad(a, ((0, 0), (BLK, BLK), (0, 0), (0, 0))).reshape(B, nb + 2, BLK, Hkv, d)
        return jnp.concatenate([ap[:, :-2], ap[:, 1:-1], ap[:, 2:]], axis=2)

    kb, vb = band(k), band(v)
    t_pos = jnp.arange(S).reshape(nb, BLK)
    s_pos = jnp.arange(nb)[:, None] * BLK - BLK + jnp.arange(3 * BLK)[None, :]
    sp = s_pos[:, None, :]
    valid = (sp >= 0) & (sp < S) & (jnp.abs(t_pos[:, :, None] - sp) <= B_WIN)
    s_band = jnp.einsum('bnqhgd,bnkhd->bnhgqk', qb, kb).astype(f32)
    s_band = jnp.where(valid[:, None, None, :, :], s_band, NEG)
    s_ctx = jnp.einsum('bnqhgd,bchd->bnhgqc', qb, k_ctx)
    _, p_ctx, p_band = joint_softmax([sink_column(sink, s_band), s_ctx, s_band])
    o = (jnp.einsum('bnhgqc,bchd->bnqhgd', p_ctx.astype(v.dtype), v_ctx)
         + jnp.einsum('bnhgqk,bnkhd->bnqhgd', p_band.astype(v.dtype), vb))
    return o.reshape(B, S, Hkv * G * d)

def global_attention(q, k, v, k_ctx, v_ctx):
    B, S, Hkv, G, d = q.shape
    nb = S // BLK
    kk = jnp.concatenate([k_ctx, k], axis=1)
    vv = jnp.concatenate([v_ctx, v], axis=1)

    def one_block(qi):
        s = jnp.einsum('bqhgd,bkhd->bhgqk', qi, kk).astype(f32)
        p = jax.nn.softmax(s, axis=-1).astype(vv.dtype)
        return jnp.einsum('bhgqk,bkhd->bqhgd', p, vv)

    qb = jnp.moveaxis(q.reshape(B, nb, BLK, Hkv, G, d), 1, 0)
    o = lax.map(one_block, qb)
    return jnp.moveaxis(o, 0, 1).reshape(B, S, Hkv * G * d)

def neighbourhood_attention(q, k, v, k_ctx, v_ctx, rpb):
    B, S, H, d = q.shape
    rows = S // GRID_W
    wr = min(NA_ROWS, rows)
    r = jnp.arange(rows)
    row_idx = jnp.clip(r - wr // 2, 0, rows - wr)[:, None] + jnp.arange(wr)[None, :]
    col = jnp.arange(GRID_W)
    col_start = jnp.clip(col - NA_COLS // 2, 0, GRID_W - NA_COLS)
    col_ok = (col[None, :] >= col_start[:, None]) & (col[None, :] < col_start[:, None] + NA_COLS)

    def gather_rows(a):
        return a.reshape(B, rows, GRID_W, H, d)[:, row_idx].reshape(B, rows, wr * GRID_W, H, d)

    kg, vg = gather_rows(k), gather_rows(v)
    dr = row_idx - r[:, None] + NA_ROWS - 1
    dc = jnp.clip(col[None, :] - col[:, None] + NA_COLS - 1, 0, 2 * NA_COLS - 2)
    bias = rpb[:, dr[:, None, :, None], dc[None, :, None, :]].astype(f32)
    bias = jnp.where(col_ok[None, None, :, None, :], bias, NEG).reshape(H, rows, GRID_W, wr * GRID_W)
    qg = q.reshape(B, rows, GRID_W, H, d)
    s_nb = jnp.einsum('brqhd,brkhd->bhrqk', qg, kg).astype(f32) + bias
    s_ctx = jnp.einsum('brqhd,bchd->bhrqc', qg, k_ctx)
    p_ctx, p_nb = joint_softmax([s_ctx, s_nb])
    o = (jnp.einsum('bhrqc,bchd->brqhd', p_ctx.astype(v.dtype), v_ctx)
         + jnp.einsum('bhrqk,brkhd->brqhd', p_nb.astype(v.dtype), vg))
    return o.reshape(B, S, H * d)

def mlstm_scan(q, k, v, log_i, log_f, state):
    B, H, T, dh = q.shape
    nc = T // A_CHUNK

    def to_chunks(a):
        return jnp.moveaxis(a.reshape(a.shape[:2] + (nc, A_CHUNK) + a.shape[3:]), 2, 0)

    xs = (to_chunks(q), to_chunks(k), to_chunks(v), to_chunks(log_i), to_chunks(log_f))
    tri = jnp.tril(jnp.ones((A_CHUNK, A_CHUNK), dtype=bool))

    def step(carry, inp):
        C, n, m = carry
        qc, kc, vc, li, lf = inp
        b = jnp.cumsum(lf, axis=-1)
        dmat = jnp.where(tri, b[..., :, None] - b[..., None, :] + li[..., None, :], -jnp.inf)
        inter = b + m[..., None]
        m_t = jnp.maximum(inter, jnp.max(dmat, axis=-1))
        w = jnp.exp(dmat - m_t[..., None])
        a = jnp.exp(inter - m_t)
        s = jnp.einsum('bhtd,bhsd->bhts', qc, kc) * w
        num = a[..., None] * jnp.einsum('bhtd,bhde->bhte', qc, C) + jnp.einsum('bhts,bhse->bhte', s, vc)
        den = a * jnp.einsum('bhtd,bhd->bht', qc, n) + jnp.sum(s, axis=-1)
        h = num / jnp.maximum(jnp.abs(den), jnp.exp(-m_t))[..., None]
        b_last = b[..., -1]
        g = b_last[..., None] - b + li
        m_new = jnp.maximum(b_last + m, jnp.max(g, axis=-1))
        decay = jnp.exp(b_last + m - m_new)
        wk = jnp.exp(g - m_new[..., None])[..., None] * kc
        C_new = decay[..., None, None] * C + jnp.einsum('bhsd,bhse->bhde', wk, vc)
        n_new = decay[..., None] * n + jnp.sum(wk, axis=2)
        return (C_new, n_new, m_new), h

    state, hs = lax.scan(step, state, xs)
    return jnp.moveaxis(hs, 0, 2).reshape(B, H, T, dh), state

def mlstm_prep(q, k, v, gates, gate_b):
    to_h = lambda a: jnp.swapaxes(heads(a.astype(f32), A_HEADS), 1, 2)
    g = (gates.astype(f32) + gate_b.astype(f32)).reshape(gates.shape[:2] + (4, A_HEADS))
    g = jnp.transpose(g, (2, 0, 3, 1))
    return (to_h(q), to_h(k) * A_DIM ** -0.5, to_h(v),
            g[0], jax.nn.log_sigmoid(g[1]), g[2], jax.nn.log_sigmoid(g[3]))

def mlstm_bidirectional(ctx_s, lat_s):
    qc, kc, vc, icf, fcf, icb, fcb = ctx_s
    ql, kl, vl, ilf, flf, ilb, flb = lat_s
    b = qc.shape[0]
    zero = (jnp.zeros((b, A_HEADS, A_DIM, A_DIM), f32), jnp.zeros((b, A_HEADS, A_DIM), f32), jnp.zeros((b, A_HEADS), f32))
    flip = lambda a: jnp.flip(a, axis=2)
    hcf, st_f = mlstm_scan(qc, kc, vc, icf, fcf, zero)
    hlf, _ = mlstm_scan(ql, kl, vl, ilf, flf, st_f)
    hcb, st_b = mlstm_scan(flip(qc), flip(kc), flip(vc), flip(icb), flip(fcb), zero)
    hlb, _ = mlstm_scan(flip(ql), flip(kl), flip(vl), flip(ilb), flip(flb), st_b)
    return hcf + flip(hcb), hlf + flip(hlb)

def mlstm_out(h, o, head_g, dtype):
    h = rms_norm_2(jnp.swapaxes(h, 1, 2), head_g.reshape(A_HEADS, A_DIM))
    return (jax.nn.sigmoid(o.astype(f32)) * h.reshape(h.shape[:2] + (A_WIDTH_2,))).astype(dtype)

def even_mixer(hc, hl, w_in, gate_b, head_g, qk_g, sink, rope, need_ctx):
    aq_l, ak_l, av_l, ao_l, ag_l, bq_l, bk_l, bv_l = split_cols(hl @ w_in, EVEN_SPLITS)
    aq_c, ak_c, av_c, ao_c, ag_c, bq_c, bk_c, bv_c = split_cols(hc @ w_in, EVEN_SPLITS)
    h_ctx, h_lat = mlstm_bidirectional(mlstm_prep(aq_c, ak_c, av_c, ag_c, gate_b),
                                       mlstm_prep(aq_l, ak_l, av_l, ag_l, gate_b))
    scale = HEAD_DIM ** -0.5
    k_c = qk_prep(heads(bk_c, B_KV), qk_g[1], None)
    v_c = heads(bv_c, B_KV)
    q_l = qk_prep(heads(bq_l, B_HEADS), qk_g[0], rope, scale)
    k_l = qk_prep(heads(bk_l, B_KV), qk_g[1], rope)
    b_lat = window_attention(group(q_l, B_KV), k_l, heads(bv_l, B_KV), k_c, v_c, sink)
    lat = jnp.concatenate([mlstm_out(h_lat, ao_l, head_g, hl.dtype), b_lat], axis=-1)
    if not need_ctx:
        return None, lat
    q_c = qk_prep(heads(bq_c, B_HEADS), qk_g[0], None, scale)
    b_ctx = context_attention(group(q_c, B_KV), k_c, v_c, sink)
    ctx_out = jnp.concatenate([mlstm_out(h_ctx, ao_c, head_g, hc.dtype), b_ctx], axis=-1)
    return ctx_out, lat

def odd_mixer(hc, hl, w_in, gqa_g, na_g, rpb, rope, need_ctx):
    cq_l, ck_l, cv_l, nq_l, nk_l, nv_l = split_cols(hl @ w_in, ODD_SPLITS)
    cq_c, ck_c, cv_c, nq_c, nk_c, nv_c = split_cols(hc @ w_in, ODD_SPLITS)
    scale = HEAD_DIM ** -0.5
    gk_c = qk_prep(heads(ck_c, C_KV), gqa_g[1], None)
    gv_c = heads(cv_c, C_KV)
    dk_c = qk_prep(heads(nk_c, D_HEADS), na_g[1], None)
    dv_c = heads(nv_c, D_HEADS)
    gq_l = qk_prep(heads(cq_l, C_HEADS), gqa_g[0], rope, scale)
    gk_l = qk_prep(heads(ck_l, C_KV), gqa_g[1], rope)
    c_lat = global_attention(group(gq_l, C_KV), gk_l, heads(cv_l, C_KV), gk_c, gv_c)
    dq_l = qk_prep(heads(nq_l, D_HEADS), na_g[0], None, scale)
    dk_l = qk_prep(heads(nk_l, D_HEADS), na_g[1], None)
    d_lat = neighbourhood_attention(dq_l, dk_l, heads(nv_l, D_HEADS), dk_c, dv_c, rpb)
    lat = jnp.concatenate([c_lat, d_lat], axis=-1)
    if not need_ctx:
        return None, lat
    gq_c = qk_prep(heads(cq_c, C_HEADS), gqa_g[0], None, scale)
    dq_c = qk_prep(heads(nq_c, D_HEADS), na_g[0], None, scale)
    ctx_out = jnp.concatenate([context_attention(group(gq_c, C_KV), gk_c, gv_c),
                               context_attention(dq_c[:, :, :, None, :], dk_c, dv_c)], axis=-1)
    return ctx_out, lat

def conv_ffn(h, w_up, conv_w, conv_b, w_down):
    u = h @ w_up
    u = lax.conv_general_dilated(u, conv_w[:, None, :].astype(u.dtype), window_strides=(1,), padding=((1, 1),),
                                 dimension_numbers=('NWC', 'WIO', 'NWC'), feature_group_count=u.shape[-1]) + conv_b
    gate, val = jnp.split(u, 2, axis=-1)
    return (jax.nn.silu(gate) * val) @ w_down

def second_inputs(seed: int = 0) -> dict:
    key = jax.random.key(seed)
    ks = jax.random.split(key, 24)
    nrm = lambda k, shape, s: jax.random.normal(k, shape, f32) * s
    D = D_MODEL
    gk = jax.random.split(ks[13], 4)
    mlstm_gate_b = jnp.concatenate([
        nrm(gk[0], (N_EVEN_2, A_HEADS), 0.1),
        3.0 + 3.0 * jax.random.uniform(gk[1], (N_EVEN_2, A_HEADS), f32),
        nrm(gk[2], (N_EVEN_2, A_HEADS), 0.1),
        3.0 + 3.0 * jax.random.uniform(gk[3], (N_EVEN_2, A_HEADS), f32)], axis=-1)
    return {
        'x': nrm(ks[0], (BATCH, SEQ, D), 1.0),
        'c': nrm(ks[1], (BATCH, D), 1.0),
        'ctx': nrm(ks[2], (BATCH, CTX_LEN, D), 1.0),
        'c_ctx': nrm(ks[3], (D,), 1.0),
        'ada_w': nrm(ks[4], (DEPTH, D, 6 * D), 0.3 * D ** -0.5),
        'ada_b': nrm(ks[5], (DEPTH, 6 * D), 0.02),
        'norm_g': 1.0 + nrm(ks[6], (DEPTH, 2, D), 0.02),
        'w_out': nrm(ks[7], (DEPTH, MIX_WIDTH, D), MIX_WIDTH ** -0.5),
        'ffn_up': nrm(ks[8], (DEPTH, D, 2 * D_FF), D ** -0.5),
        'ffn_conv_w': nrm(ks[9], (DEPTH, 3, 2 * D_FF), 3 ** -0.5),
        'ffn_conv_b': nrm(ks[10], (DEPTH, 2 * D_FF), 0.02),
        'ffn_down': nrm(ks[11], (DEPTH, D_FF, D), D_FF ** -0.5),
        'even_w_in': nrm(ks[12], (N_EVEN_2, D, EVEN_COLS), D ** -0.5),
        'mlstm_gate_b': mlstm_gate_b,
        'mlstm_head_g': 1.0 + nrm(ks[14], (N_EVEN_2, A_WIDTH_2), 0.02),
        'swa_qk_g': 1.0 + nrm(ks[15], (N_EVEN_2, 2, HEAD_DIM), 0.02),
        'swa_sink': nrm(ks[16], (N_EVEN_2, B_HEADS), 0.5),
        'odd_w_in': nrm(ks[17], (N_ODD_2, D, ODD_COLS), D ** -0.5),
        'gqa_qk_g': 1.0 + nrm(ks[18], (N_ODD_2, 2, HEAD_DIM), 0.02),
        'na_qk_g': 1.0 + nrm(ks[19], (N_ODD_2, 2, HEAD_DIM), 0.02),
        'na_rpb': nrm(ks[20], (N_ODD_2, D_HEADS, 2 * NA_ROWS - 1, 2 * NA_COLS - 1), 0.5),
    }

def second_block(x, c, ctx, c_ctx, ada_w, ada_b, norm_g, w_out, ffn_up, ffn_conv_w, ffn_conv_b, ffn_down,
              even_w_in, mlstm_gate_b, mlstm_head_g, swa_qk_g, swa_sink,
              odd_w_in, gqa_qk_g, na_qk_g, na_rpb):
    rope = axial_rope(x.shape[1])
    x_lat, x_ctx = x, ctx
    for l in range(DEPTH):
        need_ctx = l < DEPTH - 1
        mod_l = jnp.split((jax.nn.silu(c) @ ada_w[l] + ada_b[l])[:, None, :], 6, axis=-1)
        mod_c = jnp.split((jax.nn.silu(c_ctx) @ ada_w[l] + ada_b[l])[None, None, :], 6, axis=-1)
        hl = modulate(x_lat, norm_g[l, 0], mod_l[0], mod_l[1])
        hc = modulate(x_ctx, norm_g[l, 0], mod_c[0], mod_c[1])
        if l % 2 == 0:
            e = l // 2
            mix_c, mix_l = even_mixer(hc, hl, even_w_in[e], mlstm_gate_b[e], mlstm_head_g[e],
                                      swa_qk_g[e], swa_sink[e], rope, need_ctx)
        else:
            o = l // 2
            mix_c, mix_l = odd_mixer(hc, hl, odd_w_in[o], gqa_qk_g[o], na_qk_g[o], na_rpb[o], rope, need_ctx)
        x_lat = x_lat + mod_l[2] * (mix_l @ w_out[l])
        x_lat = x_lat + mod_l[5] * conv_ffn(modulate(x_lat, norm_g[l, 1], mod_l[3], mod_l[4]),
                                            ffn_up[l], ffn_conv_w[l], ffn_conv_b[l], ffn_down[l])
        if need_ctx:
            x_ctx = x_ctx + mod_c[2] * (mix_c @ w_out[l])
            x_ctx = x_ctx + mod_c[5] * conv_ffn(modulate(x_ctx, norm_g[l, 1], mod_c[3], mod_c[4]),
                                                ffn_up[l], ffn_conv_w[l], ffn_conv_b[l], ffn_down[l])
    return x_lat


def setup_inputs(seed=0):
    out = dict(first_inputs(seed))
    for name, value in second_inputs(seed + 1).items():
        if name != "x":
            out[name + "_2"] = value
    return out


def reference(
    x, attn_norm, ffn_norm, final_norm, hyb_w_in, hyb_b_f, hyb_w_out, diff_w_qkv, diff_lambda,
    diff_subln, diff_w_out, ffn_w_up, ffn_conv_w, ffn_conv_b, ffn_w_down, c_2, ctx_2, c_ctx_2,
    ada_w_2, ada_b_2, norm_g_2, w_out_2, ffn_up_2, ffn_conv_w_2, ffn_conv_b_2, ffn_down_2,
    even_w_in_2, mlstm_gate_b_2, mlstm_head_g_2, swa_qk_g_2, swa_sink_2, odd_w_in_2, gqa_qk_g_2,
    na_qk_g_2, na_rpb_2,
):
    x = first_block(
        x, attn_norm, ffn_norm, final_norm, hyb_w_in, hyb_b_f, hyb_w_out, diff_w_qkv,
        diff_lambda, diff_subln, diff_w_out, ffn_w_up, ffn_conv_w, ffn_conv_b, ffn_w_down,
    )
    return second_block(
        x, c_2, ctx_2, c_ctx_2, ada_w_2, ada_b_2, norm_g_2, w_out_2, ffn_up_2, ffn_conv_w_2,
        ffn_conv_b_2, ffn_down_2, even_w_in_2, mlstm_gate_b_2, mlstm_head_g_2, swa_qk_g_2,
        swa_sink_2, odd_w_in_2, gqa_qk_g_2, na_qk_g_2, na_rpb_2,
    )


_drawn_inputs = setup_inputs


def setup_inputs(seed=0):
    import zlib

    import numpy as np

    out = dict(_drawn_inputs(seed))
    spreads = {}
    factors = {'final_norm': 2.917,
     'diff_subln': 4.789,
     'ffn_conv_b': 7.195,
     'norm_g_2': 8.0,
     'ffn_conv_b_2': 8.0,
     'mlstm_head_g_2': 22.856,
     'swa_qk_g_2': 8.0,
     'swa_sink_2': 8.0,
     'gqa_qk_g_2': 8.0,
     'na_qk_g_2': 8.0,
     'na_rpb_2': 21.46}
    for name, (base, spread) in spreads.items():
        noise = np.random.default_rng([zlib.crc32(name.encode()), seed]).standard_normal(out[name].shape)
        drawn = base * np.exp(spread * noise) if base else spread * noise
        out[name] = jnp.asarray(drawn.astype(out[name].dtype))
    for name, factor in factors.items():
        out[name] = (out[name] * factor).astype(out[name].dtype)
    return out
```

```python
import math
from contextlib import ExitStack

import numpy as np
import concourse.bass as bass
from concourse import mybir

ALU = mybir.AluOpType
ACT = mybir.ActivationFunctionType
F32 = mybir.dt.float32
AX_X = mybir.AxisListType.X

P = 128
D = 1024
KT = D // P
DH = 64
NH = 8
FF = 2816
FC = FF // P
SEQ = 256
TT = 4
CTX, LAT, ALL = (0, 1), (2, 3), (0, 1, 2, 3)
MH, MD = 4, 128
SLOTS = 4
SLOT = 2048
BIG_N = 4 * 2832
BIG_NEG = 1e30
LAM_INIT = 0.8 - 0.6 * math.exp(-0.3 * 1)
EPS, SUB_EPS = 1e-6, 1e-5

WIDTHS = dict(ident=128, negflip=128, dilated=512, causal=256, window=1024, nbhood=512, later=128, earlier=128,
              pick8=1024, pick2=256, cos1=128, sin1=128, cos2=128, sin2=128)
AT = {}
_n = 0
for _k, _w in WIDTHS.items():
    AT[_k] = (_n, _w)
    _n += _w
NCONST = _n


def constants():
    c = {k: np.zeros((P, w), np.float32) for k, w in WIDTHS.items()}
    c["ident"][:] = np.eye(P)
    c["negflip"][:] = -np.eye(P)[::-1]
    t = np.arange(SEQ)
    delta = t[:, None] - t[None, :]
    count = ((delta >= 0) & (delta <= 128)).astype(int) + ((delta >= 0) & (delta % 4 == 0)) + ((delta >= 0) & (delta % 16 == 0))
    dil = np.where(count > 0, -np.log(np.maximum(count, 1)), BIG_NEG).astype(np.float32)
    c["dilated"][:] = dil.reshape(2, P, SEQ).transpose(1, 0, 2).reshape(P, -1)
    p = np.arange(P)
    c["causal"][:, P:] = np.where(p[None, :] > p[:, None], BIG_NEG, 0)
    win = np.where(np.abs(delta) <= 128, 0, BIG_NEG).astype(np.float32).reshape(2, P, SEQ)
    w = c["window"].reshape(P, 2, 512)
    w[:, :, SEQ:] = win.transpose(1, 0, 2)
    col = np.arange(64)
    first = np.clip(col - 8, 0, 48)
    ok = (col[None, :] >= first[:, None]) & (col[None, :] < first[:, None] + 16)
    c["nbhood"][:, SEQ:] = np.tile(np.where(ok, 0, BIG_NEG), (2, 4))
    c["later"][:] = np.where(p[:, None] > p[None, :], -BIG_NEG, 0)
    c["earlier"][:] = np.where(p[:, None] < p[None, :], -BIG_NEG, 0)
    for h in range(8):
        c["pick8"][h, h * P:(h + 1) * P] = 1
    for j in range(4):
        for s in range(2):
            c["pick2"][32 * j + s, s * P:(s + 1) * P] = 1
    f = np.float32
    inv = (1.0 / (f(10000.0) ** (np.arange(0, DH, 2, dtype=f) / f(DH)))).astype(f)
    ang = np.arange(SEQ, dtype=f)[:, None] * inv[None, :]
    ang = np.concatenate([ang, ang], -1)
    sgn = np.where(np.arange(DH) < DH // 2, -1, 1).astype(f)
    tile = lambda a: a.astype(f).reshape(2, P, DH).transpose(1, 0, 2).reshape(P, -1)
    c["cos1"][:], c["sin1"][:] = tile(np.cos(ang)), tile(np.sin(ang) * sgn)
    freq = (f(10000.0) ** (-np.arange(0, 32, 2, dtype=f) / f(32))).astype(f)
    r = (t // 64).astype(f)[:, None] * freq[None, :]
    k = (t % 64).astype(f)[:, None] * freq[None, :]
    ang = np.concatenate([r, r, k, k], -1)
    sgn = np.where(np.arange(DH) % 32 < 16, -1, 1).astype(f)
    c["cos2"][:], c["sin2"][:] = tile(np.cos(ang)), tile(np.sin(ang) * sgn)
    return np.ascontiguousarray(np.concatenate([c[k] for k in WIDTHS], 1))


class Progress:

    def __init__(self, name, eng, sem, noted):
        self.name, self.eng, self.sem, self.noted, self.n = name, eng, sem, noted, 0

    def one(self, step=None):
        self.n += 1
        if step is not None:
            self.note(step)
        return 1

    def note(self, step):
        self.noted[step] = self.n


def program(nc, io, out, known, noted, debug=None):
    with ExitStack() as ctx:
        def sb(name, width, rows=P):
            return ctx.enter_context(nc.sbuf_tensor(name, [rows, width], F32))

        ring = sb("ring", SLOTS * SLOT)
        x_t = sb("x_tokens", TT * D)
        nt = sb("normed_features", KT * 512)
        big = sb("big", BIG_N)
        qkt = sb("qk_features", 7168)
        work = sb("work", 4608)
        gate = sb("gate_rows", 2048)
        con = sb("con", NCONST)
        final_g = sb("final_g", D)
        head_g = sb("head_g", 512)
        sub_g = sb("sub_g", P)
        qk_g = sb("qk_g", 3 * P)
        sink = sb("sink", NH)
        nsink = sb("nsink", NH)
        lam_in = sb("lam_in", 256)
        lam = sb("lam", 8)
        veccol = sb("veccol", 80)
        convcol = sb("convcol", 6 * 88)
        mod = sb("mod", 3 * 512)
        modcol = sb("modcol", 64)
        acol = sb("acol", 2 * 16)
        gbias = sb("gbias", 4)
        fbias = sb("fbias", 1)
        ones = sb("ones", 1)
        stat = sb("stat", 64)
        mxs = sb("mxs", 3 * 4)
        mcol = sb("mcol", 64)
        st2 = sb("st2", 128)
        rms = sb("rms", 96)
        psum = [ctx.enter_context(nc.psum_tensor(f"bank{i}", [P, 512], F32)) for i in range(8)]

        def sem(name):
            return ctx.enter_context(nc.semaphore(name))

        tensor_done, vector_done, scalar_done, gpsimd_done = sem("tensor_done"), sem("vector_done"), sem("scalar_done"), sem("gpsimd_done")
        slot_full = [sem(f"slot{i}_full") for i in range(SLOTS)]
        loaded = sem("small_inputs_loaded")
        bias_in = sem("neighbour_bias_loaded")
        adab_in = sem("ada_bias_loaded")
        stored = sem("output_stored")
        SEM = {"T": tensor_done, "V": vector_done, "A": scalar_done, "G": gpsimd_done}

        def done(*step):
            return known.get(step, 0)

        def const(name, a=0, b=None, rows=slice(0, P)):
            o, w = AT[name]
            return con[rows, o + a:o + (w if b is None else b)]

        ident = const("ident")
        xt = x_t[:, :].rearrange("p (t d) -> p t d", t=TT)
        nT = nt[:, :].rearrange("p (k t) -> p k t", k=KT)
        wslot = ring[:, :].rearrange("p (s n) -> p s n", s=SLOTS)

        stream = []

        def add_proj(w, cuts):
            for a, b in cuts:
                for half in range(2):
                    src = w[half * 512:half * 512 + 512, a:b].rearrange("(k p) n -> p k n", p=P)
                    stream.append((src, lambda s, n=b - a: s.rearrange("p (k n) -> p k n", k=4)[:, :, 0:n]))

        def cuts_of(n):
            return [(a, min(a + 512, n)) for a in range(0, n, 512)]

        HYB_CUTS = cuts_of(3080)
        QKV_CUTS = cuts_of(3072)
        OUT_CUTS = cuts_of(1024)
        EVEN_CUTS = cuts_of(2832)
        ODD_CUTS = [(0, 512), (512, 768), (768, 1280), (1280, 1792), (1792, 2304)]

        def add_ada(w):
            for g in range(3):
                for k in range(KT):
                    stream.append((w[k * P:(k + 1) * P, g * 2048:(g + 1) * 2048], lambda s: s))

        def add_up(w):
            for f in range(FC):
                src = w.rearrange("(k p) (u f c) -> p u k f c", p=P, u=2, c=P)[:, :, :, f, :]
                stream.append((src, lambda s: s.rearrange("p (u k c) -> p u k c", u=2, c=P)))

        def add_down_rows(w):
            for f in range(0, FC, 2):
                stream.append((w[f * P:(f + 2) * P, :].rearrange("(c p) n -> p c n", p=P),
                               lambda s: s.rearrange("p (c n) -> p c n", c=2)))

        def add_down_halves(w):
            for half in range(2):
                for f in range(0, FC, 4):
                    m = min(4, FC - f)
                    stream.append((w[f * P:(f + m) * P, half * 512:half * 512 + 512].rearrange("(c p) n -> p c n", p=P),
                                   lambda s, m=m: s.rearrange("p (c n) -> p c n", c=4)[:, 0:m, :]))

        add_proj(io["hyb_w_in"][0], HYB_CUTS)
        add_proj(io["hyb_w_out"][0], OUT_CUTS)
        add_up(io["ffn_w_up"][0]); add_down_rows(io["ffn_w_down"][0])
        add_proj(io["diff_w_qkv"][0], QKV_CUTS)
        add_proj(io["diff_w_out"][0], OUT_CUTS)
        add_up(io["ffn_w_up"][1]); add_down_rows(io["ffn_w_down"][1])
        add_ada(io["ada_w_2"][0])
        add_proj(io["even_w_in_2"][0], EVEN_CUTS)
        add_proj(io["w_out_2"][0], OUT_CUTS)
        add_up(io["ffn_up_2"][0]); add_down_halves(io["ffn_down_2"][0])
        add_ada(io["ada_w_2"][1])
        add_proj(io["odd_w_in_2"][0], ODD_CUTS)
        add_proj(io["w_out_2"][1], OUT_CUTS)
        add_up(io["ffn_up_2"][1]); add_down_rows(io["ffn_down_2"][1])


        class Taken:
            n = 0

        def take(T):
            u = Taken.n
            Taken.n += 1
            T.eng.wait_ge(slot_full[u % SLOTS], 16 * (u // SLOTS + 1))
            return wslot[:, u % SLOTS, :], ("T", "slot", u)

        def fence(E, phase):
            for o in "TVAG":
                if o != E.name:
                    E.eng.wait_ge(SEM[o], done(o, "end", phase))

        XN = [work[:, 0:1024], work[:, 1024:2048], work[:, 2048:3072], work[:, 3072:4096]]

        def norm_A(A, ph, tiles):
            n = len(tiles)
            for j, t in enumerate(tiles):
                A.eng.wait_ge(scalar_done, A.n)
                A.eng.activation(gate[:, 0:D], xt[:, t, :], ACT.Square, scale=D ** -0.5,
                                        accum_out=stat[:, j:j + 1]).then_inc(scalar_done, A.one(("A", ph, "ms")))
            A.eng.wait_ge(vector_done, done("V", ph, "inverse"))
            A.eng.wait_ge(scalar_done, A.n)
            A.eng.activation(stat[:, 8:8 + n], stat[:, 4:4 + n], ACT.Sqrt).then_inc(scalar_done, A.one(("A", ph, "rstd")))

        def norm_V(V, ph, tiles):
            n = len(tiles)
            V.eng.wait_ge(scalar_done, done("A", ph, "ms"))
            V.eng.wait_ge(vector_done, V.n)
            V.eng.tensor_scalar(stat[:, 4:4 + n], stat[:, 0:n], EPS, None, ALU.add).then_inc(vector_done, V.one())
            V.eng.wait_ge(vector_done, V.n)
            V.eng.reciprocal(stat[:, 4:4 + n], stat[:, 4:4 + n]).then_inc(vector_done, V.one(("V", ph, "inverse")))
            V.eng.wait_ge(scalar_done, done("A", ph, "rstd"))
            for j, t in enumerate(tiles):
                V.eng.wait_ge(vector_done, V.n)
                V.eng.tensor_scalar(XN[j], xt[:, t, :], stat[:, 8 + j:9 + j], None, ALU.mult).then_inc(vector_done, V.one(("V", ph, "xn", j)))

        def norm_T(T, ph, tiles):
            for j in range(len(tiles)):
                T.eng.wait_ge(vector_done, done("V", ph, "xn", j))
            for k in range(KT):
                for j in range(len(tiles)):
                    i = T.eng.transpose(psum[k][:, j * P:(j + 1) * P], XN[j][:, k * P:(k + 1) * P], ident)
                i.then_inc(tensor_done, T.one(("T", ph, "k", k)))

        def norm_evac(E, ph, tiles, which, mine):
            for k in range(KT):
                if k % 2 != mine:
                    continue
                E.eng.wait_ge(tensor_done, done("T", ph, "k", k))
                for s in sorted({t // 2 for t in tiles}):
                    lo = [j for j, t in enumerate(tiles) if t // 2 == s][0] * P
                    dst, src = nT[:, k, s * SEQ:(s + 1) * SEQ], psum[k][:, lo:lo + SEQ]
                    a, b = which(k, s)
                    if E.name == "V":
                        if b is None:
                            E.eng.wait_ge(E.sem, E.n)
                            E.eng.tensor_scalar(dst, src, a, None, ALU.mult).then_inc(E.sem, E.one())
                        else:
                            E.eng.wait_ge(E.sem, E.n)
                            E.eng.tensor_scalar(dst, src, a, b, ALU.mult, ALU.add).then_inc(E.sem, E.one())
                    elif b is None:
                        E.eng.wait_ge(E.sem, E.n)
                        E.eng.activation(dst, src, ACT.Copy, scale=a).then_inc(E.sem, E.one())
                    else:
                        E.eng.wait_ge(E.sem, E.n)
                        E.eng.activation(dst, src, ACT.Identity, scale=a, bias=b).then_inc(E.sem, E.one())

        def proj_T(T, ph, cuts, tiles_of):
            for c, (a, b) in enumerate(cuts):
                tiles = tiles_of(c)
                if c >= 2:
                    T.eng.wait_ge(vector_done, done("V", ph, "out", c - 2))
                    T.eng.wait_ge(scalar_done, done("A", ph, "out", c - 2))
                for half in range(2):
                    w, slot = take(T)
                    w = w.rearrange("p (k n) -> p k n", k=4)
                    for j, t in enumerate(tiles):
                        for k in range(4):
                            i = T.eng.matmul(psum[4 * (c % 2) + j][:, 0:b - a], nT[:, half * 4 + k, t * P:(t + 1) * P],
                                             w[:, k, 0:b - a], start=(half == 0 and k == 0), stop=(half == 1 and k == 3))
                    i.then_inc(tensor_done, T.one(slot))
                T.note(("T", ph, "out", c))

        def proj_copy(E, ph, cuts, tiles_of, stride, mine):
            for c, (a, b) in enumerate(cuts):
                E.eng.wait_ge(tensor_done, done("T", ph, "out", c))
                for j, t in enumerate(tiles_of(c)):
                    if j % 2 == mine:
                        dst = big[:, t * stride + a:t * stride + b]
                        src = psum[4 * (c % 2) + j][:, 0:b - a]
                        if E.name == "V":
                            E.eng.wait_ge(E.sem, E.n)
                            E.eng.tensor_copy(dst, src).then_inc(E.sem, E.one())
                        else:
                            E.eng.wait_ge(E.sem, E.n)
                            E.eng.activation(dst, src, ACT.Copy).then_inc(E.sem, E.one())
                E.note((E.name, ph, "out", c))

        def residual_V(V, ph, cuts, tiles, gated):
            for c, (a, b) in enumerate(cuts):
                V.eng.wait_ge(tensor_done, done("T", ph, "out", c))
                for j, t in enumerate(tiles):
                    src = psum[4 * (c % 2) + j][:, 0:b - a]
                    if gated:
                        s = t // 2
                        tmp = work[:, 512 * j:512 * j + b - a]
                        V.eng.wait_ge(vector_done, V.n)
                        V.eng.tensor_tensor(tmp, src, gate[:, s * D + a:s * D + b], ALU.mult).then_inc(vector_done, V.one())
                        src = tmp
                    V.eng.wait_ge(vector_done, V.n)
                    V.eng.tensor_tensor(xt[:, t, a:b], xt[:, t, a:b], src, ALU.add).then_inc(vector_done, V.one())
                V.note(("V", ph, "out", c))

        def rope_V(V, row, n, cos, sin, axial):
            m = 4 if axial else 2
            q = DH // m
            src = row.rearrange("p (h m q) -> p h m q", m=m, q=q)
            o = work[:, 0:n * DH]
            o4 = o.rearrange("p (h m q) -> p h m q", m=m, q=q)
            r = work[:, 1024:1024 + n * DH]
            c3 = cos.rearrange("p (o e) -> p o e", o=1).to_broadcast([P, n, DH])
            s4 = sin.rearrange("p (o m q) -> p o m q", o=1, m=m)
            r4 = r.rearrange("p (h m q) -> p h m q", m=m, q=q)
            V.eng.wait_ge(vector_done, V.n)
            V.eng.tensor_tensor(o.rearrange("p (h e) -> p h e", e=DH), row.rearrange("p (h e) -> p h e", e=DH), c3, ALU.mult).then_inc(vector_done, V.one())
            for a in range(m):
                b = a ^ 1
                V.eng.wait_ge(vector_done, V.n)
                V.eng.tensor_tensor(r4[:, :, a, :], src[:, :, b, :], s4[:, :, a, :].to_broadcast([P, n, q]), ALU.mult).then_inc(vector_done, V.one())
            V.eng.wait_ge(vector_done, V.n)
            V.eng.tensor_tensor(row, o, r, ALU.add).then_inc(vector_done, V.one())

        hv = lambda a, e: a.rearrange("p (h e) -> p h e", e=e)
        over = lambda col, n, e: col.rearrange("p (h o) -> p h o", o=1).to_broadcast([P, n, e])
        under = lambda row, n, e: row.rearrange("p (o e) -> p o e", o=1).to_broadcast([P, n, e])

        def heads_rms_V(V, ph, rows, width, eps):
            at = 0
            for row, n in rows:
                sq = work[:, 0:n * width]
                V.eng.wait_ge(vector_done, V.n)
                V.eng.tensor_tensor(sq, row, row, ALU.mult).then_inc(vector_done, V.one())
                V.eng.wait_ge(vector_done, V.n)
                V.eng.tensor_reduce(rms[:, at:at + n], hv(sq, width), AX_X, ALU.add).then_inc(vector_done, V.one())
                at += n
            V.eng.wait_ge(vector_done, V.n)
            V.eng.tensor_scalar(rms[:, 0:at], rms[:, 0:at], 1.0 / width, eps, ALU.mult, ALU.add).then_inc(vector_done, V.one())
            V.eng.wait_ge(vector_done, V.n)
            V.eng.reciprocal(rms[:, 0:at], rms[:, 0:at]).then_inc(vector_done, V.one(("V", ph, "inverse")))
            V.eng.wait_ge(scalar_done, done("A", ph, "rstd"))

        def heads_rms_A(A, ph, n):
            A.eng.wait_ge(vector_done, done("V", ph, "inverse"))
            A.eng.wait_ge(scalar_done, A.n)
            A.eng.activation(rms[:, 0:n], rms[:, 0:n], ACT.Sqrt).then_inc(scalar_done, A.one(("A", ph, "rstd")))

        def heads_scale_V(V, row, n, at, g):
            V.eng.wait_ge(vector_done, V.n)
            V.eng.tensor_tensor(hv(row, DH), hv(row, DH), over(rms[:, at:at + n], n, DH), ALU.mult).then_inc(vector_done, V.one())
            V.eng.wait_ge(vector_done, V.n)
            V.eng.tensor_tensor(hv(row, DH), hv(row, DH), under(g, n, DH), ALU.mult).then_inc(vector_done, V.one())

        def turns_T(T, ph, groups, needs):
            for g, (srcs, dst, scale) in enumerate(groups):
                for e, step in needs(g):
                    T.eng.wait_ge(SEM[e], done(*step))
                if g >= 8:
                    e = "VA"[(g - 8) % 2]
                    T.eng.wait_ge(SEM[e], done(e, ph, "turn", g - 8))
                for j, s in enumerate(srcs):
                    i = T.eng.transpose(psum[g % 8][:, j * P:(j + 1) * P], s, ident)
                i.then_inc(tensor_done, T.one(("T", ph, "turn", g)))

        def turns_evac(E, ph, groups, mine):
            for g, (srcs, dst, scale) in enumerate(groups):
                if g % 2 != mine:
                    continue
                E.eng.wait_ge(tensor_done, done("T", ph, "turn", g))
                src = psum[g % 8][:, 0:len(srcs) * P]
                if E.name == "V":
                    if scale == 1.0:
                        E.eng.wait_ge(E.sem, E.n)
                        E.eng.tensor_copy(dst, src).then_inc(E.sem, E.one(("V", ph, "turn", g)))
                    else:
                        E.eng.wait_ge(E.sem, E.n)
                        E.eng.tensor_scalar(dst, src, scale, None, ALU.mult).then_inc(E.sem, E.one(("V", ph, "turn", g)))
                else:
                    E.eng.wait_ge(E.sem, E.n)
                    E.eng.activation(dst, src, ACT.Copy, scale=scale).then_inc(E.sem, E.one(("A", ph, "turn", g)))

        NB = 3
        PB = [work[:, 512 * i:512 * i + 512] for i in range(NB)]
        PTB = [work[:, 1536 + 512 * i:2048 + 512 * i] for i in range(NB)]

        def att_T(T, ph, jobs):
            n = len(jobs)
            for s in range(n + 3):
                if s < n:
                    j = jobs[s]
                    if s >= 3:
                        e = "V" if jobs[s - 3]["mask"] is not None else "A"
                        T.eng.wait_ge(SEM[e], done(e, ph, "read", s - 3))
                    bank = psum[s % 3]
                    for (a, b, terms) in j["scores"]:
                        for m, (l, r) in enumerate(terms):
                            i = T.eng.matmul(bank[:, a:b], l, r, start=(m == 0), stop=(m == len(terms) - 1))
                    i.then_inc(tensor_done, T.one(("T", ph, "scores", s)))
                if 0 <= s - 2 < n:
                    q = s - 2
                    T.eng.wait_ge(vector_done, done("V", ph, "probs", q))
                    if q >= 2:
                        T.eng.wait_ge(scalar_done, done("A", ph, "turned", q - 2))
                    for c in range(jobs[q]["n"] // P):
                        i = T.eng.transpose(psum[3 + q % 2][:, c * P:(c + 1) * P], PB[q % NB][:, c * P:(c + 1) * P], ident)
                    i.then_inc(tensor_done, T.one(("T", ph, "turn", q)))
                if 0 <= s - 3 < n:
                    q = s - 3
                    j = jobs[q]
                    T.eng.wait_ge(scalar_done, done("A", ph, "turned", q))
                    ob, oa, ob_cols, first, last, tok = j["out"]
                    if j["open"] and j["group"] >= 2:
                        T.eng.wait_ge(scalar_done, done("A", ph, "group", j["group"] - 2))
                    nc_ = j["n"] // P
                    for c in range(nc_):
                        pt = PTB[q % NB][:, c * P:(c + 1) * P]
                        o = psum[5 + j["group"] % 2][oa, ob_cols]
                        l, r = (pt, j["v"][c]) if tok else (j["v"][c], pt)
                        i = T.eng.matmul(o, l, r, start=(first and c == 0), stop=(last and c == nc_ - 1))
                    i.then_inc(tensor_done, T.one(("T", ph, "out", q)))

        def att_V(V, ph, jobs):
            n = len(jobs)
            for s in range(n + 1):
                if s < n:
                    j = jobs[s]
                    V.eng.wait_ge(tensor_done, done("T", ph, "scores", s))
                    mn = mxs[:, s % NB:s % NB + 1]
                    if s >= NB:
                        V.eng.wait_ge(tensor_done, done("T", ph, "turn", s - NB))
                    init = j["sink"] if j["sink"] is not None else None
                    if j["mask"] is not None:
                        V.eng.wait_ge(vector_done, V.n)
                        V.eng.tensor_tensor_reduce(out=PB[s % NB][:, 0:j["n"]], in0=psum[s % 3][:, 0:j["n"]], in1=j["mask"],
                                                          scale=1.0, scalar=(3e38 if init is None else init), op0=ALU.add, op1=ALU.min,
                                                          accum_out=mn).then_inc(vector_done, V.one(("V", ph, "read", s)))
                    else:
                        V.eng.wait_ge(vector_done, V.n)
                        V.eng.tensor_reduce(mn, psum[s % 3][:, 0:j["n"]], AX_X, ALU.min).then_inc(vector_done, V.one())
                        if init is not None:
                            V.eng.wait_ge(vector_done, V.n)
                            V.eng.tensor_tensor(mn, mn, init, ALU.min).then_inc(vector_done, V.one())
                    V.note(("V", ph, "max", s))
                if 0 <= s - 1 < n:
                    q = s - 1
                    j = jobs[q]
                    den, r = mxs[:, 3 + q % NB:4 + q % NB], mxs[:, 9 + q % NB:10 + q % NB]
                    V.eng.wait_ge(scalar_done, done("A", ph, "exp", q))
                    if j["sink"] is not None:
                        V.eng.wait_ge(vector_done, V.n)
                        V.eng.tensor_tensor(den, den, mxs[:, 6 + q % NB:7 + q % NB], ALU.add).then_inc(vector_done, V.one())
                    V.eng.wait_ge(vector_done, V.n)
                    V.eng.reciprocal(r, den).then_inc(vector_done, V.one())
                    if j["factor"] is None:
                        V.eng.wait_ge(vector_done, V.n)
                        V.eng.tensor_scalar(PB[q % NB][:, 0:j["n"]], PB[q % NB][:, 0:j["n"]], r, None, ALU.mult).then_inc(vector_done, V.one(("V", ph, "probs", q)))
                    else:
                        V.eng.wait_ge(vector_done, V.n)
                        V.eng.tensor_scalar(PB[q % NB][:, 0:j["n"]], PB[q % NB][:, 0:j["n"]], r, j["factor"], ALU.mult, ALU.mult).then_inc(vector_done, V.one(("V", ph, "probs", q)))

        def att_A(A, ph, jobs):
            n = len(jobs)
            for s in range(n + 3):
                if s < n:
                    j = jobs[s]
                    A.eng.wait_ge(vector_done, done("V", ph, "max", s))
                    if s >= NB:
                        A.eng.wait_ge(vector_done, done("V", ph, "probs", s - NB))
                    src = PB[s % NB] if j["mask"] is not None else psum[s % 3]
                    mn = mxs[:, s % NB:s % NB + 1]
                    A.eng.wait_ge(scalar_done, A.n)
                    A.eng.activation(PB[s % NB][:, 0:j["n"]], src[:, 0:j["n"]], ACT.Exp, bias=mn, scale=-1.0,
                                            accum_out=mxs[:, 3 + s % NB:4 + s % NB]).then_inc(scalar_done, A.one(("A", ph, "read", s)))
                    if j["sink"] is not None:
                        A.eng.wait_ge(scalar_done, A.n)
                        A.eng.activation(mxs[:, 6 + s % NB:7 + s % NB], j["sink"], ACT.Exp, bias=mn, scale=-1.0).then_inc(scalar_done, A.one())
                    A.note(("A", ph, "exp", s))
                if 0 <= s - 2 < n:
                    q = s - 2
                    A.eng.wait_ge(tensor_done, done("T", ph, "turn", q))
                    if q >= NB:
                        A.eng.wait_ge(tensor_done, done("T", ph, "out", q - NB))
                    m = jobs[q]["n"]
                    A.eng.wait_ge(scalar_done, A.n)
                    A.eng.activation(PTB[q % NB][:, 0:m], psum[3 + q % 2][:, 0:m], ACT.Copy).then_inc(scalar_done, A.one(("A", ph, "turned", q)))
                if 0 <= s - 3 < n and jobs[s - 3]["close"] is not None:
                    q = s - 3
                    src_cols, dst = jobs[q]["close"]
                    A.eng.wait_ge(tensor_done, done("T", ph, "out", q))
                    A.eng.wait_ge(scalar_done, A.n)
                    A.eng.activation(dst, psum[5 + jobs[q]["group"] % 2][:, src_cols], ACT.Copy).then_inc(scalar_done, A.one(("A", ph, "group", jobs[q]["group"])))

        def jobs_of_pairs(heads, tiles, tile0, scores, n, mask, sink_of, values, dst):
            jobs = []
            group = 0
            for pair in range(heads // 2):
                for ti, t in enumerate(tiles):
                    for par in range(2):
                        h = 2 * pair + par
                        lastj = ti == len(tiles) - 1 and par == 1
                        jobs.append(dict(
                            n=n(t), scores=scores(h, t), mask=mask(t), sink=sink_of(h), factor=None, v=values(h, t),
                            out=(None, slice(64 * par, 64 * par + 64), slice(ti * P, (ti + 1) * P), True, True, False),
                            open=(ti == 0 and par == 0), group=group,
                            close=(slice(0, len(tiles) * P), dst(pair)) if lastj else None))
                group += 1
            return jobs

        def up_T(T, ph, lo, n):
            for f in range(FC):
                w, slot = take(T)
                w = w.rearrange("p (u k c) -> p u k c", u=2, c=P)
                if f >= 4:
                    T.eng.wait_ge(vector_done, done("V", ph, "h", f - 4))
                for u in range(2):
                    for k in range(KT):
                        i = T.eng.matmul(psum[2 * (f % 4) + u][:, 0:n], w[:, u, k, :], nT[:, k, lo:lo + n],
                                         start=(k == 0), stop=(k == KT - 1))
                i.then_inc(tensor_done, T.one(slot))
                T.note(("T", ph, "up", f))

        cbuf = lambda f, i, n: qkt[:, ((f % 2) * 3 + i) * 512:((f % 2) * 3 + i) * 512 + n]
        hT = lambda f, n: big[:, f * n:(f + 1) * n]

        def up_A(A, ph, n, taps, both):
            mid, bias = taps
            for f in range(FC):
                A.eng.wait_ge(tensor_done, done("T", ph, "up", f))
                if f >= 2:
                    A.eng.wait_ge(vector_done, done("V", ph, "h", f - 2))
                for u in range(2 if both else 1):
                    A.eng.wait_ge(scalar_done, A.n)
                    A.eng.activation(cbuf(f, u, n), psum[2 * (f % 4) + u][:, 0:n], ACT.Identity,
                                            scale=mid(u, f), bias=bias(u, f)).then_inc(scalar_done, A.one())
                A.note(("A", ph, "mid", f))
                A.eng.wait_ge(vector_done, done("V", ph, "conv", f))
                A.eng.wait_ge(scalar_done, A.n)
                A.eng.activation(cbuf(f, 2, n), cbuf(f, 0, n), ACT.Silu).then_inc(scalar_done, A.one(("A", ph, "silu", f)))

        def up_V_causal(V, ph, n, tap):
            for f in range(FC):
                g = psum[2 * (f % 4)]
                c = cbuf(f, 0, n)
                V.eng.wait_ge(scalar_done, done("A", ph, "mid", f))
                for back in (1, 2):
                    V.eng.wait_ge(vector_done, V.n)
                    V.eng.scalar_tensor_tensor(out=c[:, back:n], in0=g[:, 0:n - back], scalar=tap(2 - back, f),
                                                      in1=c[:, back:n], op0=ALU.mult, op1=ALU.add).then_inc(vector_done, V.one())
                V.note(("V", ph, "conv", f))
                V.eng.wait_ge(scalar_done, done("A", ph, "silu", f))
                V.eng.wait_ge(vector_done, V.n)
                V.eng.tensor_tensor(hT(f, n), psum[2 * (f % 4) + 1][:, 0:n], cbuf(f, 2, n), ALU.mult).then_inc(vector_done, V.one(("V", ph, "h", f)))

        def up_V_both(V, ph, n, tap):
            for f in range(FC):
                V.eng.wait_ge(scalar_done, done("A", ph, "mid", f))
                for u in range(2):
                    g = psum[2 * (f % 4) + u][:, 0:n].rearrange("p (s t) -> p s t", t=SEQ)
                    c = cbuf(f, u, n).rearrange("p (s t) -> p s t", t=SEQ)
                    V.eng.wait_ge(vector_done, V.n)
                    V.eng.scalar_tensor_tensor(out=c[:, :, 1:], in0=g[:, :, 0:SEQ - 1], scalar=tap(u, 0, f),
                                                      in1=c[:, :, 1:], op0=ALU.mult, op1=ALU.add).then_inc(vector_done, V.one())
                    V.eng.wait_ge(vector_done, V.n)
                    V.eng.scalar_tensor_tensor(out=c[:, :, 0:SEQ - 1], in0=g[:, :, 1:], scalar=tap(u, 2, f),
                                                      in1=c[:, :, 0:SEQ - 1], op0=ALU.mult, op1=ALU.add).then_inc(vector_done, V.one())
                    if u == 0:
                        V.note(("V", ph, "conv", f))
                V.eng.wait_ge(scalar_done, done("A", ph, "silu", f))
                V.eng.wait_ge(vector_done, V.n)
                V.eng.tensor_tensor(hT(f, n), cbuf(f, 1, n), cbuf(f, 2, n), ALU.mult).then_inc(vector_done, V.one(("V", ph, "h", f)))

        def down_T(T, ph, tiles):
            n = len(tiles) * P
            if len(tiles) == 2:
                for f0 in range(0, FC, 2):
                    w, slot = take(T)
                    w = w.rearrange("p (c n) -> p c n", c=2)
                    for c in range(2):
                        f = f0 + c
                        for j in range(2):
                            for half in range(2):
                                i = T.eng.matmul(psum[4 * half + j][:, :], hT(f, n)[:, j * P:(j + 1) * P], w[:, c, half * 512:half * 512 + 512],
                                                 start=(f == 0), stop=(f == FC - 1))
                    i.then_inc(tensor_done, T.one(slot))
                T.note(("T", ph, "out", 0))
                T.note(("T", ph, "out", 1))
            else:
                for half in range(2):
                    for f0 in range(0, FC, 4):
                        w, slot = take(T)
                        w = w.rearrange("p (c n) -> p c n", c=4)
                        for c in range(min(4, FC - f0)):
                            f = f0 + c
                            for j in range(4):
                                i = T.eng.matmul(psum[4 * half + j][:, :], hT(f, n)[:, j * P:(j + 1) * P], w[:, c, :],
                                                 start=(f == 0), stop=(f == FC - 1))
                        i.then_inc(tensor_done, T.one(slot))
                    T.note(("T", ph, "out", half))

        silu_c = st2[:, 64:80]

        def ada_T(T, ph):
            for g in range(3):
                for k in range(KT):
                    w, slot = take(T)
                    for j in range(4):
                        i = T.eng.matmul(psum[g][32 * j:32 * j + 2, :], silu_c[:, 2 * k:2 * k + 2],
                                         w[:, j * 512:(j + 1) * 512], start=(k == 0), stop=(k == KT - 1))
                    i.then_inc(tensor_done, T.one(slot))
            T.note(("T", ph, "rows"))
            T.eng.wait_ge(vector_done, done("V", ph, "rows"))
            n = 0
            for w, idx in enumerate((0, 1, 3, 4)):
                for k in range(KT):
                    g, j = idx // 2, (idx % 2) * 2 + k // 4
                    r = slice(32 * j, 32 * j + 2)
                    i = T.eng.matmul(psum[4 + j][:, 2 * n:2 * n + 2], mod[r, g * 512 + (k % 4) * P:g * 512 + (k % 4 + 1) * P],
                                     const("ident", 32 * j, 32 * j + 2, r), start=True, stop=True, tile_position=(32 * j, 0))
                    n += 1
            i.then_inc(tensor_done, T.one(("T", ph, "cols")))

        def ada_V(V, ph, layer):
            V.eng.wait_ge(tensor_done, done("T", ph, "rows"))
            V.eng.wait_ge(adab_in, 16 * 8 * (layer + 1))
            for g in range(3):
                for j in range(4):
                    r = slice(32 * j, 32 * j + 2)
                    m = mod[r, g * 512:(g + 1) * 512]
                    V.eng.wait_ge(vector_done, V.n)
                    V.eng.tensor_tensor(m, psum[g][r, :], m, ALU.add).then_inc(vector_done, V.one())
            V.note(("V", ph, "rows"))
            V.eng.wait_ge(tensor_done, done("T", ph, "cols"))
            for w, idx in enumerate((0, 1, 3, 4)):
                for half in range(2):
                    a = w * 16 + half * 8
                    V.eng.wait_ge(vector_done, V.n)
                    V.eng.tensor_copy(modcol[:, a:a + 8], psum[4 + (idx % 2) * 2 + half][:, a:a + 8]).then_inc(vector_done, V.one())
            for m, w in enumerate((1, 3)):
                g3 = veccol[:, 32 + layer * 16 + m * 8:32 + layer * 16 + m * 8 + 8].rearrange("p (k o) -> p k o", o=1).to_broadcast([P, KT, 2])
                V.eng.wait_ge(vector_done, V.n)
                V.eng.scalar_tensor_tensor(
                    out=acol[:, m * 16:(m + 1) * 16].rearrange("p (k s) -> p k s", s=2),
                    in0=modcol[:, w * 16:(w + 1) * 16].rearrange("p (k s) -> p k s", s=2),
                    scalar=1.0, in1=g3, op0=ALU.add, op1=ALU.mult).then_inc(vector_done, V.one())

        def gates_T(T, ph, idx, streams):
            n = 0
            for s in streams:
                for half in range(2):
                    g, j = idx // 2, (idx % 2) * 2 + half
                    r = slice(32 * j, 32 * j + 2)
                    i = T.eng.matmul(psum[2 * s + half][:, :], const("pick2", s * P, (s + 1) * P, r), mod[r, g * 512:(g + 1) * 512],
                                     start=True, stop=True, tile_position=(32 * j, 0))
                    n += 1
            i.then_inc(tensor_done, T.one(("T", ph, "gates")))

        def gates_A(A, ph, streams):
            A.eng.wait_ge(tensor_done, done("T", ph, "gates"))
            for s in streams:
                for half in range(2):
                    A.eng.wait_ge(scalar_done, A.n)
                    A.eng.activation(gate[:, s * D + half * 512:s * D + half * 512 + 512], psum[2 * s + half][:, :], ACT.Copy).then_inc(scalar_done, A.one())

        S1 = 3080
        tok1 = lambda t: big[:, (t - 2) * S1:(t - 1) * S1]
        f256 = lambda i: qkt[:, i * SEQ:(i + 1) * SEQ]
        frow = gate[0:NH, :]

        def turns_l0():
            g = []
            for kind, scale in ((0, -0.125), (1, 1.0), (3, -0.125), (4, 1.0)):
                for pr in range(4):
                    i = {0: 0, 1: 4, 3: 8, 4: 12}[kind] + pr
                    g.append(([big[:, j * S1 + kind * 512 + pr * P:j * S1 + kind * 512 + (pr + 1) * P] for j in range(2)], f256(i), scale))
            return g

        def jobs_l0(which):
            base = 0 if which == "dilated" else 8
            vcol = 1024 if which == "dilated" else 2560
            def scores(h, t):
                r = slice(64 * (h % 2), 64 * (h % 2) + 64)
                n = (t + 1) * P
                terms = [(f256(base + h // 2)[r, t * P:(t + 1) * P], f256(base + 4 + h // 2)[r, 0:n])]
                if which == "forget":
                    terms.append((const("pick8", h * P, (h + 1) * P, slice(0, NH)), frow[:, 512:512 + n]))
                return [(0, n, terms)]
            mask = (lambda t: const("dilated", t * SEQ, t * SEQ + (t + 1) * P)) if which == "dilated" else \
                   (lambda t: const("causal", P - t * P, 2 * P))
            vals = lambda h, t: [big[:, c * S1 + vcol + h * DH:c * S1 + vcol + (h + 1) * DH] for c in range(t + 1)]
            off = 0 if which == "dilated" else 4
            return jobs_of_pairs(NH, (0, 1), 0, scores, lambda t: (t + 1) * P, mask, lambda h: None, vals,
                                 lambda pair: nT[:, off + pair, SEQ:2 * SEQ])

        S2 = 3072
        def turns_l1():
            g = []
            for kind, scale in ((0, -0.125), (1, 1.0)):
                for pr in range(8):
                    g.append(([big[:, j * S2 + kind * 1024 + pr * P:j * S2 + kind * 1024 + (pr + 1) * P] for j in range(2)],
                              f256(kind * 8 + pr), scale))
            return g

        def jobs_l1():
            jobs = []
            group = 0
            for t in range(2):
                for h0 in range(0, NH, 4):
                    for h in range(h0, h0 + 4):
                        for m in range(2):
                            r = slice(64 * m, 64 * m + 64)
                            n = (t + 1) * P
                            jobs.append(dict(
                                n=n, scores=[(0, n, [(f256(h)[r, t * P:(t + 1) * P], f256(8 + h)[r, 0:n])])],
                                mask=const("causal", P - t * P, 2 * P), sink=None, factor=(lam[:, 4:5] if m else None),
                                v=[big[:, c * S2 + 2048 + h * P:c * S2 + 2048 + (h + 1) * P] for c in range(t + 1)],
                                out=(None, slice(0, P), slice((h - h0) * P, (h - h0 + 1) * P), m == 0, m == 1, True),
                                open=(h == h0 and m == 0), group=group,
                                close=(slice(0, 512), big[:, t * S2 + h0 * P:t * S2 + (h0 + 4) * P]) if (h == h0 + 3 and m) else None))
                    group += 1
            return jobs

        S3 = 2832
        row3 = lambda t, a, b: big[:, t * S3 + a:t * S3 + b]
        f512 = lambda i: qkt[:, i * 512:(i + 1) * 512]
        kdup = lambda t: work[:, 2048 + t * 256:2048 + (t + 1) * 256]

        def turns_e(part):
            g = []
            if part == 0:
                for h in range(MH):
                    g.append(([row3(t, h * P, (h + 1) * P) for t in ALL], f512(h), 1.0))
                    g.append(([row3(t, 512 + h * P, 512 + (h + 1) * P) for t in ALL], f512(4 + h), MD ** -0.5))
            else:
                for pr in range(4):
                    g.append(([row3(t, 2064 + pr * P, 2064 + (pr + 1) * P) for t in ALL], f512(8 + pr), -0.125))
                for kv in range(2):
                    g.append(([kdup(t)[:, kv * P:(kv + 1) * P] for t in ALL], f512(12 + kv), 1.0))
            return g

        def jobs_e(stream):
            def scores(h, t):
                r = slice(64 * (h % 2), 64 * (h % 2) + 64)
                return [(0, 512 if stream else 256, [(f512(8 + h // 2)[r, t * P:(t + 1) * P], f512(12 + h // 4)[r, 0:(512 if stream else 256)])])]
            n = 512 if stream else 256
            vals = lambda h, t: [row3(c, 2704 + (h // 4) * DH, 2704 + (h // 4 + 1) * DH) for c in range(n // P)]
            mask = (lambda t: const("window", (t - 2) * 512, (t - 1) * 512)) if stream else (lambda t: None)
            return jobs_of_pairs(NH, LAT if stream else CTX, 0, scores, lambda t: n, mask, lambda h: nsink[:, h:h + 1], vals,
                                 lambda pair: nT[:, 4 + pair, stream * SEQ:(stream + 1) * SEQ])

        S4 = 2304
        row4 = lambda t, a, b: big[:, t * S4 + a:t * S4 + b]
        OQ, OK_, NQ, NK = 0, 1024, 2048, 3072

        def turns_o():
            g = []
            for pr in range(4):
                g.append(([row4(t, pr * P, (pr + 1) * P) for t in LAT], qkt[:, OQ + pr * SEQ:OQ + (pr + 1) * SEQ], -0.125))
            for kv in range(2):
                g.append(([kdup(t)[:, kv * P:(kv + 1) * P] for t in ALL], qkt[:, OK_ + kv * 512:OK_ + (kv + 1) * 512], 1.0))
            for pr in range(4):
                g.append(([row4(t, 768 + pr * P, 768 + (pr + 1) * P) for t in LAT], qkt[:, NQ + pr * SEQ:NQ + (pr + 1) * SEQ], -0.125))
            for pr in range(4):
                g.append(([row4(t, 1280 + pr * P, 1280 + (pr + 1) * P) for t in ALL], qkt[:, NK + pr * 512:NK + (pr + 1) * 512], 1.0))
            return g

        def nbias(h, t):
            o = (h % 4) * 512 + t * SEQ
            return qkt[:, 5120 + o:5120 + o + SEQ] if h < 4 else big[:, 4 * S4 + o:4 * S4 + o + SEQ]

        def jobs_o(which):
            def scores(h, t):
                r = slice(64 * (h % 2), 64 * (h % 2) + 64)
                if which == "global":
                    q = qkt[r, OQ + (h // 2) * SEQ + (t - 2) * P:OQ + (h // 2) * SEQ + (t - 1) * P]
                    return [(0, 512, [(q, qkt[r, OK_ + (h // 4) * 512:OK_ + (h // 4 + 1) * 512])])]
                q = qkt[r, NQ + (h // 2) * SEQ + (t - 2) * P:NQ + (h // 2) * SEQ + (t - 1) * P]
                k = NK + (h // 2) * 512
                return [(0, SEQ, [(q, qkt[r, k:k + SEQ])]),
                        (SEQ, 512, [(q, qkt[r, k + SEQ:k + 512]), (const("negflip"), nbias(h, t - 2))])]
            if which == "global":
                vals = lambda h, t: [row4(c, 640 + (h // 4) * DH, 640 + (h // 4 + 1) * DH) for c in ALL]
                mask = lambda t: None
            else:
                vals = lambda h, t: [row4(c, 1792 + h * DH, 1792 + (h + 1) * DH) for c in ALL]
                mask = lambda t: const("nbhood")
            off = 0 if which == "global" else 4
            return jobs_of_pairs(NH, LAT, 0, scores, lambda t: 512, mask, lambda h: None, vals,
                                 lambda pair: nT[:, off + pair, SEQ:2 * SEQ])

        mrow = lambda d, i: nt[0:MH, (d * 4 + i) * 512:(d * 4 + i + 1) * 512]
        PT = lambda d, s: work[:, d * 2048 + s * 512:d * 2048 + (s + 1) * 512]
        WT = lambda i: gate[:, (i % 4) * 512:(i % 4 + 1) * 512]
        REACH = [{s: [t for t in range(4) if t >= s] for s in range(4)}, {0: [0, 2, 3], 1: [0, 1, 2, 3], 2: [2], 3: [2, 3]}]

        def runs(tiles):
            out_, a = [], tiles[0]
            for x, y in zip(tiles, tiles[1:] + [99]):
                if y != x + 1:
                    out_.append((a * P, (x + 1) * P))
                    a = y
            return out_

        def mgate_T(T, ph):
            for g in range(4):
                for t in ALL:
                    i = T.eng.matmul(psum[g][0:MH, t * P:(t + 1) * P], row3(t, 2048 + 4 * g, 2052 + 4 * g), ident, start=True, stop=True)
                i.then_inc(tensor_done, T.one(("T", ph, "gates", g)))
            T.eng.wait_ge(vector_done, done("V", ph, "rows"))
            n = 0
            for d in range(2):
                for what in range(2):
                    for t in ALL:
                        i = T.eng.matmul(psum[4][:, 4 * n:4 * n + 4], mrow(d, what)[:, t * P:(t + 1) * P],
                                         const("ident", 0, MH, slice(0, MH)), start=True, stop=True)
                        n += 1
            i.then_inc(tensor_done, T.one(("T", ph, "cols")))

        def log_sigmoid(V, A, ph, key, x, t1, t2):
            if V is not None:
                V.eng.wait_ge(vector_done, V.n)
                V.eng.scalar_tensor_tensor(out=t1, in0=x, scalar=-1.0, in1=x, op0=ALU.mult, op1=ALU.max).then_inc(vector_done, V.one(("V", ph, "abs", key)))
                V.eng.wait_ge(scalar_done, done("A", ph, "log", key))
                V.eng.wait_ge(vector_done, V.n)
                V.eng.scalar_tensor_tensor(out=x, in0=x, scalar=0.0, in1=t2, op0=ALU.min, op1=ALU.subtract).then_inc(vector_done, V.one())
            else:
                A.eng.wait_ge(vector_done, done("V", ph, "abs", key))
                A.eng.wait_ge(scalar_done, A.n)
                A.eng.activation(t1, t1, ACT.Exp, scale=-1.0).then_inc(scalar_done, A.one())
                A.eng.wait_ge(scalar_done, A.n)
                A.eng.activation(t2, t1, ACT.Ln, bias=1.0).then_inc(scalar_done, A.one(("A", ph, "log", key)))

        def mgate_V(V, ph):
            for g in range(4):
                V.eng.wait_ge(tensor_done, done("T", ph, "gates", g))
                V.eng.wait_ge(vector_done, V.n)
                V.eng.tensor_scalar(mrow(g // 2, g % 2), psum[g][0:MH, :], gbias[0:MH, g:g + 1], None, ALU.add).then_inc(vector_done, V.one())
            for d in range(2):
                a, f, B, M = (mrow(d, i) for i in range(4))
                log_sigmoid(V, None, ph, d, f, B, M)
                zero = work[0:MH, 0:512]
                if d == 0:
                    V.eng.wait_ge(vector_done, V.n)
                    V.eng.memset(zero, 0.0).then_inc(vector_done, V.one())
                    V.eng.wait_ge(vector_done, V.n)
                    V.eng.tensor_tensor_scan(B, f, zero, 0.0, ALU.add, ALU.add).then_inc(vector_done, V.one())
                    V.eng.wait_ge(vector_done, V.n)
                    V.eng.tensor_tensor(a, a, B, ALU.subtract).then_inc(vector_done, V.one())
                    V.eng.wait_ge(vector_done, V.n)
                    V.eng.tensor_tensor_scan(M, a, a, 0.0, ALU.max, ALU.max).then_inc(vector_done, V.one())
                else:
                    c, l = (lambda x: x[:, 0:SEQ][:, ::-1]), (lambda x: x[:, SEQ:512][:, ::-1])
                    V.eng.wait_ge(vector_done, V.n)
                    V.eng.tensor_tensor_scan(c(B), c(f), c(zero), 0.0, ALU.add, ALU.add).then_inc(vector_done, V.one())
                    V.eng.wait_ge(vector_done, V.n)
                    V.eng.tensor_tensor_scan(l(B), l(f), l(zero), B[:, 0:1], ALU.add, ALU.add).then_inc(vector_done, V.one())
                    V.eng.wait_ge(vector_done, V.n)
                    V.eng.tensor_tensor(a, a, B, ALU.subtract).then_inc(vector_done, V.one())
                    V.eng.wait_ge(vector_done, V.n)
                    V.eng.tensor_tensor_scan(c(M), c(a), c(a), 0.0, ALU.max, ALU.max).then_inc(vector_done, V.one())
                    V.eng.wait_ge(vector_done, V.n)
                    V.eng.tensor_tensor_scan(l(M), l(a), l(a), M[:, 0:1], ALU.max, ALU.max).then_inc(vector_done, V.one())
                V.eng.wait_ge(vector_done, V.n)
                V.eng.tensor_tensor(f, B, M, ALU.add).then_inc(vector_done, V.one())
                V.eng.wait_ge(vector_done, V.n)
                V.eng.tensor_scalar(M, M, -1.0, None, ALU.mult).then_inc(vector_done, V.one())
            V.note(("V", ph, "rows"))
            V.eng.wait_ge(tensor_done, done("T", ph, "cols"))
            V.eng.wait_ge(vector_done, V.n)
            V.eng.tensor_copy(mcol[:, :], psum[4][:, 0:64]).then_inc(vector_done, V.one(("V", ph, "cols")))

        def mgate_A(A, ph):
            for d in range(2):
                log_sigmoid(None, A, ph, d, None, mrow(d, 2), mrow(d, 3))
            A.eng.wait_ge(vector_done, done("V", ph, "cols"))
            for d in range(2):
                c = mcol[:, d * 32 + 16:d * 32 + 32]
                A.eng.wait_ge(scalar_done, A.n)
                A.eng.activation(c, c, ACT.Exp, scale=-1.0).then_inc(scalar_done, A.one())

        def mlstm_T(T, ph):
            w = 0
            for h in range(MH):
                for s in range(4):
                    sb_ = psum[s % 2]
                    n = 4 * h + s
                    if n >= 2:
                        T.eng.wait_ge(vector_done, done("V", ph, "pt", n - 2))
                    i = T.eng.matmul(sb_[:, :], f512(4 + h)[:, s * P:(s + 1) * P], f512(h), start=True, stop=True)
                    i.then_inc(tensor_done, T.one(("T", ph, "qk", n)))
                    for d in range(2):
                        if w >= 2:
                            T.eng.wait_ge(scalar_done, done("A", ph, "w", w - 2))
                        for a, b in runs(REACH[d][s]):
                            i = T.eng.matmul(psum[2 + w % 2][:, a:b], const("pick8", h * P, (h + 1) * P, slice(0, MH)), mrow(d, 3)[:, a:b],
                                             start=True, stop=(not a <= s * P < b), skip_group_check=True)
                            if a <= s * P < b:
                                i = T.eng.matmul(psum[2 + w % 2][:, s * P:(s + 1) * P], ident, const("later" if d == 0 else "earlier"),
                                                 start=False, stop=True, skip_group_check=True)
                        i.then_inc(tensor_done, T.one(("T", ph, "wexp", w)))
                        w += 1
                for d in range(2):
                    g = 2 * h + d
                    T.eng.wait_ge(vector_done, done("V", ph, "pt", 4 * h + 3))
                    if g >= 2:
                        T.eng.wait_ge(vector_done, done("V", ph, "h", g - 2))
                    for t in range(4):
                        srcs = [s for s in range(4) if t in REACH[d][s]]
                        for m, s in enumerate(srcs):
                            p = PT(d, s)[:, t * P:(t + 1) * P]
                            T.eng.matmul(psum[4 + g % 2][:, t * P:(t + 1) * P], p, row3(s, 1024 + h * P, 1024 + (h + 1) * P),
                                         start=(m == 0), stop=(m == len(srcs) - 1))
                            i = T.eng.matmul(psum[6 + g % 2][:, t:t + 1], p, ones[:, :],
                                             start=(m == 0), stop=(m == len(srcs) - 1))
                    i.then_inc(tensor_done, T.one(("T", ph, "sum", g)))

        def mlstm_A(A, ph):
            w = 0
            for h in range(MH):
                for s in range(4):
                    for d in range(2):
                        A.eng.wait_ge(tensor_done, done("T", ph, "wexp", w))
                        if w >= 4:
                            A.eng.wait_ge(vector_done, done("V", ph, "pt", (w - 4) // 2))
                        for a, b in runs(REACH[d][s]):
                            A.eng.wait_ge(scalar_done, A.n)
                            A.eng.activation(WT(w)[:, a:b], psum[2 + w % 2][:, a:b], ACT.Exp,
                                                    bias=mcol[:, d * 32 + s * 4 + h:d * 32 + s * 4 + h + 1]).then_inc(scalar_done, A.one())
                        A.note(("A", ph, "w", w))
                        w += 1

        def mlstm_V(V, ph):
            w = 0

            def finish(g):
                h, d = g // 2, g % 2
                V.eng.wait_ge(tensor_done, done("T", ph, "sum", g))
                den = psum[6 + g % 2][:, 0:4]
                r = st2[:, 0:4]
                V.eng.wait_ge(vector_done, V.n)
                V.eng.tensor_copy(st2[:, 4:8], den).then_inc(vector_done, V.one())
                V.eng.wait_ge(vector_done, V.n)
                V.eng.scalar_tensor_tensor(out=r, in0=st2[:, 4:8], scalar=-1.0, in1=st2[:, 4:8], op0=ALU.mult, op1=ALU.max).then_inc(vector_done, V.one())
                e = mcol[:, d * 32 + 16:d * 32 + 32].rearrange("p (t h) -> p t h", h=MH)[:, :, h]
                V.eng.wait_ge(vector_done, V.n)
                V.eng.tensor_tensor(r, r, e, ALU.max).then_inc(vector_done, V.one())
                V.eng.wait_ge(vector_done, V.n)
                V.eng.reciprocal(r, r).then_inc(vector_done, V.one())
                num = psum[4 + g % 2][:, :].rearrange("p (t e) -> p t e", e=P)
                hh = big[:, :].rearrange("p (t e) -> p t e", e=S3)[:, :, h * P:(h + 1) * P]
                rb = r.rearrange("p (t o) -> p t o", o=1).to_broadcast([P, 4, P])
                if d == 0:
                    V.eng.wait_ge(vector_done, V.n)
                    V.eng.tensor_tensor(hh, num, rb, ALU.mult).then_inc(vector_done, V.one(("V", ph, "h", g)))
                else:
                    tmp = work[:, 4096:4608].rearrange("p (t e) -> p t e", e=P)
                    V.eng.wait_ge(vector_done, V.n)
                    V.eng.tensor_tensor(tmp, num, rb, ALU.mult).then_inc(vector_done, V.one(("V", ph, "h", g)))
                    V.eng.wait_ge(vector_done, V.n)
                    V.eng.tensor_tensor(hh, hh, tmp, ALU.add).then_inc(vector_done, V.one())

            for h in range(MH):
                for s in range(4):
                    n = 4 * h + s
                    V.eng.wait_ge(tensor_done, done("T", ph, "qk", n))
                    if h >= 1:
                        V.eng.wait_ge(tensor_done, done("T", ph, "sum", 2 * h - 1))
                    for d in range(2):
                        V.eng.wait_ge(scalar_done, done("A", ph, "w", w))
                        for a, b in runs(REACH[d][s]):
                            V.eng.wait_ge(vector_done, V.n)
                            V.eng.tensor_tensor(PT(d, s)[:, a:b], psum[s % 2][:, a:b], WT(w)[:, a:b], ALU.mult).then_inc(vector_done, V.one())
                        w += 1
                    V.note(("V", ph, "pt", n))
                for d in range(2):
                    finish(2 * h + d)

        def mout_A(A, ph):
            for t in ALL:
                A.eng.wait_ge(scalar_done, A.n)
                A.eng.activation(row3(t, 1536, 2048), row3(t, 1536, 2048), ACT.Sigmoid).then_inc(scalar_done, A.one(("A", ph, "gate", t)))
            heads_rms_A(A, ph, TT * MH)

        def mout_V(V, ph):
            heads_rms_V(V, ph, [(row3(t, 0, 512), MH) for t in ALL], MD, EPS)
            for t in ALL:
                h = row3(t, 0, 512)
                V.eng.wait_ge(vector_done, V.n)
                V.eng.tensor_tensor(hv(h, MD), hv(h, MD), over(rms[:, t * MH:(t + 1) * MH], MH, MD), ALU.mult).then_inc(vector_done, V.one())
                V.eng.wait_ge(vector_done, V.n)
                V.eng.tensor_tensor(h, h, head_g[:, :], ALU.mult).then_inc(vector_done, V.one())
                V.eng.wait_ge(vector_done, V.n)
                V.eng.tensor_tensor(h, h, row3(t, 1536, 2048), ALU.mult).then_inc(vector_done, V.one())

        def turns_mout():
            return [([row3(t, h * P, (h + 1) * P) for t in ALL], nT[:, h, :], 1.0) for h in range(MH)]

        def turns_sub():
            return [([big[:, j * S2 + h * P:j * S2 + (h + 1) * P] for j in range(2)], nT[:, h, SEQ:512], 1.0) for h in range(NH)]

        none = lambda g: []

        def lay(kind, layer, k):
            base = {"attn": 0, "ffn": 16}[kind] + layer * 8 + k
            return veccol[:, base:base + 1]

        def tap1(layer):
            c = lambda j, f: convcol[:, layer * 88 + j * 22 + f:layer * 88 + j * 22 + f + 1]
            return c

        def tap2(layer):
            def c(u, j, f):
                o = (2 + 2 * layer) * 88 + 44 * j + 22 * u + f
                return convcol[:, o:o + 1]
            return c

        phases = []

        def phase(name, T=None, V=None, A=None, G=None):
            phases.append((name, {"T": T, "V": V, "A": A, "G": G}))

        vrows, crow = work[0:80, 0:P], [work[0:88, P * (1 + i):P * (2 + i)] for i in range(6)]

        def setup_T(T):
            T.eng.wait_ge(loaded, 16 * N_LOADS)
            T.eng.transpose(psum[0][:, 0:80], vrows, const("ident", 0, 80, slice(0, 80)))
            for i in range(4):
                T.eng.transpose(psum[1][:, i * 88:(i + 1) * 88], crow[i], const("ident", 0, 88, slice(0, 88)))
            for i in range(4, 6):
                m = T.eng.transpose(psum[2][:, (i - 4) * 88:(i - 3) * 88], crow[i], const("ident", 0, 88, slice(0, 88)))
            m.then_inc(tensor_done, T.one(("T", "setup", "cols")))

        def setup_V(V):
            V.eng.wait_ge(loaded, 16 * N_LOADS)
            V.eng.wait_ge(vector_done, V.n)
            V.eng.memset(ones[:, :], 1.0).then_inc(vector_done, V.one())
            V.eng.wait_ge(tensor_done, done("T", "setup", "cols"))
            V.eng.wait_ge(vector_done, V.n)
            V.eng.tensor_copy(veccol[:, :], psum[0][:, 0:80]).then_inc(vector_done, V.one(("V", "setup", "vec")))
            V.eng.wait_ge(vector_done, V.n)
            V.eng.tensor_copy(convcol[:, 0:352], psum[1][:, 0:352]).then_inc(vector_done, V.one())
            V.eng.wait_ge(vector_done, V.n)
            V.eng.tensor_copy(convcol[:, 352:528], psum[2][:, 0:176]).then_inc(vector_done, V.one())
            V.eng.wait_ge(vector_done, V.n)
            V.eng.tensor_scalar(nsink[:, :], sink[:, :], -1.0, None, ALU.mult).then_inc(vector_done, V.one())
            V.eng.wait_ge(vector_done, V.n)
            V.eng.tensor_scalar(sub_g[:, :], sub_g[:, :], 1.0 - LAM_INIT, None, ALU.mult).then_inc(vector_done, V.one())
            l4 = lam_in[:, :].rearrange("p (a b e) -> p a b e", a=2, b=2)
            pr = work[:, 2048:2176].rearrange("p (a e) -> p a e", a=2)
            V.eng.wait_ge(vector_done, V.n)
            V.eng.tensor_tensor(pr, l4[:, :, 0, :], l4[:, :, 1, :], ALU.mult).then_inc(vector_done, V.one())
            V.eng.wait_ge(vector_done, V.n)
            V.eng.tensor_reduce(lam[:, 0:2], pr, AX_X, ALU.add).then_inc(vector_done, V.one(("V", "setup", "dots")))
            V.eng.wait_ge(scalar_done, done("A", "setup", "exps"))
            V.eng.wait_ge(vector_done, V.n)
            V.eng.tensor_tensor(lam[:, 5:6], lam[:, 3:4], lam[:, 2:3], ALU.subtract).then_inc(vector_done, V.one())
            V.eng.wait_ge(vector_done, V.n)
            V.eng.tensor_scalar(lam[:, 4:5], lam[:, 5:6], LAM_INIT, None, ALU.subtract).then_inc(vector_done, V.one())

        def setup_A(A):
            A.eng.wait_ge(vector_done, done("V", "setup", "dots"))
            A.eng.wait_ge(scalar_done, A.n)
            A.eng.activation(lam[:, 2:4], lam[:, 0:2], ACT.Exp).then_inc(scalar_done, A.one(("A", "setup", "exps")))
            A.eng.wait_ge(scalar_done, A.n)
            A.eng.activation(silu_c.rearrange("p (k s) -> p s k", s=2),
                                    veccol[:, 64:80].rearrange("p (s k) -> p s k", s=2), ACT.Silu).then_inc(scalar_done, A.one())

        phase("setup", setup_T, setup_V, setup_A)

        def norm_phase(ph, tiles, which):
            phase(ph, lambda T: norm_T(T, ph, tiles),
                  lambda V: (norm_V(V, ph, tiles), norm_evac(V, ph, tiles, which, 0)),
                  lambda A: (norm_A(A, ph, tiles), norm_evac(A, ph, tiles, which, 1)))

        def proj_phase(ph, cuts, tiles_of, stride, base=0):
            def cp(E, mine):
                for c, (a, b) in enumerate(cuts):
                    E.eng.wait_ge(tensor_done, done("T", ph, "out", c))
                    for j, t in enumerate(tiles_of(c)):
                        if j % 2 == mine:
                            dst = big[:, (t - base) * stride + a:(t - base) * stride + b]
                            src = psum[4 * (c % 2) + j][:, 0:b - a]
                            if E.name == "V":
                                E.eng.wait_ge(E.sem, E.n)
                                E.eng.tensor_copy(dst, src).then_inc(E.sem, E.one())
                            else:
                                E.eng.wait_ge(E.sem, E.n)
                                E.eng.activation(dst, src, ACT.Copy).then_inc(E.sem, E.one())
                    E.note((E.name, ph, "out", c))
            phase(ph, lambda T: proj_T(T, ph, cuts, tiles_of), lambda V: cp(V, 0), lambda A: cp(A, 1))

        def out_phase(ph, tiles, gate_idx):
            streams = sorted({t // 2 for t in tiles})
            if gate_idx is not None:
                phase(ph + " gates", lambda T: gates_T(T, ph, gate_idx, streams), None, lambda A: gates_A(A, ph, streams))
            phase(ph, lambda T: (proj_T(T, ph, OUT_CUTS, lambda c: tiles)), lambda V: residual_V(V, ph, OUT_CUTS, tiles, gate_idx is not None),
                  lambda A: [A.note(("A", ph, "out", c)) for c in range(2)])

        def ffn_phases(ph, tiles, layer, block, gate_idx):
            n = len(tiles) * P
            lo = 512 - n
            if block == 1:
                tap = tap1(layer)
                phase(ph + " up", lambda T: up_T(T, ph + " up", lo, n), lambda V: up_V_causal(V, ph + " up", n, tap),
                      lambda A: up_A(A, ph + " up", n, (lambda u, f: tap(2, f), lambda u, f: tap(3, f)), False))
            else:
                tap = tap2(layer)
                phase(ph + " up", lambda T: up_T(T, ph + " up", lo, n), lambda V: up_V_both(V, ph + " up", n, tap),
                      lambda A: up_A(A, ph + " up", n, (lambda u, f: tap(u, 1, f), lambda u, f: tap(u, 3, f)), True))
            streams = sorted({t // 2 for t in tiles})
            if gate_idx is not None:
                phase(ph + " gates", lambda T: gates_T(T, ph, gate_idx, streams), None, lambda A: gates_A(A, ph, streams))
            phase(ph + " down", lambda T: down_T(T, ph + " down", tiles),
                  lambda V: residual_V(V, ph + " down", OUT_CUTS, tiles, gate_idx is not None))

        def turn_phase(ph, groups, V=None):
            phase(ph, lambda T: turns_T(T, ph, groups, none), lambda V_: turns_evac(V_, ph, groups, 0), lambda A: turns_evac(A, ph, groups, 1))

        def att_phase(ph, jobs):
            phase(ph, lambda T: att_T(T, ph, jobs), lambda V: att_V(V, ph, jobs), lambda A: att_A(A, ph, jobs))

        norm_phase("1.0 norm", LAT, lambda k, s: (lay("attn", 0, k), None))
        proj_phase("1.0 in", HYB_CUTS, lambda c: LAT, S1, 2)

        def rope_l0(V):
            for j in range(2):
                cs, sn = const("cos1", j * DH, (j + 1) * DH), const("sin1", j * DH, (j + 1) * DH)
                rope_V(V, big[:, j * S1:j * S1 + 1024], 16, cs, sn, False)
        phase("1.0 rope", None, rope_l0)
        turn_phase("1.0 turn", turns_l0())

        def fox_T(T):
            for j in range(2):
                i = T.eng.matmul(psum[0][0:NH, j * P:(j + 1) * P], big[:, j * S1 + 3072:j * S1 + 3080], ident, start=True, stop=True)
            i.then_inc(tensor_done, T.one(("T", "fox", "rows")))

        def fox_V(V):
            f, t1, c, t2 = (frow[:, i * SEQ:(i + 1) * SEQ] for i in range(4))
            V.eng.wait_ge(tensor_done, done("T", "fox", "rows"))
            V.eng.wait_ge(vector_done, V.n)
            V.eng.tensor_scalar(f, psum[0][0:NH, 0:SEQ], fbias[0:NH, 0:1], None, ALU.add).then_inc(vector_done, V.one())
            log_sigmoid(V, None, "fox", 0, f, t1, t2)
            V.eng.wait_ge(vector_done, V.n)
            V.eng.memset(t1, 0.0).then_inc(vector_done, V.one())
            V.eng.wait_ge(vector_done, V.n)
            V.eng.tensor_tensor_scan(c, f, t1, 0.0, ALU.add, ALU.add).then_inc(vector_done, V.one())

        def fox_A(A):
            log_sigmoid(None, A, "fox", 0, None, frow[:, SEQ:2 * SEQ], frow[:, 3 * SEQ:4 * SEQ])
        phase("1.0 decay", fox_T, fox_V, fox_A)

        ja = jobs_l0("dilated")
        jb = jobs_l0("forget")
        for j in jb:
            j["group"] += 4
        att_phase("1.0 attention", ja + jb)
        out_phase("1.0 out", LAT, None)
        norm_phase("1.0 norm2", LAT, lambda k, s: (lay("ffn", 0, k), None))
        ffn_phases("1.0 ffn", LAT, 0, 1, None)
        norm_phase("1.1 norm", LAT, lambda k, s: (lay("attn", 1, k), None))
        proj_phase("1.1 in", QKV_CUTS, lambda c: LAT, S2, 2)

        def rope_l1(V):
            for j in range(2):
                cs, sn = const("cos1", j * DH, (j + 1) * DH), const("sin1", j * DH, (j + 1) * DH)
                for part in range(2):
                    rope_V(V, big[:, j * S2 + part * 1024:j * S2 + (part + 1) * 1024], 16, cs, sn, False)
        phase("1.1 rope", None, rope_l1)
        turn_phase("1.1 turn", turns_l1())
        att_phase("1.1 attention", jobs_l1())

        def subln_V(V):
            o = lambda j: big[:, j * S2:j * S2 + D]
            heads_rms_V(V, "subln", [(o(j), NH) for j in range(2)], P, SUB_EPS)
            for j in range(2):
                h = hv(o(j), P)
                V.eng.wait_ge(vector_done, V.n)
                V.eng.tensor_tensor(h, h, over(rms[:, j * NH:(j + 1) * NH], NH, P), ALU.mult).then_inc(vector_done, V.one())
                V.eng.wait_ge(vector_done, V.n)
                V.eng.tensor_tensor(h, h, under(sub_g[:, :], NH, P), ALU.mult).then_inc(vector_done, V.one())
        phase("1.1 subln", None, subln_V, lambda A: heads_rms_A(A, "subln", 2 * NH))
        turn_phase("1.1 turn2", turns_sub())
        out_phase("1.1 out", LAT, None)
        norm_phase("1.1 norm2", LAT, lambda k, s: (lay("ffn", 1, k), None))
        ffn_phases("1.1 ffn", LAT, 1, 1, None)

        def final_A(A):
            for j, t in enumerate(LAT):
                A.eng.wait_ge(scalar_done, A.n)
                A.eng.activation(gate[:, 0:D], xt[:, t, :], ACT.Square, scale=D ** -0.5, accum_out=stat[:, j:j + 1]).then_inc(scalar_done, A.one(("A", "final", "ms")))
            A.eng.wait_ge(vector_done, done("V", "final", "inverse"))
            A.eng.wait_ge(scalar_done, A.n)
            A.eng.activation(stat[:, 8:10], stat[:, 4:6], ACT.Sqrt).then_inc(scalar_done, A.one(("A", "final", "rstd")))

        def final_V(V):
            V.eng.wait_ge(scalar_done, done("A", "final", "ms"))
            V.eng.wait_ge(vector_done, V.n)
            V.eng.tensor_scalar(stat[:, 4:6], stat[:, 0:2], EPS, None, ALU.add).then_inc(vector_done, V.one())
            V.eng.wait_ge(vector_done, V.n)
            V.eng.reciprocal(stat[:, 4:6], stat[:, 4:6]).then_inc(vector_done, V.one(("V", "final", "inverse")))
            V.eng.wait_ge(scalar_done, done("A", "final", "rstd"))
            for j, t in enumerate(LAT):
                V.eng.wait_ge(vector_done, V.n)
                V.eng.scalar_tensor_tensor(out=xt[:, t, :], in0=xt[:, t, :], scalar=stat[:, 8 + j:9 + j], in1=final_g[:, :],
                                                  op0=ALU.mult, op1=ALU.mult).then_inc(vector_done, V.one())
        phase("1 final", None, final_V, final_A)

        def shift_scale(m):
            return lambda k, s: (acol[:, m * 16 + 2 * k + s:m * 16 + 2 * k + s + 1],
                                 modcol[:, 2 * m * 16 + 2 * k + s:2 * m * 16 + 2 * k + s + 1])

        def ada_bias_load(G, layer):
            for j in range(4):
                for s in range(2):
                    src = io["ada_b_2"][layer:layer + 1, :].rearrange("o (g j n) -> o g j n", g=3, j=4)[:, :, j, :]
                    G.eng.dma_start(mod[32 * j + s:32 * j + s + 1, :].rearrange("p (g n) -> p g n", g=3), src).then_inc(adab_in, 16)

        def ada_phase(layer):
            ph = f"2.{layer} ada"
            phase(ph, lambda T: ada_T(T, ph), lambda V: ada_V(V, ph, layer), None, lambda G: ada_bias_load(G, layer))

        ada_phase(0)
        norm_phase("2.0 norm", ALL, shift_scale(0))
        proj_phase("2.0 in", EVEN_CUTS, lambda c: ALL, S3)
        turn_phase("2.0 turn", turns_e(0))
        phase("2.0 mgate", lambda T: mgate_T(T, "mg"), lambda V: mgate_V(V, "mg"), lambda A: mgate_A(A, "mg"))
        phase("2.0 mlstm", lambda T: mlstm_T(T, "ml"), lambda V: mlstm_V(V, "ml"), lambda A: mlstm_A(A, "ml"))
        phase("2.0 mout", None, lambda V: mout_V(V, "mo"), lambda A: mout_A(A, "mo"))
        turn_phase("2.0 turn2", turns_mout())

        def dup_V(V, t, k):
            d = kdup(t).rearrange("p (g two e) -> p g two e", g=2, two=2)
            for m in range(2):
                V.eng.wait_ge(vector_done, V.n)
                V.eng.tensor_copy(d[:, :, m, :], k.rearrange("p (g e) -> p g e", g=2)).then_inc(vector_done, V.one())

        def swa_prep(V):
            rows_ = [(row3(t, 2064, 2704), NH + 2) for t in ALL]
            heads_rms_V(V, "swa", rows_, DH, EPS)
            for t in ALL:
                q, k = row3(t, 2064, 2576), row3(t, 2576, 2704)
                heads_scale_V(V, q, NH, 10 * t, qk_g[:, 0:DH])
                heads_scale_V(V, k, 2, 10 * t + NH, qk_g[:, DH:2 * DH])
                if t in LAT:
                    cs, sn = const("cos2", (t - 2) * DH, (t - 1) * DH), const("sin2", (t - 2) * DH, (t - 1) * DH)
                    rope_V(V, row3(t, 2064, 2704), NH + 2, cs, sn, True)
                dup_V(V, t, k)
        phase("2.0 qk", None, swa_prep, lambda A: heads_rms_A(A, "swa", 40))
        turn_phase("2.0 turn3", turns_e(1))
        js = jobs_e(0)
        jl = jobs_e(1)
        for j in jl:
            j["group"] += 4
        att_phase("2.0 attention", js + jl)
        out_phase("2.0 out", ALL, 2)
        norm_phase("2.0 norm2", ALL, shift_scale(1))
        ffn_phases("2.0 ffn", ALL, 0, 2, 5)
        ada_phase(1)
        norm_phase("2.1 norm", ALL, shift_scale(0))

        def bias_load(G):
            rpb = io["na_rpb_2"]
            for h in range(NH):
                for t in range(2):
                    for r in range(2):
                        off = h * 465 + (r - 2 * t - 1 + 7) * 31 - 63 + 15
                        src = bass.AP(tensor=rpb.tensor, offset=off, ap=[[1, 64], [31, 4], [1, 64]])
                        G.eng.dma_start(nbias(h, t)[64 * r:64 * r + 64, :].rearrange("p (a b) -> p a b", a=4), src).then_inc(bias_in, 16)

        ODD_T = lambda c: LAT if c in (0, 2) else ALL
        proj_phase("2.1 in", ODD_CUTS, ODD_T, S4)
        phases[-1][1]["G"] = bias_load

        def odd_prep(V):
            rows_, g, at = [], [], []
            for t in ALL:
                rows_ += [(row4(t, 512, 640), 2), (row4(t, 1280, 1792), NH)]
                g += [3, 5]
                if t in LAT:
                    rows_ += [(row4(t, 0, 512), NH), (row4(t, 768, 1280), NH)]
                    g += [2, 4]
            heads_rms_V(V, "odd", rows_, DH, EPS)
            n = 0
            for (row, m), gi in zip(rows_, g):
                heads_scale_V(V, row, m, n, qk_g[:, gi * DH:(gi + 1) * DH])
                n += m
            for t in ALL:
                if t in LAT:
                    cs, sn = const("cos2", (t - 2) * DH, (t - 1) * DH), const("sin2", (t - 2) * DH, (t - 1) * DH)
                    rope_V(V, row4(t, 0, 640), NH + 2, cs, sn, True)
                dup_V(V, t, row4(t, 512, 640))
        phase("2.1 qk", None, odd_prep, lambda A: heads_rms_A(A, "odd", 72))
        turn_phase("2.1 turn", turns_o())
        jg = jobs_o("global")
        jn = jobs_o("near")
        for j in jn:
            j["group"] += 4

        def odd_att_T(T):
            T.eng.wait_ge(bias_in, 16 * 4 * NH)
            att_T(T, "2.1 attention", jg + jn)
        phase("2.1 attention", odd_att_T, lambda V: att_V(V, "2.1 attention", jg + jn), lambda A: att_A(A, "2.1 attention", jg + jn))
        out_phase("2.1 out", LAT, 2)
        norm_phase("2.1 norm2", LAT, shift_scale(1))
        ffn_phases("2.1 ffn", LAT, 1, 2, 5)

        def bcast(v, n):
            return bass.AP(tensor=v.tensor, offset=v.offset, ap=[[0, P], [1, n]])

        rows = lambda a: a.rearrange("(r n) -> r n", n=P)
        loads = [
            (con[:, :], io["const"]),
            (xt[:, 2:4, :], io["x"][0].rearrange("(t p) d -> p t d", p=P)),
            (xt[:, 0:2, :], io["ctx_2"][0].rearrange("(t p) d -> p t d", p=P)),
            (vrows[0:16, :], rows(io["attn_norm"].rearrange("a n -> (a n)"))),
            (vrows[16:32, :], rows(io["ffn_norm"].rearrange("a n -> (a n)"))),
            (vrows[32:64, :], rows(io["norm_g_2"].rearrange("a b n -> (a b n)"))),
            (vrows[64:72, :], rows(io["c_ctx_2"])),
            (vrows[72:80, :], rows(io["c_2"][0])),
            (final_g[:, :], bcast(io["final_norm"], D)),
            (head_g[:, :], bcast(io["mlstm_head_g_2"], 512)),
            (sub_g[:, :], bcast(io["diff_subln"], P)),
            (qk_g[:, 0:P], bcast(io["swa_qk_g_2"], P)),
            (qk_g[:, P:2 * P], bcast(io["gqa_qk_g_2"], P)),
            (qk_g[:, 2 * P:3 * P], bcast(io["na_qk_g_2"], P)),
            (sink[:, :], bcast(io["swa_sink_2"], NH)),
            (lam_in[:, :], bcast(io["diff_lambda"], 256)),
            (gbias[0:MH, :], io["mlstm_gate_b_2"][0].rearrange("(g h) -> h g", h=MH)),
            (fbias[0:NH, :], io["hyb_b_f"][0].rearrange("(h o) -> h o", o=1)),
        ]
        for l in range(2):
            loads.append((crow[l][0:66, :], rows(io["ffn_conv_w"][l].rearrange("a n -> (a n)"))))
            loads.append((crow[l][66:88, :], rows(io["ffn_conv_b"][l])))
            w2 = rows(io["ffn_conv_w_2"][l].rearrange("a n -> (a n)"))
            loads.append((crow[2 + 2 * l][0:88, :], w2[0:88, :]))
            loads.append((crow[3 + 2 * l][0:44, :], w2[88:132, :]))
            loads.append((crow[3 + 2 * l][44:88, :], rows(io["ffn_conv_b_2"][l])))
        N_LOADS = len(loads)

        block = ctx.enter_context(nc.Block())

        def run(E):
            before = None
            for name, parts in phases:
                if before is not None:
                    fence(E, before)
                if parts[E.name] is not None:
                    parts[E.name](E)
                E.note((E.name, "end", name))
                before = name
            return before

        @block.sync
        def _(sp):
            for u, (src, view) in enumerate(stream):
                if u >= SLOTS:
                    sp.wait_ge(tensor_done, done("T", "slot", u - SLOTS))
                sp.dma_start(view(wslot[:, u % SLOTS, :]), src).then_inc(slot_full[u % SLOTS], 16)
            last = phases[-1][0]
            sp.wait_ge(vector_done, done("V", "end", last))
            sp.dma_start(out[0].rearrange("(t p) d -> p t d", p=P), xt[:, 2:4, :]).then_inc(stored, 16)
            sp.wait_ge(stored, 16)

        @block.scalar
        def _(act):
            for dst, src in loads:
                act.dma_start(dst, src).then_inc(loaded, 16)
            run(Progress("A", act, scalar_done, noted))

        @block.gpsimd
        def _(pool):
            run(Progress("G", pool, gpsimd_done, noted))

        @block.tensor
        def _(pe):
            run(Progress("T", pe, tensor_done, noted))
            assert Taken.n == len(stream), (Taken.n, len(stream))

        @block.vector
        def _(dve):
            run(Progress("V", dve, vector_done, noted))


_INS = ["x", "attn_norm", "ffn_norm", "final_norm", "hyb_w_in", "hyb_b_f", "hyb_w_out", "diff_w_qkv", "diff_lambda",
        "diff_subln", "diff_w_out", "ffn_w_up", "ffn_conv_w", "ffn_conv_b", "ffn_w_down", "c_2", "ctx_2", "c_ctx_2",
        "ada_w_2", "ada_b_2", "norm_g_2", "w_out_2", "ffn_up_2", "ffn_conv_w_2", "ffn_conv_b_2", "ffn_down_2",
        "even_w_in_2", "mlstm_gate_b_2", "mlstm_head_g_2", "swa_qk_g_2", "swa_sink_2", "odd_w_in_2", "gqa_qk_g_2",
        "na_qk_g_2", "na_rpb_2"]


def kernel(**inputs):
    import concourse.bacc as bacc
    from concourse.bass_utils import run_bass_kernel_spmd

    known, noted = {}, {}
    for _ in range(2):
        nc = bacc.Bacc("TRN2", target_bir_lowering=False, num_devices=1)
        arrays, io = {}, {}
        for name in _INS + ["const"]:
            a = constants() if name == "const" else np.ascontiguousarray(inputs[name])
            arrays[f"in_{name}"] = a
            io[name] = nc.dram_tensor(f"in_{name}", a.shape, F32, kind="ExternalInput").ap()
        out = nc.dram_tensor("out_0", (1, SEQ, D), F32, kind="ExternalOutput").ap()
        noted = {}
        with nc.allow_non_contiguous_dma(reason="columns of weights, and a few small vectors"):
            program(nc, io, out, known, noted)
        known = noted
    r = run_bass_kernel_spmd(nc, [arrays], core_ids=[0])
    return r.results[0]["out_0"]
```

```python
import math
from contextlib import ExitStack

import numpy as np
import concourse.bass as bass
from concourse import mybir

ALU = mybir.AluOpType
ACT = mybir.ActivationFunctionType
F32 = mybir.dt.float32
AX_X = mybir.AxisListType.X

P = 128
D = 1024
KT = D // P
DH = 64
NH = 8
FF = 2816
FC = FF // P
SEQ = 256
TT = 4
CTX, LAT, ALL = (0, 1), (2, 3), (0, 1, 2, 3)
MH, MD = 4, 128
SLOTS = 4
SLOT = 2048
BIG_N = 4 * 2836
BIG_NEG = 1e30
LAM_INIT = 0.8 - 0.6 * math.exp(-0.3 * 1)
EPS, SUB_EPS = 1e-6, 1e-5

WIDTHS = dict(ident=128, negflip=128, dilated=512, causal=256, window=1024, nbhood=512, later=128, earlier=128,
              pick8=1024, pick2=256, cos1=128, sin1=128, cos2=128, sin2=128)
AT = {}
_n = 0
for _k, _w in WIDTHS.items():
    AT[_k] = (_n, _w)
    _n += _w
NCONST = _n


def constants():
    c = {k: np.zeros((P, w), np.float32) for k, w in WIDTHS.items()}
    c["ident"][:] = np.eye(P)
    c["negflip"][:] = -np.eye(P)[::-1]
    t = np.arange(SEQ)
    delta = t[:, None] - t[None, :]
    count = ((delta >= 0) & (delta <= 128)).astype(int) + ((delta >= 0) & (delta % 4 == 0)) + ((delta >= 0) & (delta % 16 == 0))
    dil = np.where(count > 0, -np.log(np.maximum(count, 1)), BIG_NEG).astype(np.float32)
    c["dilated"][:] = dil.reshape(2, P, SEQ).transpose(1, 0, 2).reshape(P, -1)
    p = np.arange(P)
    c["causal"][:, P:] = np.where(p[None, :] > p[:, None], BIG_NEG, 0)
    win = np.where(np.abs(delta) <= 128, 0, BIG_NEG).astype(np.float32).reshape(2, P, SEQ)
    w = c["window"].reshape(P, 2, 512)
    w[:, :, SEQ:] = win.transpose(1, 0, 2)
    col = np.arange(64)
    first = np.clip(col - 8, 0, 48)
    ok = (col[None, :] >= first[:, None]) & (col[None, :] < first[:, None] + 16)
    c["nbhood"][:, SEQ:] = np.tile(np.where(ok, 0, BIG_NEG), (2, 4))
    c["later"][:] = np.where(p[:, None] > p[None, :], -BIG_NEG, 0)
    c["earlier"][:] = np.where(p[:, None] < p[None, :], -BIG_NEG, 0)
    for h in range(8):
        c["pick8"][h, h * P:(h + 1) * P] = 1
    for j in range(4):
        for s in range(2):
            c["pick2"][32 * j + s, s * P:(s + 1) * P] = 1
    f = np.float32
    inv = (1.0 / (f(10000.0) ** (np.arange(0, DH, 2, dtype=f) / f(DH)))).astype(f)
    ang = np.arange(SEQ, dtype=f)[:, None] * inv[None, :]
    ang = np.concatenate([ang, ang], -1)
    sgn = np.where(np.arange(DH) < DH // 2, -1, 1).astype(f)
    tile = lambda a: a.astype(f).reshape(2, P, DH).transpose(1, 0, 2).reshape(P, -1)
    c["cos1"][:], c["sin1"][:] = tile(np.cos(ang)), tile(np.sin(ang) * sgn)
    freq = (f(10000.0) ** (-np.arange(0, 32, 2, dtype=f) / f(32))).astype(f)
    r = (t // 64).astype(f)[:, None] * freq[None, :]
    k = (t % 64).astype(f)[:, None] * freq[None, :]
    ang = np.concatenate([r, r, k, k], -1)
    sgn = np.where(np.arange(DH) % 32 < 16, -1, 1).astype(f)
    c["cos2"][:], c["sin2"][:] = tile(np.cos(ang)), tile(np.sin(ang) * sgn)
    return np.ascontiguousarray(np.concatenate([c[k] for k in WIDTHS], 1))


class Progress:

    def __init__(self, name, eng, sem, noted):
        self.name, self.eng, self.sem, self.noted, self.n = name, eng, sem, noted, 0

    def one(self, step=None):
        self.n += 1
        if step is not None:
            self.note(step)
        return 1

    def note(self, step):
        self.noted[step] = self.n


def program(nc, io, out, known, noted, debug=None):
    with ExitStack() as ctx:
        def sb(name, width, rows=P):
            return ctx.enter_context(nc.sbuf_tensor(name, [rows, width], F32))

        ring = sb("ring", SLOTS * SLOT)
        x_t = sb("x_tokens", TT * D)
        nt = sb("normed_features", KT * 512)
        big = sb("big", BIG_N)
        qkt = sb("qk_features", 7168)
        work = sb("work", 4608)
        gate = sb("gate_rows", 2048)
        con = sb("con", NCONST)
        final_g = sb("final_g", D)
        head_g = sb("head_g", 512)
        sub_g = sb("sub_g", P)
        qk_g = sb("qk_g", 3 * P)
        sink = sb("sink", NH)
        nsink = sb("nsink", NH)
        lam_in = sb("lam_in", 256)
        lam = sb("lam", 8)
        veccol = sb("veccol", 80)
        convcol = sb("convcol", 6 * 88)
        mod = sb("mod", 2 * 3 * 512)
        modcol = sb("modcol", 2 * 64)
        acol = sb("acol", 2 * 2 * 16)
        gbias = sb("gbias", 4)
        fbias = sb("fbias", 1)
        stat = sb("stat", 64)
        mxs = sb("mxs", 3 * 4)
        mcol = sb("mcol", 64)
        st2 = sb("st2", 128)
        rms = sb("rms", 96)
        psum = [ctx.enter_context(nc.psum_tensor(f"bank{i}", [P, 512], F32)) for i in range(8)]

        def sem(name):
            return ctx.enter_context(nc.semaphore(name))

        tensor_done, vector_done, scalar_done, gpsimd_done = sem("tensor_done"), sem("vector_done"), sem("scalar_done"), sem("gpsimd_done")
        slot_full = [sem(f"slot{i}_full") for i in range(SLOTS)]
        loaded = sem("small_inputs_loaded")
        bias_in = sem("neighbour_bias_loaded")
        adab_in = sem("ada_bias_loaded")
        stored = sem("output_stored")
        SEM = {"T": tensor_done, "V": vector_done, "A": scalar_done, "G": gpsimd_done}

        def done(*step):
            return known.get(step, 0)

        def const(name, a=0, b=None, rows=slice(0, P)):
            o, w = AT[name]
            return con[rows, o + a:o + (w if b is None else b)]

        ident = const("ident")
        xt = x_t[:, :].rearrange("p (t d) -> p t d", t=TT)
        nT = nt[:, :].rearrange("p (k t) -> p k t", k=KT)
        wslot = ring[:, :].rearrange("p (s n) -> p s n", s=SLOTS)

        stream = []

        def add_proj(w, cuts):
            for a, b in cuts:
                for half in range(2):
                    src = w[half * 512:half * 512 + 512, a:b].rearrange("(k p) n -> p k n", p=P)
                    stream.append((src, lambda s, n=b - a: s.rearrange("p (k n) -> p k n", k=4)[:, :, 0:n]))

        def cuts_of(n):
            return [(a, min(a + 512, n)) for a in range(0, n, 512)]

        HYB_CUTS = [(3072, 3080), (0, 512), (512, 1024), (1536, 2048), (2048, 2560), (1024, 1536), (2560, 3072)]
        QKV_CUTS = cuts_of(3072)
        OUT_CUTS = cuts_of(1024)
        EVEN_CUTS = [(2048, 2448), (2448, 2832), (0, 512), (512, 1024), (1536, 2048), (1024, 1536)]
        ODD_CUTS = [(512, 768), (0, 512), (768, 1280), (1280, 1792), (1792, 2304)]

        ADA_AFTER = [2 if f >= FC - 2 else 1 for f in range(FC)]

        def ada_slots(w):
            return [(w[k * P:(k + 1) * P, g * 2048:(g + 1) * 2048], lambda s: s) for g in range(3) for k in range(KT)]

        def add_up(w, ada=None):
            left = ada_slots(ada) if ada is not None else []
            for f in range(FC):
                src = w.rearrange("(k p) (u f c) -> p u k f c", p=P, u=2, c=P)[:, :, :, f, :]
                stream.append((src, lambda s: s.rearrange("p (u k c) -> p u k c", u=2, c=P)))
                if left:
                    stream.extend(left[:ADA_AFTER[f]])
                    left = left[ADA_AFTER[f]:]

        def add_down_rows(w):
            for f in range(0, FC, 2):
                stream.append((w[f * P:(f + 2) * P, :].rearrange("(c p) n -> p c n", p=P),
                               lambda s: s.rearrange("p (c n) -> p c n", c=2)))

        def add_down_halves(w):
            for half in range(2):
                for f in range(0, FC, 4):
                    m = min(4, FC - f)
                    stream.append((w[f * P:(f + m) * P, half * 512:half * 512 + 512].rearrange("(c p) n -> p c n", p=P),
                                   lambda s, m=m: s.rearrange("p (c n) -> p c n", c=4)[:, 0:m, :]))

        add_proj(io["hyb_w_in"][0], HYB_CUTS)
        add_proj(io["hyb_w_out"][0], OUT_CUTS)
        add_up(io["ffn_w_up"][0], io["ada_w_2"][0]); add_down_rows(io["ffn_w_down"][0])
        add_proj(io["diff_w_qkv"][0], QKV_CUTS)
        add_proj(io["diff_w_out"][0], OUT_CUTS)
        add_up(io["ffn_w_up"][1], io["ada_w_2"][1]); add_down_rows(io["ffn_w_down"][1])
        add_proj(io["even_w_in_2"][0], EVEN_CUTS)
        add_proj(io["w_out_2"][0], OUT_CUTS)
        add_up(io["ffn_up_2"][0]); add_down_halves(io["ffn_down_2"][0])
        add_proj(io["odd_w_in_2"][0], ODD_CUTS)
        add_proj(io["w_out_2"][1], OUT_CUTS)
        add_up(io["ffn_up_2"][1]); add_down_rows(io["ffn_down_2"][1])


        class Taken:
            n = 0

        def take(T):
            u = Taken.n
            Taken.n += 1
            T.eng.wait_ge(slot_full[u % SLOTS], 16 * (u // SLOTS + 1))
            return wslot[:, u % SLOTS, :], ("T", "slot", u)

        def fence(E, phase):
            for o in "TVAG":
                if o != E.name:
                    E.eng.wait_ge(SEM[o], done(o, "end", phase))

        XN = [work[:, 0:1024], work[:, 1024:2048], work[:, 2048:3072], work[:, 3072:4096]]

        def norm_A(A, ph, tiles):
            n = len(tiles)
            for j, t in enumerate(tiles):
                A.eng.wait_ge(scalar_done, A.n)
                A.eng.activation(gate[:, 0:D], xt[:, t, :], ACT.Square, scale=D ** -0.5,
                                        accum_out=stat[:, j:j + 1]).then_inc(scalar_done, A.one(("A", ph, "ms")))
            A.eng.wait_ge(vector_done, done("V", ph, "inverse"))
            A.eng.wait_ge(scalar_done, A.n)
            A.eng.activation(stat[:, 8:8 + n], stat[:, 4:4 + n], ACT.Sqrt).then_inc(scalar_done, A.one(("A", ph, "rstd")))

        def norm_V(V, ph, tiles):
            n = len(tiles)
            V.eng.wait_ge(scalar_done, done("A", ph, "ms"))
            V.eng.wait_ge(vector_done, V.n)
            V.eng.tensor_scalar(stat[:, 4:4 + n], stat[:, 0:n], EPS, None, ALU.add).then_inc(vector_done, V.one())
            V.eng.wait_ge(vector_done, V.n)
            V.eng.reciprocal(stat[:, 4:4 + n], stat[:, 4:4 + n]).then_inc(vector_done, V.one(("V", ph, "inverse")))
            V.eng.wait_ge(scalar_done, done("A", ph, "rstd"))
            for j, t in enumerate(tiles):
                V.eng.wait_ge(vector_done, V.n)
                V.eng.tensor_scalar(XN[j], xt[:, t, :], stat[:, 8 + j:9 + j], None, ALU.mult).then_inc(vector_done, V.one(("V", ph, "xn", j)))

        def norm_T(T, ph, tiles):
            for j in range(len(tiles)):
                T.eng.wait_ge(vector_done, done("V", ph, "xn", j))
            for k in range(KT):
                for j in range(len(tiles)):
                    i = T.eng.transpose(psum[k][:, j * P:(j + 1) * P], XN[j][:, k * P:(k + 1) * P], ident)
                i.then_inc(tensor_done, T.one(("T", ph, "k", k)))

        def norm_evac(E, ph, tiles, which, mine):
            for k in range(KT):
                if k % 2 != mine:
                    continue
                E.eng.wait_ge(tensor_done, done("T", ph, "k", k))
                for s in sorted({t // 2 for t in tiles}):
                    lo = [j for j, t in enumerate(tiles) if t // 2 == s][0] * P
                    dst, src = nT[:, k, s * SEQ:(s + 1) * SEQ], psum[k][:, lo:lo + SEQ]
                    a, b = which(k, s)
                    if E.name == "V":
                        if b is None:
                            E.eng.wait_ge(E.sem, E.n)
                            E.eng.tensor_scalar(dst, src, a, None, ALU.mult).then_inc(E.sem, E.one())
                        else:
                            E.eng.wait_ge(E.sem, E.n)
                            E.eng.tensor_scalar(dst, src, a, b, ALU.mult, ALU.add).then_inc(E.sem, E.one())
                    elif b is None:
                        E.eng.wait_ge(E.sem, E.n)
                        E.eng.activation(dst, src, ACT.Copy, scale=a).then_inc(E.sem, E.one())
                    else:
                        E.eng.wait_ge(E.sem, E.n)
                        E.eng.activation(dst, src, ACT.Identity, scale=a, bias=b).then_inc(E.sem, E.one())

        def pieces_of(cuts, tiles_of, reader):
            out_ = []
            for c, (a, b) in enumerate(cuts):
                for j, t in enumerate(tiles_of(c)):
                    out_.append(dict(n=len(out_), c=c, j=j, t=t, a=a, b=b, reader=reader(c, j)))
            return out_

        def proj_T(T, ph, cuts, pieces, banks, between):
            for c, (a, b) in enumerate(cuts):
                mine = [p for p in pieces if p["c"] == c]
                for half in range(2):
                    w, slot = take(T)
                    w = w.rearrange("p (k n) -> p k n", k=4)
                    for p in mine:
                        if half == 0 and p["n"] >= banks:
                            q = pieces[p["n"] - banks]
                            T.eng.wait_ge(SEM[q["reader"]], done(q["reader"], ph, "piece", q["n"]))
                        for k in range(4):
                            i = T.eng.matmul(psum[p["n"] % banks][:, 0:b - a], nT[:, half * 4 + k, p["t"] * P:(p["t"] + 1) * P],
                                             w[:, k, 0:b - a], start=(half == 0 and k == 0), stop=(half == 1 and k == 3))
                        i.then_inc(tensor_done, T.one(("T", ph, "piece", p["n"]) if half else None))
                        if p is mine[-1]:
                            T.note(slot)
                        for step in between.get((c, half, p["j"]), []):
                            step(T)

        def proj_read(E, ph, cuts, pieces, banks, dst, after):
            for c in range(len(cuts)):
                for p in pieces:
                    if p["c"] != c or p["reader"] != E.name:
                        continue
                    E.eng.wait_ge(tensor_done, done("T", ph, "piece", p["n"]))
                    src = psum[p["n"] % banks][:, 0:p["b"] - p["a"]]
                    to, view, func = dst(c, p["t"], p["a"], p["b"])
                    if E.name == "V":
                        E.eng.wait_ge(E.sem, E.n)
                        E.eng.tensor_copy(to, view(src)).then_inc(E.sem, E.one(("V", ph, "piece", p["n"])))
                    else:
                        E.eng.wait_ge(E.sem, E.n)
                        E.eng.activation(to, view(src), func).then_inc(E.sem, E.one(("A", ph, "piece", p["n"])))
                if E.name == "V" and c in after:
                    E.eng.wait_ge(scalar_done, done("A", ph, "piece", [p["n"] for p in pieces if p["c"] == c and p["reader"] == "A"][-1]))
                for step in after.get(c, []):
                    step(E)

        def residual_V(V, ph, parts, gated):
            for n, (step, bank, t, a, b) in enumerate(parts):
                V.eng.wait_ge(tensor_done, done(*step))
                src = psum[bank][:, 0:b - a]
                if gated:
                    s = t // 2
                    tmp = work[:, 512 * (n % 4):512 * (n % 4) + b - a]
                    V.eng.wait_ge(vector_done, V.n)
                    V.eng.tensor_tensor(tmp, src, gate[:, s * D + a:s * D + b], ALU.mult).then_inc(vector_done, V.one())
                    src = tmp
                V.eng.wait_ge(vector_done, V.n)
                V.eng.tensor_tensor(xt[:, t, a:b], xt[:, t, a:b], src, ALU.add).then_inc(vector_done, V.one(("V", ph, "x", n)))

        def rope_V(V, row, n, cos, sin, axial):
            m = 4 if axial else 2
            q = DH // m
            src = row.rearrange("p (h m q) -> p h m q", m=m, q=q)
            o = work[:, 0:n * DH]
            o4 = o.rearrange("p (h m q) -> p h m q", m=m, q=q)
            r = work[:, 1024:1024 + n * DH]
            c3 = cos.rearrange("p (o e) -> p o e", o=1).to_broadcast([P, n, DH])
            s4 = sin.rearrange("p (o m q) -> p o m q", o=1, m=m)
            r4 = r.rearrange("p (h m q) -> p h m q", m=m, q=q)
            V.eng.wait_ge(vector_done, V.n)
            V.eng.tensor_tensor(o.rearrange("p (h e) -> p h e", e=DH), row.rearrange("p (h e) -> p h e", e=DH), c3, ALU.mult).then_inc(vector_done, V.one())
            for a in range(m):
                b = a ^ 1
                V.eng.wait_ge(vector_done, V.n)
                V.eng.tensor_tensor(r4[:, :, a, :], src[:, :, b, :], s4[:, :, a, :].to_broadcast([P, n, q]), ALU.mult).then_inc(vector_done, V.one())
            V.eng.wait_ge(vector_done, V.n)
            V.eng.tensor_tensor(row, o, r, ALU.add).then_inc(vector_done, V.one())

        hv = lambda a, e: a.rearrange("p (h e) -> p h e", e=e)
        over = lambda col, n, e: col.rearrange("p (h o) -> p h o", o=1).to_broadcast([P, n, e])
        under = lambda row, n, e: row.rearrange("p (o e) -> p o e", o=1).to_broadcast([P, n, e])

        def heads_rms_V(V, ph, rows, width, eps):
            at = 0
            for row, n in rows:
                sq = work[:, 0:n * width]
                V.eng.wait_ge(vector_done, V.n)
                V.eng.tensor_tensor(sq, row, row, ALU.mult).then_inc(vector_done, V.one())
                V.eng.wait_ge(vector_done, V.n)
                V.eng.tensor_reduce(rms[:, at:at + n], hv(sq, width), AX_X, ALU.add).then_inc(vector_done, V.one())
                at += n
            V.eng.wait_ge(vector_done, V.n)
            V.eng.tensor_scalar(rms[:, 0:at], rms[:, 0:at], 1.0 / width, eps, ALU.mult, ALU.add).then_inc(vector_done, V.one())
            V.eng.wait_ge(vector_done, V.n)
            V.eng.reciprocal(rms[:, 0:at], rms[:, 0:at]).then_inc(vector_done, V.one(("V", ph, "inverse")))
            V.eng.wait_ge(scalar_done, done("A", ph, "rstd"))

        def heads_rms_A(A, ph, n):
            A.eng.wait_ge(vector_done, done("V", ph, "inverse"))
            A.eng.wait_ge(scalar_done, A.n)
            A.eng.activation(rms[:, 0:n], rms[:, 0:n], ACT.Sqrt).then_inc(scalar_done, A.one(("A", ph, "rstd")))

        def heads_scale_V(V, row, n, at, g):
            V.eng.wait_ge(vector_done, V.n)
            V.eng.tensor_tensor(hv(row, DH), hv(row, DH), over(rms[:, at:at + n], n, DH), ALU.mult).then_inc(vector_done, V.one())
            V.eng.wait_ge(vector_done, V.n)
            V.eng.tensor_tensor(hv(row, DH), hv(row, DH), under(g, n, DH), ALU.mult).then_inc(vector_done, V.one())

        def turn_T(T, ph, groups, g, banks, needs):
            srcs = groups[g][0]
            for e, step in needs:
                T.eng.wait_ge(SEM[e], done(*step))
            if g >= len(banks):
                e = "VA"[(g - len(banks)) % 2]
                T.eng.wait_ge(SEM[e], done(e, ph, "turn", g - len(banks)))
            for j, s in enumerate(srcs):
                i = T.eng.transpose(psum[banks[g % len(banks)]][:, j * P:(j + 1) * P], s, ident)
            i.then_inc(tensor_done, T.one(("T", ph, "turn", g)))

        def turns_T(T, ph, groups, banks=tuple(range(8)), needs=()):
            for g in range(len(groups)):
                turn_T(T, ph, groups, g, banks, needs if g == 0 else ())

        def turns_evac(E, ph, groups, which, banks=tuple(range(8))):
            for g in which:
                srcs, dst, scale = groups[g]
                if "VA"[g % 2] != E.name:
                    continue
                E.eng.wait_ge(tensor_done, done("T", ph, "turn", g))
                src = psum[banks[g % len(banks)]][:, 0:len(srcs) * P]
                if E.name == "V":
                    if scale == 1.0:
                        E.eng.wait_ge(E.sem, E.n)
                        E.eng.tensor_copy(dst, src).then_inc(E.sem, E.one(("V", ph, "turn", g)))
                    else:
                        E.eng.wait_ge(E.sem, E.n)
                        E.eng.tensor_scalar(dst, src, scale, None, ALU.mult).then_inc(E.sem, E.one(("V", ph, "turn", g)))
                else:
                    E.eng.wait_ge(E.sem, E.n)
                    E.eng.activation(dst, src, ACT.Copy, scale=scale).then_inc(E.sem, E.one(("A", ph, "turn", g)))

        NB = 3
        PB = [work[:, 512 * i:512 * i + 512] for i in range(NB)]
        PTB = [work[:, 1536 + 512 * i:2048 + 512 * i] for i in range(NB)]

        def att_T(T, ph, jobs):
            n = len(jobs)
            for s in range(n + 3):
                if s < n:
                    j = jobs[s]
                    if s >= 3:
                        e = "V" if jobs[s - 3]["mask"] is not None else "A"
                        T.eng.wait_ge(SEM[e], done(e, ph, "read", s - 3))
                    bank = psum[s % 3]
                    for (a, b, terms) in j["scores"]:
                        for m, (l, r) in enumerate(terms):
                            i = T.eng.matmul(bank[:, a:b], l, r, start=(m == 0), stop=(m == len(terms) - 1))
                    i.then_inc(tensor_done, T.one(("T", ph, "scores", s)))
                if 0 <= s - 2 < n:
                    q = s - 2
                    T.eng.wait_ge(vector_done, done("V", ph, "probs", q))
                    if q >= 2:
                        T.eng.wait_ge(scalar_done, done("A", ph, "turned", q - 2))
                    for c in range(jobs[q]["n"] // P):
                        i = T.eng.transpose(psum[3 + q % 2][:, c * P:(c + 1) * P], PB[q % NB][:, c * P:(c + 1) * P], ident)
                    i.then_inc(tensor_done, T.one(("T", ph, "turn", q)))
                if 0 <= s - 3 < n:
                    q = s - 3
                    j = jobs[q]
                    T.eng.wait_ge(scalar_done, done("A", ph, "turned", q))
                    ob, oa, ob_cols, first, last, tok = j["out"]
                    if j["open"] and j["group"] >= 2:
                        T.eng.wait_ge(scalar_done, done("A", ph, "group", j["group"] - 2))
                    nc_ = j["n"] // P
                    for c in range(nc_):
                        pt = PTB[q % NB][:, c * P:(c + 1) * P]
                        o = psum[5 + j["group"] % 2][oa, ob_cols]
                        l, r = (pt, j["v"][c]) if tok else (j["v"][c], pt)
                        i = T.eng.matmul(o, l, r, start=(first and c == 0), stop=(last and c == nc_ - 1))
                    i.then_inc(tensor_done, T.one(("T", ph, "out", q)))

        def att_V(V, ph, jobs):
            n = len(jobs)
            for s in range(n + 1):
                if s < n:
                    j = jobs[s]
                    V.eng.wait_ge(tensor_done, done("T", ph, "scores", s))
                    mn = mxs[:, s % NB:s % NB + 1]
                    if s >= NB:
                        V.eng.wait_ge(tensor_done, done("T", ph, "turn", s - NB))
                    init = j["sink"] if j["sink"] is not None else None
                    if j["mask"] is not None:
                        V.eng.wait_ge(vector_done, V.n)
                        V.eng.tensor_tensor_reduce(out=PB[s % NB][:, 0:j["n"]], in0=psum[s % 3][:, 0:j["n"]], in1=j["mask"],
                                                          scale=1.0, scalar=(3e38 if init is None else init), op0=ALU.add, op1=ALU.min,
                                                          accum_out=mn).then_inc(vector_done, V.one(("V", ph, "read", s)))
                    else:
                        V.eng.wait_ge(vector_done, V.n)
                        V.eng.tensor_reduce(mn, psum[s % 3][:, 0:j["n"]], AX_X, ALU.min).then_inc(vector_done, V.one())
                        if init is not None:
                            V.eng.wait_ge(vector_done, V.n)
                            V.eng.tensor_tensor(mn, mn, init, ALU.min).then_inc(vector_done, V.one())
                    V.note(("V", ph, "max", s))
                if 0 <= s - 1 < n:
                    q = s - 1
                    j = jobs[q]
                    den, r = mxs[:, 3 + q % NB:4 + q % NB], mxs[:, 9 + q % NB:10 + q % NB]
                    V.eng.wait_ge(scalar_done, done("A", ph, "exp", q))
                    if j["sink"] is not None:
                        V.eng.wait_ge(vector_done, V.n)
                        V.eng.tensor_tensor(den, den, mxs[:, 6 + q % NB:7 + q % NB], ALU.add).then_inc(vector_done, V.one())
                    V.eng.wait_ge(vector_done, V.n)
                    V.eng.reciprocal(r, den).then_inc(vector_done, V.one())
                    if j["factor"] is None:
                        V.eng.wait_ge(vector_done, V.n)
                        V.eng.tensor_scalar(PB[q % NB][:, 0:j["n"]], PB[q % NB][:, 0:j["n"]], r, None, ALU.mult).then_inc(vector_done, V.one(("V", ph, "probs", q)))
                    else:
                        V.eng.wait_ge(vector_done, V.n)
                        V.eng.tensor_scalar(PB[q % NB][:, 0:j["n"]], PB[q % NB][:, 0:j["n"]], r, j["factor"], ALU.mult, ALU.mult).then_inc(vector_done, V.one(("V", ph, "probs", q)))

        def att_A(A, ph, jobs):
            n = len(jobs)
            for s in range(n + 3):
                if s < n:
                    j = jobs[s]
                    A.eng.wait_ge(vector_done, done("V", ph, "max", s))
                    if s >= NB:
                        A.eng.wait_ge(vector_done, done("V", ph, "probs", s - NB))
                    src = PB[s % NB] if j["mask"] is not None else psum[s % 3]
                    mn = mxs[:, s % NB:s % NB + 1]
                    A.eng.wait_ge(scalar_done, A.n)
                    A.eng.activation(PB[s % NB][:, 0:j["n"]], src[:, 0:j["n"]], ACT.Exp, bias=mn, scale=-1.0,
                                            accum_out=mxs[:, 3 + s % NB:4 + s % NB]).then_inc(scalar_done, A.one(("A", ph, "read", s)))
                    if j["sink"] is not None:
                        A.eng.wait_ge(scalar_done, A.n)
                        A.eng.activation(mxs[:, 6 + s % NB:7 + s % NB], j["sink"], ACT.Exp, bias=mn, scale=-1.0).then_inc(scalar_done, A.one())
                    A.note(("A", ph, "exp", s))
                if 0 <= s - 2 < n:
                    q = s - 2
                    A.eng.wait_ge(tensor_done, done("T", ph, "turn", q))
                    if q >= NB:
                        A.eng.wait_ge(tensor_done, done("T", ph, "out", q - NB))
                    m = jobs[q]["n"]
                    A.eng.wait_ge(scalar_done, A.n)
                    A.eng.activation(PTB[q % NB][:, 0:m], psum[3 + q % 2][:, 0:m], ACT.Copy).then_inc(scalar_done, A.one(("A", ph, "turned", q)))
                if 0 <= s - 3 < n and jobs[s - 3]["close"] is not None:
                    q = s - 3
                    src_cols, dst = jobs[q]["close"]
                    A.eng.wait_ge(tensor_done, done("T", ph, "out", q))
                    A.eng.wait_ge(scalar_done, A.n)
                    A.eng.activation(dst, psum[5 + jobs[q]["group"] % 2][:, src_cols], ACT.Copy).then_inc(scalar_done, A.one(("A", ph, "group", jobs[q]["group"])))

        def jobs_of_pairs(heads, tiles, tile0, scores, n, mask, sink_of, values, dst):
            jobs = []
            group = 0
            for pair in range(heads // 2):
                for ti, t in enumerate(tiles):
                    for par in range(2):
                        h = 2 * pair + par
                        lastj = ti == len(tiles) - 1 and par == 1
                        jobs.append(dict(
                            n=n(t), scores=scores(h, t), mask=mask(t), sink=sink_of(h), factor=None, v=values(h, t),
                            out=(None, slice(64 * par, 64 * par + 64), slice(ti * P, (ti + 1) * P), True, True, False),
                            open=(ti == 0 and par == 0), group=group,
                            close=(slice(0, len(tiles) * P), dst(pair)) if lastj else None))
                group += 1
            return jobs

        def up_bank(f, u, n):
            return psum[f % 4][:, u * n:(u + 1) * n] if n == SEQ else psum[2 * (f % 4) + u][:, 0:n]

        def up_T(T, ph, lo, n, ada):
            tile = 0
            for f in range(FC):
                w, slot = take(T)
                w = w.rearrange("p (u k c) -> p u k c", u=2, c=P)
                if f >= 4:
                    T.eng.wait_ge(vector_done, done("V", ph, "h", f - 4))
                for u in range(2):
                    for k in range(KT):
                        i = T.eng.matmul(up_bank(f, u, n), w[:, u, k, :], nT[:, k, lo:lo + n],
                                         start=(k == 0), stop=(k == KT - 1))
                i.then_inc(tensor_done, T.one(slot))
                T.note(("T", ph, "up", f))
                for _ in range(ADA_AFTER[f] if ada else 0):
                    ada_tile_T(T, ph, tile)
                    tile += 1

        cbuf = lambda f, i, n: qkt[:, ((f % 2) * 3 + i) * 512:((f % 2) * 3 + i) * 512 + n]
        hT = lambda f, n: big[:, f * n:(f + 1) * n]

        def up_A(A, ph, n, taps, both):
            mid, bias = taps
            for f in range(FC):
                A.eng.wait_ge(tensor_done, done("T", ph, "up", f))
                if f >= 2:
                    A.eng.wait_ge(vector_done, done("V", ph, "h", f - 2))
                for u in range(2 if both else 1):
                    A.eng.wait_ge(scalar_done, A.n)
                    A.eng.activation(cbuf(f, u, n), up_bank(f, u, n), ACT.Identity,
                                            scale=mid(u, f), bias=bias(u, f)).then_inc(scalar_done, A.one())
                A.note(("A", ph, "mid", f))
                A.eng.wait_ge(vector_done, done("V", ph, "conv", f))
                A.eng.wait_ge(scalar_done, A.n)
                A.eng.activation(cbuf(f, 2, n), cbuf(f, 0, n), ACT.Silu).then_inc(scalar_done, A.one(("A", ph, "silu", f)))

        def up_V_causal(V, ph, n, tap):
            for f in range(FC):
                g = up_bank(f, 0, n)
                c = cbuf(f, 0, n)
                V.eng.wait_ge(scalar_done, done("A", ph, "mid", f))
                for back in (1, 2):
                    V.eng.wait_ge(vector_done, V.n)
                    V.eng.scalar_tensor_tensor(out=c[:, back:n], in0=g[:, 0:n - back], scalar=tap(2 - back, f),
                                                      in1=c[:, back:n], op0=ALU.mult, op1=ALU.add).then_inc(vector_done, V.one())
                V.note(("V", ph, "conv", f))
                V.eng.wait_ge(scalar_done, done("A", ph, "silu", f))
                V.eng.wait_ge(vector_done, V.n)
                V.eng.tensor_tensor(hT(f, n), up_bank(f, 1, n), cbuf(f, 2, n), ALU.mult).then_inc(vector_done, V.one(("V", ph, "h", f)))

        def up_V_both(V, ph, n, tap):
            for f in range(FC):
                V.eng.wait_ge(scalar_done, done("A", ph, "mid", f))
                for u in range(2):
                    g = up_bank(f, u, n).rearrange("p (s t) -> p s t", t=SEQ)
                    c = cbuf(f, u, n).rearrange("p (s t) -> p s t", t=SEQ)
                    V.eng.wait_ge(vector_done, V.n)
                    V.eng.scalar_tensor_tensor(out=c[:, :, 1:], in0=g[:, :, 0:SEQ - 1], scalar=tap(u, 0, f),
                                                      in1=c[:, :, 1:], op0=ALU.mult, op1=ALU.add).then_inc(vector_done, V.one())
                    V.eng.wait_ge(vector_done, V.n)
                    V.eng.scalar_tensor_tensor(out=c[:, :, 0:SEQ - 1], in0=g[:, :, 1:], scalar=tap(u, 2, f),
                                                      in1=c[:, :, 0:SEQ - 1], op0=ALU.mult, op1=ALU.add).then_inc(vector_done, V.one())
                    if u == 0:
                        V.note(("V", ph, "conv", f))
                V.eng.wait_ge(scalar_done, done("A", ph, "silu", f))
                V.eng.wait_ge(vector_done, V.n)
                V.eng.tensor_tensor(hT(f, n), cbuf(f, 1, n), cbuf(f, 2, n), ALU.mult).then_inc(vector_done, V.one(("V", ph, "h", f)))

        def down_T(T, ph, tiles):
            n = len(tiles) * P
            if len(tiles) == 2:
                for f0 in range(0, FC, 2):
                    w, slot = take(T)
                    w = w.rearrange("p (c n) -> p c n", c=2)
                    for c in range(2):
                        f = f0 + c
                        for j in range(2):
                            for half in range(2):
                                i = T.eng.matmul(psum[4 * half + j][:, :], hT(f, n)[:, j * P:(j + 1) * P], w[:, c, half * 512:half * 512 + 512],
                                                 start=(f == 0), stop=(f == FC - 1))
                    i.then_inc(tensor_done, T.one(slot))
                T.note(("T", ph, "out", 0))
                T.note(("T", ph, "out", 1))
            else:
                for half in range(2):
                    for f0 in range(0, FC, 4):
                        w, slot = take(T)
                        w = w.rearrange("p (c n) -> p c n", c=4)
                        for c in range(min(4, FC - f0)):
                            f = f0 + c
                            for j in range(4):
                                i = T.eng.matmul(psum[4 * half + j][:, :], hT(f, n)[:, j * P:(j + 1) * P], w[:, c, :],
                                                 start=(f == 0), stop=(f == FC - 1))
                        i.then_inc(tensor_done, T.one(slot))
                    T.note(("T", ph, "out", half))

        silu_c = st2[:, 64:80]

        def ada_tile_T(T, ph, tile):
            g, k = tile // KT, tile % KT
            w, slot = take(T)
            for j in range(4):
                i = T.eng.matmul(psum[4 + g][32 * j:32 * j + 2, :], silu_c[:, 2 * k:2 * k + 2],
                                 w[:, j * 512:(j + 1) * 512], start=(k == 0), stop=(k == KT - 1))
            i.then_inc(tensor_done, T.one(slot))
            if k == KT - 1:
                T.note(("T", ph, "rows", g))

        def ada_rows_V(V, ph, layer):
            V.eng.wait_ge(adab_in, 16 * 8 * 2)
            for g in range(3):
                V.eng.wait_ge(tensor_done, done("T", ph, "rows", g))
                for j in range(4):
                    r = slice(32 * j, 32 * j + 2)
                    m = mod[r, (layer * 3 + g) * 512:(layer * 3 + g + 1) * 512]
                    V.eng.wait_ge(vector_done, V.n)
                    V.eng.tensor_tensor(m, psum[4 + g][r, :], m, ALU.add).then_inc(vector_done, V.one())
            V.note(("V", ph, "rows"))

        def ada_cols_T(T, ph, layer):
            n = 0
            for w, idx in enumerate((0, 1, 3, 4)):
                for k in range(KT):
                    g, j = idx // 2, (idx % 2) * 2 + k // 4
                    r = slice(32 * j, 32 * j + 2)
                    at = (layer * 3 + g) * 512 + (k % 4) * P
                    i = T.eng.matmul(psum[(2, 3, 6, 7)[j]][:, 2 * n:2 * n + 2], mod[r, at:at + P],
                                     const("ident", 32 * j, 32 * j + 2, r), start=True, stop=True, tile_position=(32 * j, 0))
                    n += 1
            i.then_inc(tensor_done, T.one(("T", ph, "cols")))

        def ada_cols_V(V, ph, layer):
            V.eng.wait_ge(tensor_done, done("T", ph, "cols"))
            for w, idx in enumerate((0, 1, 3, 4)):
                for half in range(2):
                    a = w * 16 + half * 8
                    V.eng.wait_ge(vector_done, V.n)
                    V.eng.tensor_copy(modcol[:, layer * 64 + a:layer * 64 + a + 8],
                                      psum[(2, 3, 6, 7)[(idx % 2) * 2 + half]][:, a:a + 8]).then_inc(vector_done, V.one())
            for m, w in enumerate((1, 3)):
                g3 = veccol[:, 32 + layer * 16 + m * 8:32 + layer * 16 + m * 8 + 8].rearrange("p (k o) -> p k o", o=1).to_broadcast([P, KT, 2])
                V.eng.wait_ge(vector_done, V.n)
                V.eng.scalar_tensor_tensor(
                    out=acol[:, layer * 32 + m * 16:layer * 32 + (m + 1) * 16].rearrange("p (k s) -> p k s", s=2),
                    in0=modcol[:, layer * 64 + w * 16:layer * 64 + (w + 1) * 16].rearrange("p (k s) -> p k s", s=2),
                    scalar=1.0, in1=g3, op0=ALU.add, op1=ALU.mult).then_inc(vector_done, V.one())

        def gates_T(T, ph, idx, streams, layer):
            n = 0
            for s in streams:
                for half in range(2):
                    g, j = idx // 2, (idx % 2) * 2 + half
                    r = slice(32 * j, 32 * j + 2)
                    i = T.eng.matmul(psum[2 * s + half][:, :], const("pick2", s * P, (s + 1) * P, r), mod[r, (layer * 3 + g) * 512:(layer * 3 + g + 1) * 512],
                                     start=True, stop=True, tile_position=(32 * j, 0))
                    n += 1
            i.then_inc(tensor_done, T.one(("T", ph, "gates")))

        def gates_A(A, ph, streams):
            A.eng.wait_ge(tensor_done, done("T", ph, "gates"))
            for s in streams:
                for half in range(2):
                    A.eng.wait_ge(scalar_done, A.n)
                    A.eng.activation(gate[:, s * D + half * 512:s * D + half * 512 + 512], psum[2 * s + half][:, :], ACT.Copy).then_inc(scalar_done, A.one())

        S1 = 3080
        tok1 = lambda t: big[:, (t - 2) * S1:(t - 1) * S1]
        f256 = lambda i: qkt[:, i * SEQ:(i + 1) * SEQ]
        frow = gate[0:NH, :]

        def turns_l0():
            return [([big[:, j * S1 + kind * 512 + pr * P:j * S1 + kind * 512 + (pr + 1) * P] for pr in (p2, p2 + 1) for j in range(2)],
                     qkt[:, (base + p2) * SEQ:(base + p2 + 2) * SEQ], scale)
                    for base, kind, scale in ((0, 0, -0.125), (4, 1, 1.0), (8, 3, -0.125), (12, 4, 1.0)) for p2 in (0, 2)]

        def jobs_l0(which):
            base = 0 if which == "dilated" else 8
            vcol = 1024 if which == "dilated" else 2560
            def scores(h, t):
                r = slice(64 * (h % 2), 64 * (h % 2) + 64)
                n = (t + 1) * P
                terms = [(f256(base + h // 2)[r, t * P:(t + 1) * P], f256(base + 4 + h // 2)[r, 0:n])]
                if which == "forget":
                    terms.append((const("pick8", h * P, (h + 1) * P, slice(0, NH)), frow[:, 512:512 + n]))
                return [(0, n, terms)]
            mask = (lambda t: const("dilated", t * SEQ, t * SEQ + (t + 1) * P)) if which == "dilated" else \
                   (lambda t: const("causal", P - t * P, 2 * P))
            vals = lambda h, t: [big[:, c * S1 + vcol + h * DH:c * S1 + vcol + (h + 1) * DH] for c in range(t + 1)]
            off = 0 if which == "dilated" else 4
            return jobs_of_pairs(NH, (0, 1), 0, scores, lambda t: (t + 1) * P, mask, lambda h: None, vals,
                                 lambda pair: nT[:, off + pair, SEQ:2 * SEQ])

        S2 = 3072
        def turns_l1():
            return [([big[:, j * S2 + kind * 1024 + pr * P:j * S2 + kind * 1024 + (pr + 1) * P] for pr in (p2, p2 + 1) for j in range(2)],
                     qkt[:, (kind * 8 + p2) * SEQ:(kind * 8 + p2 + 2) * SEQ], scale)
                    for kind, scale in ((0, -0.125), (1, 1.0)) for p2 in (0, 2, 4, 6)]

        def jobs_l1():
            jobs = []
            group = 0
            for t in range(2):
                for h0 in range(0, NH, 4):
                    for h in range(h0, h0 + 4):
                        for m in range(2):
                            r = slice(64 * m, 64 * m + 64)
                            n = (t + 1) * P
                            jobs.append(dict(
                                n=n, scores=[(0, n, [(f256(h)[r, t * P:(t + 1) * P], f256(8 + h)[r, 0:n])])],
                                mask=const("causal", P - t * P, 2 * P), sink=None, factor=(lam[:, 4:5] if m else None),
                                v=[big[:, c * S2 + 2048 + h * P:c * S2 + 2048 + (h + 1) * P] for c in range(t + 1)],
                                out=(None, slice(0, P), slice((h - h0) * P, (h - h0 + 1) * P), m == 0, m == 1, True),
                                open=(h == h0 and m == 0), group=group,
                                close=(slice(0, 512), big[:, t * S2 + h0 * P:t * S2 + (h0 + 4) * P]) if (h == h0 + 3 and m) else None))
                    group += 1
            return jobs

        S3 = 2832 + MH

        def row3(t, a, b):
            o = t * S3 + (MH if a >= 1536 else 0)
            return big[:, o + a:o + b]

        vals3 = lambda t: big[:, t * S3 + 1024:t * S3 + 1536 + MH].rearrange("p (h e) -> p h e", e=MD + 1)
        f512 = lambda i: qkt[:, i * 512:(i + 1) * 512]
        kdup = lambda t: final_g[:, t * 256:(t + 1) * 256]

        def turns_e(part):
            g = []
            if part == 0:
                for h in range(MH):
                    g.append(([row3(t, h * P, (h + 1) * P) for t in ALL], f512(h), 1.0))
                    g.append(([row3(t, 512 + h * P, 512 + (h + 1) * P) for t in ALL], f512(4 + h), MD ** -0.5))
            else:
                for pr in range(4):
                    g.append(([row3(t, 2064 + pr * P, 2064 + (pr + 1) * P) for t in ALL], f512(8 + pr), -0.125))
                for kv in range(2):
                    g.append(([kdup(t)[:, kv * P:(kv + 1) * P] for t in ALL], f512(12 + kv), 1.0))
            return g

        def jobs_e(stream):
            def scores(h, t):
                r = slice(64 * (h % 2), 64 * (h % 2) + 64)
                return [(0, 512 if stream else 256, [(f512(8 + h // 2)[r, t * P:(t + 1) * P], f512(12 + h // 4)[r, 0:(512 if stream else 256)])])]
            n = 512 if stream else 256
            vals = lambda h, t: [row3(c, 2704 + (h // 4) * DH, 2704 + (h // 4 + 1) * DH) for c in range(n // P)]
            mask = (lambda t: const("window", (t - 2) * 512, (t - 1) * 512)) if stream else (lambda t: None)
            return jobs_of_pairs(NH, LAT if stream else CTX, 0, scores, lambda t: n, mask, lambda h: nsink[:, h:h + 1], vals,
                                 lambda pair: nT[:, 4 + pair, stream * SEQ:(stream + 1) * SEQ])

        S4 = 2304
        row4 = lambda t, a, b: big[:, t * S4 + a:t * S4 + b]
        OQ, OK_, NQ, NK = 0, 1024, 2048, 3072

        def turns_o():
            g = [([kdup(t)[:, kv * P:(kv + 1) * P] for t in ALL], qkt[:, OK_ + kv * 512:OK_ + (kv + 1) * 512], 1.0) for kv in range(2)]
            for at, col in ((OQ, 0), (NQ, 768)):
                for p2 in (0, 2):
                    g.append(([row4(t, col + pr * P, col + (pr + 1) * P) for pr in (p2, p2 + 1) for t in LAT],
                              qkt[:, at + p2 * SEQ:at + (p2 + 2) * SEQ], -0.125))
            for pr in range(4):
                g.append(([row4(t, 1280 + pr * P, 1280 + (pr + 1) * P) for t in ALL], qkt[:, NK + pr * 512:NK + (pr + 1) * 512], 1.0))
            return g

        def nbias(h, t):
            o = (h % 4) * 512 + t * SEQ
            return qkt[:, 5120 + o:5120 + o + SEQ] if h < 4 else big[:, 4 * S4 + o:4 * S4 + o + SEQ]

        def jobs_o(which):
            def scores(h, t):
                r = slice(64 * (h % 2), 64 * (h % 2) + 64)
                if which == "global":
                    q = qkt[r, OQ + (h // 2) * SEQ + (t - 2) * P:OQ + (h // 2) * SEQ + (t - 1) * P]
                    return [(0, 512, [(q, qkt[r, OK_ + (h // 4) * 512:OK_ + (h // 4 + 1) * 512])])]
                q = qkt[r, NQ + (h // 2) * SEQ + (t - 2) * P:NQ + (h // 2) * SEQ + (t - 1) * P]
                k = NK + (h // 2) * 512
                return [(0, SEQ, [(q, qkt[r, k:k + SEQ])]),
                        (SEQ, 512, [(q, qkt[r, k + SEQ:k + 512]), (const("negflip"), nbias(h, t - 2))])]
            if which == "global":
                vals = lambda h, t: [row4(c, 640 + (h // 4) * DH, 640 + (h // 4 + 1) * DH) for c in ALL]
                mask = lambda t: None
            else:
                vals = lambda h, t: [row4(c, 1792 + h * DH, 1792 + (h + 1) * DH) for c in ALL]
                mask = lambda t: const("nbhood")
            off = 0 if which == "global" else 4
            return jobs_of_pairs(NH, LAT, 0, scores, lambda t: 512, mask, lambda h: None, vals,
                                 lambda pair: nT[:, off + pair, SEQ:2 * SEQ])

        mrow = lambda d, i: (gate[0:MH, i * 512:(i + 1) * 512] if d == 0 else work[0:MH, 2560 + i * 512:3072 + i * 512])
        negM = lambda d: nt[0:MH, d * 512:(d + 1) * 512]
        PT = lambda d, s: work[:, d * 2048 + s * 512:d * 2048 + (s + 1) * 512]
        WT = lambda i: gate[:, (i % 4) * 512:(i % 4 + 1) * 512]
        REACH = [{s: [t for t in range(4) if t >= s] for s in range(4)}, {0: [0, 2, 3], 1: [0, 1, 2, 3], 2: [2], 3: [2, 3]}]

        def runs(tiles):
            out_, a = [], tiles[0]
            for x, y in zip(tiles, tiles[1:] + [99]):
                if y != x + 1:
                    out_.append((a * P, (x + 1) * P))
                    a = y
            return out_

        def mgate_rows_T(T, ph):
            for q in (2, 3):
                e = "VA"[q % 2]
                T.eng.wait_ge(SEM[e], done(e, "2.0 in", "piece", q))
            for g in range(4):
                for t in ALL:
                    i = T.eng.matmul(psum[7][32 * g:32 * g + MH, t * P:(t + 1) * P], row3(t, 2048 + 4 * g, 2052 + 4 * g), ident, start=True, stop=True)
            i.then_inc(tensor_done, T.one(("T", ph, "gates")))

        def mgate_cols_T(T, ph):
            T.eng.wait_ge(vector_done, done("V", ph, "rows"))
            n = 0
            for d in range(2):
                for what in range(2):
                    for t in ALL:
                        i = T.eng.matmul(psum[7][:, 4 * n:4 * n + 4], mrow(d, what)[:, t * P:(t + 1) * P],
                                         const("ident", 0, MH, slice(0, MH)), start=True, stop=True)
                        n += 1
            i.then_inc(tensor_done, T.one(("T", ph, "cols")))

        def log_sigmoid(V, A, ph, key, x, t1, t2):
            if V is not None:
                V.eng.wait_ge(vector_done, V.n)
                V.eng.scalar_tensor_tensor(out=t1, in0=x, scalar=-1.0, in1=x, op0=ALU.mult, op1=ALU.max).then_inc(vector_done, V.one(("V", ph, "abs", key)))
                V.eng.wait_ge(scalar_done, done("A", ph, "log", key))
                V.eng.wait_ge(vector_done, V.n)
                V.eng.scalar_tensor_tensor(out=x, in0=x, scalar=0.0, in1=t2, op0=ALU.min, op1=ALU.subtract).then_inc(vector_done, V.one())
            else:
                A.eng.wait_ge(vector_done, done("V", ph, "abs", key))
                A.eng.wait_ge(scalar_done, A.n)
                A.eng.activation(t1, t1, ACT.Exp, scale=-1.0).then_inc(scalar_done, A.one())
                A.eng.wait_ge(scalar_done, A.n)
                A.eng.activation(t2, t1, ACT.Ln, bias=1.0).then_inc(scalar_done, A.one(("A", ph, "log", key)))

        def mgate_V(V, ph):
            V.eng.wait_ge(tensor_done, done("T", ph, "gates"))
            for g in range(4):
                V.eng.wait_ge(vector_done, V.n)
                V.eng.tensor_scalar(mrow(g // 2, g % 2), psum[7][32 * g:32 * g + MH, :], gbias[0:MH, g:g + 1], None, ALU.add).then_inc(vector_done, V.one())
            for d in range(2):
                a, f, B, M = (mrow(d, i) for i in range(4))
                log_sigmoid(V, None, ph, d, f, B, M)
                zero = work[0:MH, 2048:2560]
                if d == 0:
                    V.eng.wait_ge(vector_done, V.n)
                    V.eng.memset(zero, 0.0).then_inc(vector_done, V.one())
                    V.eng.wait_ge(vector_done, V.n)
                    V.eng.tensor_tensor_scan(B, f, zero, 0.0, ALU.add, ALU.add).then_inc(vector_done, V.one())
                    V.eng.wait_ge(vector_done, V.n)
                    V.eng.tensor_tensor(a, a, B, ALU.subtract).then_inc(vector_done, V.one())
                    V.eng.wait_ge(vector_done, V.n)
                    V.eng.tensor_tensor_scan(M, a, a, 0.0, ALU.max, ALU.max).then_inc(vector_done, V.one())
                else:
                    c, l = (lambda x: x[:, 0:SEQ][:, ::-1]), (lambda x: x[:, SEQ:512][:, ::-1])
                    V.eng.wait_ge(vector_done, V.n)
                    V.eng.tensor_tensor_scan(c(B), c(f), c(zero), 0.0, ALU.add, ALU.add).then_inc(vector_done, V.one())
                    V.eng.wait_ge(vector_done, V.n)
                    V.eng.tensor_tensor_scan(l(B), l(f), l(zero), B[:, 0:1], ALU.add, ALU.add).then_inc(vector_done, V.one())
                    V.eng.wait_ge(vector_done, V.n)
                    V.eng.tensor_tensor(a, a, B, ALU.subtract).then_inc(vector_done, V.one())
                    V.eng.wait_ge(vector_done, V.n)
                    V.eng.tensor_tensor_scan(c(M), c(a), c(a), 0.0, ALU.max, ALU.max).then_inc(vector_done, V.one())
                    V.eng.wait_ge(vector_done, V.n)
                    V.eng.tensor_tensor_scan(l(M), l(a), l(a), M[:, 0:1], ALU.max, ALU.max).then_inc(vector_done, V.one())
                V.eng.wait_ge(vector_done, V.n)
                V.eng.tensor_tensor(f, B, M, ALU.add).then_inc(vector_done, V.one())
            V.note(("V", ph, "rows"))

        def mgate_cols_V(V, ph):
            V.eng.wait_ge(tensor_done, done("T", ph, "cols"))
            V.eng.wait_ge(vector_done, V.n)
            V.eng.tensor_copy(mcol[:, :], psum[7][:, 0:64]).then_inc(vector_done, V.one(("V", ph, "cols")))

        def mgate_A(A, ph):
            for d in range(2):
                log_sigmoid(None, A, ph, d, None, mrow(d, 2), mrow(d, 3))

        def mgate_cols_A(A, ph):
            A.eng.wait_ge(vector_done, done("V", ph, "cols"))
            for d in range(2):
                c = mcol[:, d * 32 + 16:d * 32 + 32]
                A.eng.wait_ge(scalar_done, A.n)
                A.eng.activation(c, c, ACT.Exp, scale=-1.0).then_inc(scalar_done, A.one())

        MASKED = lambda d: work[:, 4096 + d * 512:4608 + d * 512] if d == 0 else final_g[:, 0:512]
        W = MD + 1
        PIECES = [(s, d) for s in range(4) for d in range(2)]

        def mlstm_T(T, ph):
            def spread(h):
                for d in range(2):
                    if h >= 1:
                        T.eng.wait_ge(scalar_done, done("A", ph, "w", 8 * h - 1))
                        T.eng.wait_ge(vector_done, done("V", ph, "masked", 2 * (h - 1) + d))
                    i = T.eng.matmul(psum[2 + d][:, :], const("pick8", h * P, (h + 1) * P, slice(0, MH)), negM(d), start=True, stop=True)
                    i.then_inc(tensor_done, T.one(("T", ph, "spread", 2 * h + d)))

            T.eng.wait_ge(vector_done, done("V", ph, "-M"))
            spread(0)
            for h in range(MH):
                for s in range(4):
                    n = 4 * h + s
                    if n >= 2:
                        T.eng.wait_ge(vector_done, done("V", ph, "pt", n - 2))
                    i = T.eng.matmul(psum[s % 2][:, :], f512(4 + h)[:, s * P:(s + 1) * P], f512(h), start=True, stop=True)
                    i.then_inc(tensor_done, T.one(("T", ph, "qk", n)))
                if h + 1 < MH:
                    spread(h + 1)
                for d in range(2):
                    g = 2 * h + d
                    T.eng.wait_ge(vector_done, done("V", ph, "pt", 4 * h + 3))
                    if g >= 2:
                        T.eng.wait_ge(vector_done, done("V", ph, "h", g - 2))
                    for t in range(4):
                        srcs = [s for s in range(4) if t in REACH[d][s]]
                        for m, s in enumerate(srcs):
                            i = T.eng.matmul(psum[4 + 2 * (g % 2) + t // 2][:, (t % 2) * W:(t % 2 + 1) * W], PT(d, s)[:, t * P:(t + 1) * P],
                                             vals3(s)[:, h, :], start=(m == 0), stop=(m == len(srcs) - 1))
                    i.then_inc(tensor_done, T.one(("T", ph, "sum", g)))

        def mlstm_A(A, ph):
            for h in range(MH):
                for w8, (s, d) in enumerate(PIECES):
                    w = 8 * h + w8
                    if s == 0:
                        A.eng.wait_ge(tensor_done, done("T", ph, "spread", 2 * h + d))
                        A.eng.wait_ge(vector_done, done("V", ph, "masked", 2 * h + d))
                    if w == 0:
                        A.eng.wait_ge(vector_done, done("V", ph, "-M"))
                    if w >= 4:
                        A.eng.wait_ge(vector_done, done("V", ph, "pt", (w - 4) // 2))
                    col = mcol[:, d * 32 + s * 4 + h:d * 32 + s * 4 + h + 1]
                    A.eng.wait_ge(scalar_done, A.n)
                    A.eng.activation(WT(w)[:, s * P:(s + 1) * P], MASKED(d)[:, s * P:(s + 1) * P], ACT.Exp, bias=col).then_inc(scalar_done, A.one())
                    rest = [t for t in REACH[d][s] if t != s]
                    for a, b in (runs(rest) if rest else []):
                        A.eng.wait_ge(scalar_done, A.n)
                        A.eng.activation(WT(w)[:, a:b], psum[2 + d][:, a:b], ACT.Exp, bias=col).then_inc(scalar_done, A.one())
                    A.note(("A", ph, "w", w))

        def mlstm_V(V, ph):
            def mask(h):
                for d in range(2):
                    V.eng.wait_ge(tensor_done, done("T", ph, "spread", 2 * h + d))
                    if h >= 1:
                        V.eng.wait_ge(scalar_done, done("A", ph, "w", 8 * h - 1))
                    m = const("later" if d == 0 else "earlier").rearrange("p (o n) -> p o n", o=1).to_broadcast([P, 4, P])
                    V.eng.wait_ge(vector_done, V.n)
                    V.eng.tensor_tensor(MASKED(d).rearrange("p (t n) -> p t n", n=P), psum[2 + d][:, :].rearrange("p (t n) -> p t n", n=P),
                                        m, ALU.add).then_inc(vector_done, V.one(("V", ph, "masked", 2 * h + d)))

            def finish(g):
                h, d = g // 2, g % 2
                V.eng.wait_ge(tensor_done, done("T", ph, "sum", g))
                banks = [psum[4 + 2 * (g % 2) + i][:, 0:2 * W].rearrange("p (t e) -> p t e", e=W) for i in range(2)]
                r = st2[:, 0:4]
                for i in range(2):
                    V.eng.wait_ge(vector_done, V.n)
                    V.eng.tensor_copy(st2[:, 4 + 2 * i:6 + 2 * i], banks[i][:, :, MD]).then_inc(vector_done, V.one())
                V.eng.wait_ge(vector_done, V.n)
                V.eng.scalar_tensor_tensor(out=r, in0=st2[:, 4:8], scalar=-1.0, in1=st2[:, 4:8], op0=ALU.mult, op1=ALU.max).then_inc(vector_done, V.one())
                e = mcol[:, d * 32 + 16:d * 32 + 32].rearrange("p (t h) -> p t h", h=MH)[:, :, h]
                V.eng.wait_ge(vector_done, V.n)
                V.eng.tensor_tensor(r, r, e, ALU.max).then_inc(vector_done, V.one())
                V.eng.wait_ge(vector_done, V.n)
                V.eng.reciprocal(r, r).then_inc(vector_done, V.one())
                hh = big[:, :].rearrange("p (t e) -> p t e", e=S3)[:, :, h * P:(h + 1) * P]
                rb = r.rearrange("p (t o) -> p t o", o=1).to_broadcast([P, 4, P])
                to = hh if d == 0 else final_g[:, 512:1024].rearrange("p (t e) -> p t e", e=P)
                for i in range(2):
                    V.eng.wait_ge(vector_done, V.n)
                    V.eng.tensor_tensor(to[:, 2 * i:2 * i + 2, :], banks[i][:, :, 0:MD], rb[:, 2 * i:2 * i + 2, :], ALU.mult).then_inc(vector_done, V.one())
                V.note(("V", ph, "h", g))
                if d == 1:
                    V.eng.wait_ge(vector_done, V.n)
                    V.eng.tensor_tensor(hh, hh, to, ALU.add).then_inc(vector_done, V.one())

            for d in range(2):
                V.eng.wait_ge(vector_done, V.n)
                V.eng.tensor_scalar(negM(d), mrow(d, 3), -1.0, None, ALU.mult).then_inc(vector_done, V.one(("V", ph, "-M")))
            mask(0)
            for h in range(MH):
                for s in range(4):
                    n = 4 * h + s
                    V.eng.wait_ge(tensor_done, done("T", ph, "qk", n))
                    if h >= 1 and s == 0:
                        V.eng.wait_ge(tensor_done, done("T", ph, "sum", 2 * h - 1))
                    for d in range(2):
                        V.eng.wait_ge(scalar_done, done("A", ph, "w", 8 * h + 2 * s + d))
                        for a, b in runs(REACH[d][s]):
                            V.eng.wait_ge(vector_done, V.n)
                            V.eng.tensor_tensor(PT(d, s)[:, a:b], psum[s % 2][:, a:b], WT(2 * s + d)[:, a:b], ALU.mult).then_inc(vector_done, V.one())
                    V.note(("V", ph, "pt", n))
                if h + 1 < MH:
                    mask(h + 1)
                for d in range(2):
                    finish(2 * h + d)

        def mout_A(A, ph):
            heads_rms_A(A, ph, TT * MH)

        def mout_V(V, ph):
            heads_rms_V(V, ph, [(row3(t, 0, 512), MH) for t in ALL], MD, EPS)
            for t in ALL:
                h = row3(t, 0, 512)
                V.eng.wait_ge(vector_done, V.n)
                V.eng.tensor_tensor(hv(h, MD), hv(h, MD), over(rms[:, t * MH:(t + 1) * MH], MH, MD), ALU.mult).then_inc(vector_done, V.one())
                V.eng.wait_ge(vector_done, V.n)
                V.eng.tensor_tensor(h, h, head_g[:, :], ALU.mult).then_inc(vector_done, V.one())
                V.eng.wait_ge(vector_done, V.n)
                V.eng.tensor_tensor(h, h, row3(t, 1536, 2048), ALU.mult).then_inc(vector_done, V.one())

        def turns_mout():
            return [([row3(t, h * P, (h + 1) * P) for t in ALL], nT[:, h, :], 1.0) for h in range(MH)]

        def turns_sub():
            return [([big[:, j * S2 + h * P:j * S2 + (h + 1) * P] for j in range(2)], nT[:, h, SEQ:512], 1.0) for h in range(NH)]

        none = lambda g: []

        def lay(kind, layer, k):
            base = {"attn": 0, "ffn": 16}[kind] + layer * 8 + k
            return veccol[:, base:base + 1]

        def tap1(layer):
            c = lambda j, f: convcol[:, layer * 88 + j * 22 + f:layer * 88 + j * 22 + f + 1]
            return c

        def tap2(layer):
            def c(u, j, f):
                o = (2 + 2 * layer) * 88 + 44 * j + 22 * u + f
                return convcol[:, o:o + 1]
            return c

        phases = []

        def phase(name, T=None, V=None, A=None, G=None):
            phases.append((name, {"T": T, "V": V, "A": A, "G": G}))

        vrows, crow = work[0:80, 0:P], [work[0:88, P * (1 + i):P * (2 + i)] for i in range(6)]

        def setup_T(T):
            T.eng.wait_ge(loaded, 16 * N_LOADS)
            T.eng.transpose(psum[0][:, 0:80], vrows, const("ident", 0, 80, slice(0, 80)))
            for i in range(4):
                T.eng.transpose(psum[1][:, i * 88:(i + 1) * 88], crow[i], const("ident", 0, 88, slice(0, 88)))
            for i in range(4, 6):
                m = T.eng.transpose(psum[2][:, (i - 4) * 88:(i - 3) * 88], crow[i], const("ident", 0, 88, slice(0, 88)))
            m.then_inc(tensor_done, T.one(("T", "setup", "cols")))

        def setup_V(V):
            V.eng.wait_ge(loaded, 16 * N_LOADS)
            V.eng.wait_ge(vector_done, V.n)
            V.eng.memset(lam[:, 6:8], 0.0).then_inc(vector_done, V.one())
            V.eng.wait_ge(tensor_done, done("T", "setup", "cols"))
            V.eng.wait_ge(vector_done, V.n)
            V.eng.tensor_copy(veccol[:, :], psum[0][:, 0:80]).then_inc(vector_done, V.one(("V", "setup", "vec")))
            V.eng.wait_ge(vector_done, V.n)
            V.eng.tensor_copy(convcol[:, 0:352], psum[1][:, 0:352]).then_inc(vector_done, V.one())
            V.eng.wait_ge(vector_done, V.n)
            V.eng.tensor_copy(convcol[:, 352:528], psum[2][:, 0:176]).then_inc(vector_done, V.one())
            V.eng.wait_ge(vector_done, V.n)
            V.eng.tensor_scalar(nsink[:, :], sink[:, :], -1.0, None, ALU.mult).then_inc(vector_done, V.one())
            V.eng.wait_ge(vector_done, V.n)
            V.eng.tensor_scalar(sub_g[:, :], sub_g[:, :], 1.0 - LAM_INIT, None, ALU.mult).then_inc(vector_done, V.one())
            l4 = lam_in[:, :].rearrange("p (a b e) -> p a b e", a=2, b=2)
            pr = work[:, 2048:2176].rearrange("p (a e) -> p a e", a=2)
            V.eng.wait_ge(vector_done, V.n)
            V.eng.tensor_tensor(pr, l4[:, :, 0, :], l4[:, :, 1, :], ALU.mult).then_inc(vector_done, V.one())
            V.eng.wait_ge(vector_done, V.n)
            V.eng.tensor_reduce(lam[:, 0:2], pr, AX_X, ALU.add).then_inc(vector_done, V.one(("V", "setup", "dots")))
            V.eng.wait_ge(scalar_done, done("A", "setup", "exps"))
            V.eng.wait_ge(vector_done, V.n)
            V.eng.tensor_tensor(lam[:, 5:6], lam[:, 3:4], lam[:, 2:3], ALU.subtract).then_inc(vector_done, V.one())
            V.eng.wait_ge(vector_done, V.n)
            V.eng.tensor_scalar(lam[:, 4:5], lam[:, 5:6], LAM_INIT, None, ALU.subtract).then_inc(vector_done, V.one())

        def setup_A(A):
            A.eng.wait_ge(vector_done, done("V", "setup", "dots"))
            A.eng.wait_ge(scalar_done, A.n)
            A.eng.activation(lam[:, 2:4], lam[:, 0:2], ACT.Exp).then_inc(scalar_done, A.one(("A", "setup", "exps")))
            A.eng.wait_ge(scalar_done, A.n)
            A.eng.activation(silu_c.rearrange("p (k s) -> p s k", s=2),
                                    veccol[:, 64:80].rearrange("p (s k) -> p s k", s=2), ACT.Silu).then_inc(scalar_done, A.one())

        def ada_bias_load(G):
            for layer in range(2):
                for j in range(4):
                    for s in range(2):
                        src = io["ada_b_2"][layer:layer + 1, :].rearrange("o (g j n) -> o g j n", g=3, j=4)[:, :, j, :]
                        dst = mod[32 * j + s:32 * j + s + 1, layer * 1536:(layer + 1) * 1536]
                        G.eng.dma_start(dst.rearrange("p (g n) -> p g n", g=3), src).then_inc(adab_in, 16)

        phase("setup", setup_T, setup_V, setup_A, ada_bias_load)

        def norm_phase(ph, tiles, which):
            phase(ph, lambda T: norm_T(T, ph, tiles),
                  lambda V: (norm_V(V, ph, tiles), norm_evac(V, ph, tiles, which, 0)),
                  lambda A: (norm_A(A, ph, tiles), norm_evac(A, ph, tiles, which, 1)))

        def proj_phase(ph, cuts, tiles_of, dst, reader=lambda c, j: "VA"[j % 2], between={}, after_V={}, after_A={}, G=None):
            pieces = pieces_of(cuts, tiles_of, reader)
            banks = 7 if len(tiles_of(len(cuts) - 1)) == 4 else 6
            phase(ph, lambda T: proj_T(T, ph, cuts, pieces, banks, between),
                  lambda V: proj_read(V, ph, cuts, pieces, banks, dst, after_V),
                  lambda A: proj_read(A, ph, cuts, pieces, banks, dst, after_A), G)

        def out_phase(ph, tiles, gate_idx, layer=0):
            streams = sorted({t // 2 for t in tiles})
            if gate_idx is not None:
                phase(ph + " gates", lambda T: gates_T(T, ph, gate_idx, streams, layer), None, lambda A: gates_A(A, ph, streams))
            pieces = pieces_of(OUT_CUTS, lambda c: tiles, lambda c, j: "V")
            parts = [(("T", ph, "piece", p["n"]), p["n"], p["t"], p["a"], p["b"]) for p in pieces]
            phase(ph, lambda T: proj_T(T, ph, OUT_CUTS, pieces, 8, {}), lambda V: residual_V(V, ph, parts, gate_idx is not None))

        def down_parts(ph, tiles):
            return [(("T", ph, "out", half), 4 * half + j, t, 512 * half, 512 * half + 512) for half in range(2) for j, t in enumerate(tiles)]

        def ffn_phases(ph, tiles, layer, block, gate_idx):
            n = len(tiles) * P
            lo = 512 - n
            up, down = ph + " up", ph + " down"
            if block == 1:
                tap = tap1(layer)
                phase(up, lambda T: up_T(T, up, lo, n, True),
                      lambda V: (up_V_causal(V, up, n, tap), ada_rows_V(V, up, layer)),
                      lambda A: up_A(A, up, n, (lambda u, f: tap(2, f), lambda u, f: tap(3, f)), False))
                phase(down, lambda T: (down_T(T, down, tiles), ada_cols_T(T, down, layer)),
                      lambda V: (residual_V(V, down, down_parts(down, tiles), False), ada_cols_V(V, down, layer)))
                return
            tap = tap2(layer)
            phase(up, lambda T: up_T(T, up, lo, n, False), lambda V: up_V_both(V, up, n, tap),
                  lambda A: up_A(A, up, n, (lambda u, f: tap(u, 1, f), lambda u, f: tap(u, 3, f)), True))
            streams = sorted({t // 2 for t in tiles})
            phase(ph + " gates", lambda T: gates_T(T, ph, gate_idx, streams, layer), None, lambda A: gates_A(A, ph, streams))
            phase(down, lambda T: down_T(T, down, tiles),
                  lambda V: residual_V(V, down, down_parts(down, tiles), True))

        def turn_phase(ph, groups):
            all_ = range(len(groups))
            phase(ph, lambda T: turns_T(T, ph, groups), lambda V: turns_evac(V, ph, groups, all_), lambda A: turns_evac(A, ph, groups, all_))

        def plain(base, stride):
            return lambda c, t, a, b: (big[:, (t - base) * stride + a:(t - base) * stride + b], lambda s: s, ACT.Copy)

        def att_phase(ph, jobs):
            phase(ph, lambda T: att_T(T, ph, jobs), lambda V: att_V(V, ph, jobs), lambda A: att_A(A, ph, jobs))

        norm_phase("1.0 norm", LAT, lambda k, s: (lay("attn", 0, k), None))
        l0_turns = turns_l0()

        def rope_1(V, stride, col):
            for j in range(2):
                cs, sn = const("cos1", j * DH, (j + 1) * DH), const("sin1", j * DH, (j + 1) * DH)
                rope_V(V, big[:, j * stride + col:j * stride + col + 512], 8, cs, sn, False)
            V.note(("V", "rope", stride, col))

        def fox_T(T):
            for j in range(2):
                e = "VA"[j]
                T.eng.wait_ge(SEM[e], done(e, "1.0 in", "piece", j))
                i = T.eng.matmul(psum[7][0:NH, j * P:(j + 1) * P], big[:, j * S1 + 3072:j * S1 + 3080], ident, start=True, stop=True)
            i.then_inc(tensor_done, T.one(("T", "fox", "rows")))

        def fox_V(V):
            f, t1, c, t2 = (frow[:, i * SEQ:(i + 1) * SEQ] for i in range(4))
            V.eng.wait_ge(tensor_done, done("T", "fox", "rows"))
            V.eng.wait_ge(vector_done, V.n)
            V.eng.tensor_scalar(f, psum[7][0:NH, 0:SEQ], fbias[0:NH, 0:1], None, ALU.add).then_inc(vector_done, V.one(("V", "fox", "rows")))
            log_sigmoid(V, None, "fox", 0, f, t1, t2)
            V.eng.wait_ge(vector_done, V.n)
            V.eng.memset(t1, 0.0).then_inc(vector_done, V.one())
            V.eng.wait_ge(vector_done, V.n)
            V.eng.tensor_tensor_scan(c, f, t1, 0.0, ALU.add, ALU.add).then_inc(vector_done, V.one())

        def fox_A(A):
            log_sigmoid(None, A, "fox", 0, None, frow[:, SEQ:2 * SEQ], frow[:, 3 * SEQ:4 * SEQ])
        def turn_step(ph, groups, g, banks, *needs):
            return lambda T: turn_T(T, ph, groups, g, banks, needs)

        def evac_step(ph, groups, which, banks):
            return lambda E: turns_evac(E, ph, groups, which, banks)

        SIDE = (6, 7)
        both_read = lambda ph, n: [("V", ("V", ph, "piece", n)), ("A", ("A", ph, "piece", n + 1))]
        l0 = lambda g, *needs: turn_step("1.0 turn", l0_turns, g, SIDE, *needs)
        l0_evac = lambda *which: evac_step("1.0 turn", l0_turns, which, SIDE)
        proj_phase("1.0 in", HYB_CUTS, lambda c: LAT, plain(2, S1),
                   between={(1, 0, 1): [fox_T],
                            (3, 0, 1): [l0(0, ("V", ("V", "rope", S1, 0)), ("V", ("V", "fox", "rows")))], (3, 1, 0): [l0(1)],
                            (4, 0, 1): [l0(2, ("V", ("V", "rope", S1, 512)))], (4, 1, 0): [l0(3)],
                            (5, 0, 1): [l0(4, *both_read("1.0 in", 6))], (5, 1, 0): [l0(5)],
                            (6, 0, 1): [l0(6, *both_read("1.0 in", 8))], (6, 1, 0): [l0(7)]},
                   after_V={0: [fox_V], 1: [lambda V: rope_1(V, S1, 0)], 2: [lambda V: rope_1(V, S1, 512), l0_evac(0, 1)],
                            3: [l0_evac(2, 3)], 4: [l0_evac(4, 5)], 5: [l0_evac(6, 7)]},
                   after_A={0: [fox_A], 2: [l0_evac(0, 1)], 3: [l0_evac(2, 3)], 4: [l0_evac(4, 5)], 5: [l0_evac(6, 7)]})
        ja = jobs_l0("dilated")
        jb = jobs_l0("forget")
        for j in jb:
            j["group"] += 4
        att_phase("1.0 attention", ja + jb)
        out_phase("1.0 out", LAT, None)
        norm_phase("1.0 norm2", LAT, lambda k, s: (lay("ffn", 0, k), None))
        ffn_phases("1.0 ffn", LAT, 0, 1, None)
        norm_phase("1.1 norm", LAT, lambda k, s: (lay("attn", 1, k), None))
        l1_turns = turns_l1()
        l1 = lambda g, *needs: turn_step("1.1 turn", l1_turns, g, SIDE, *needs)
        l1_evac = lambda *which: evac_step("1.1 turn", l1_turns, which, SIDE)
        roped = lambda col: ("V", ("V", "rope", S2, col))
        proj_phase("1.1 in", QKV_CUTS, lambda c: LAT, plain(2, S2),
                   between={(2, 0, 1): [l1(0, roped(0))], (2, 1, 0): [l1(1)], (3, 0, 1): [l1(2, roped(512))], (3, 1, 0): [l1(3)],
                            (4, 0, 1): [l1(4, roped(1024))], (4, 1, 0): [l1(5)], (5, 0, 1): [l1(6, roped(1536))], (5, 1, 0): [l1(7)]},
                   after_V={0: [lambda V: rope_1(V, S2, 0)], 1: [lambda V: rope_1(V, S2, 512), l1_evac(0, 1)],
                            2: [lambda V: rope_1(V, S2, 1024), l1_evac(2, 3)],
                            3: [lambda V: rope_1(V, S2, 1536), l1_evac(4, 5)], 4: [l1_evac(6, 7)]},
                   after_A={1: [l1_evac(0, 1)], 2: [l1_evac(2, 3)], 3: [l1_evac(4, 5)], 4: [l1_evac(6, 7)]})
        att_phase("1.1 attention", jobs_l1())

        def subln_V(V):
            o = lambda j: big[:, j * S2:j * S2 + D]
            heads_rms_V(V, "subln", [(o(j), NH) for j in range(2)], P, SUB_EPS)
            for j in range(2):
                h = hv(o(j), P)
                V.eng.wait_ge(vector_done, V.n)
                V.eng.tensor_tensor(h, h, over(rms[:, j * NH:(j + 1) * NH], NH, P), ALU.mult).then_inc(vector_done, V.one())
                V.eng.wait_ge(vector_done, V.n)
                V.eng.tensor_tensor(h, h, under(sub_g[:, :], NH, P), ALU.mult).then_inc(vector_done, V.one())
        phase("1.1 subln", None, subln_V, lambda A: heads_rms_A(A, "subln", 2 * NH))
        turn_phase("1.1 turn2", turns_sub())
        out_phase("1.1 out", LAT, None)
        norm_phase("1.1 norm2", LAT, lambda k, s: (lay("ffn", 1, k), None))
        ffn_phases("1.1 ffn", LAT, 1, 1, None)

        def final_A(A):
            for j, t in enumerate(LAT):
                A.eng.wait_ge(scalar_done, A.n)
                A.eng.activation(gate[:, 0:D], xt[:, t, :], ACT.Square, scale=D ** -0.5, accum_out=stat[:, j:j + 1]).then_inc(scalar_done, A.one(("A", "final", "ms")))
            A.eng.wait_ge(vector_done, done("V", "final", "inverse"))
            A.eng.wait_ge(scalar_done, A.n)
            A.eng.activation(stat[:, 8:10], stat[:, 4:6], ACT.Sqrt).then_inc(scalar_done, A.one(("A", "final", "rstd")))

        def final_V(V):
            V.eng.wait_ge(scalar_done, done("A", "final", "ms"))
            V.eng.wait_ge(vector_done, V.n)
            V.eng.tensor_scalar(stat[:, 4:6], stat[:, 0:2], EPS, None, ALU.add).then_inc(vector_done, V.one())
            V.eng.wait_ge(vector_done, V.n)
            V.eng.reciprocal(stat[:, 4:6], stat[:, 4:6]).then_inc(vector_done, V.one(("V", "final", "inverse")))
            V.eng.wait_ge(scalar_done, done("A", "final", "rstd"))
            for j, t in enumerate(LAT):
                V.eng.wait_ge(vector_done, V.n)
                V.eng.scalar_tensor_tensor(out=xt[:, t, :], in0=xt[:, t, :], scalar=stat[:, 8 + j:9 + j], in1=final_g[:, :],
                                                  op0=ALU.mult, op1=ALU.mult).then_inc(vector_done, V.one())
        phase("1 final", None, final_V, final_A)

        def shift_scale(layer, m):
            a, b = layer * 32 + m * 16, layer * 64 + 2 * m * 16
            return lambda k, s: (acol[:, a + 2 * k + s:a + 2 * k + s + 1], modcol[:, b + 2 * k + s:b + 2 * k + s + 1])

        norm_phase("2.0 norm", ALL, shift_scale(0, 0))
        def dup_V(V, t, k):
            d = kdup(t).rearrange("p (g two e) -> p g two e", g=2, two=2)
            for m in range(2):
                V.eng.wait_ge(vector_done, V.n)
                V.eng.tensor_copy(d[:, :, m, :], k.rearrange("p (g e) -> p g e", g=2)).then_inc(vector_done, V.one())

        def swa_prep(V):
            rows_ = [(row3(t, 2064, 2704), NH + 2) for t in ALL]
            heads_rms_V(V, "swa", rows_, DH, EPS)
            for t in ALL:
                q, k = row3(t, 2064, 2576), row3(t, 2576, 2704)
                heads_scale_V(V, q, NH, 10 * t, qk_g[:, 0:DH])
                heads_scale_V(V, k, 2, 10 * t + NH, qk_g[:, DH:2 * DH])
                if t in LAT:
                    cs, sn = const("cos2", (t - 2) * DH, (t - 1) * DH), const("sin2", (t - 2) * DH, (t - 1) * DH)
                    rope_V(V, row3(t, 2064, 2704), NH + 2, cs, sn, True)
                dup_V(V, t, k)
            V.note(("V", "swa prep"))

        def even_dst(c, t, a, b):
            if (a, b) == (1024, 1536):
                return vals3(t)[:, :, 0:MD], lambda s: s.rearrange("p (h e) -> p h e", e=MD), ACT.Copy
            return row3(t, a, b), lambda s: s, (ACT.Sigmoid if (a, b) == (1536, 2048) else ACT.Copy)

        def value_ones(V):
            for t in ALL:
                V.eng.wait_ge(vector_done, V.n)
                V.eng.memset(vals3(t)[:, :, MD:MD + 1], 1.0).then_inc(vector_done, V.one())

        e0, e1 = turns_e(0), turns_e(1)
        LAST = (7,)
        e0_turn = lambda g, *needs: turn_step("2.0 turn", e0, g, LAST, *needs)
        e1_turn = lambda g, *needs: turn_step("2.0 turn3", e1, g, LAST, *needs)
        e0_evac, e1_evac = evac_step("2.0 turn", e0, range(8), LAST), evac_step("2.0 turn3", e1, range(6), LAST)
        proj_phase("2.0 in", EVEN_CUTS, lambda c: ALL, even_dst, lambda c, j: "A" if c == 4 else "VA"[j % 2],
                   between={(1, 0, 1): [lambda T: mgate_rows_T(T, "mg")], (3, 1, 0): [lambda T: mgate_cols_T(T, "mg")],
                            (4, 0, 1): [e1_turn(0, ("V", ("V", "swa prep")), ("V", ("V", "mg", "cols")))], (4, 0, 2): [e1_turn(1)], (4, 0, 3): [e1_turn(2)],
                            (4, 1, 0): [e1_turn(3)], (4, 1, 1): [e1_turn(4)], (4, 1, 2): [e1_turn(5)],
                            (5, 0, 0): [e0_turn(0, ("V", ("V", "2.0 turn3", "turn", 4)), ("A", ("A", "2.0 turn3", "turn", 5)), *both_read("2.0 in", 14), *both_read("2.0 in", 10))],
                            (5, 0, 1): [e0_turn(1)], (5, 0, 2): [e0_turn(2)], (5, 0, 3): [e0_turn(3)],
                            (5, 1, 0): [e0_turn(4)], (5, 1, 1): [e0_turn(5)], (5, 1, 2): [e0_turn(6)], (5, 1, 3): [e0_turn(7)]},
                   after_V={0: [value_ones], 1: [lambda V: mgate_V(V, "mg")], 2: [swa_prep],
                            3: [lambda V: mgate_cols_V(V, "mg"), e1_evac], 4: [e0_evac]},
                   after_A={1: [lambda A: mgate_A(A, "mg")], 2: [lambda A: heads_rms_A(A, "swa", 40)],
                            3: [lambda A: mgate_cols_A(A, "mg"), e1_evac], 4: [e0_evac]})
        phase("2.0 mlstm", lambda T: mlstm_T(T, "ml"), lambda V: mlstm_V(V, "ml"), lambda A: mlstm_A(A, "ml"))
        phase("2.0 mout", None, lambda V: mout_V(V, "mo"), lambda A: mout_A(A, "mo"))
        turn_phase("2.0 turn2", turns_mout())

        js = jobs_e(0)
        jl = jobs_e(1)
        for j in jl:
            j["group"] += 4
        att_phase("2.0 attention", js + jl)
        out_phase("2.0 out", ALL, 2)
        norm_phase("2.0 norm2", ALL, shift_scale(0, 1))
        ffn_phases("2.0 ffn", ALL, 0, 2, 5)
        norm_phase("2.1 norm", ALL, shift_scale(1, 0))

        def bias_load(G):
            rpb = io["na_rpb_2"]
            for h in range(NH):
                for t in range(2):
                    for r in range(2):
                        off = h * 465 + (r - 2 * t - 1 + 7) * 31 - 63 + 15
                        src = bass.AP(tensor=rpb.tensor, offset=off, ap=[[1, 64], [31, 4], [1, 64]])
                        G.eng.dma_start(nbias(h, t)[64 * r:64 * r + 64, :].rearrange("p (a b) -> p a b", a=4), src).then_inc(bias_in, 16)

        def odd_prep(V, key, rows_, dup):
            heads_rms_V(V, key, [(row4(t, a, b), n) for t, a, b, n, g, rot in rows_], DH, EPS)
            at = 0
            for t, a, b, n, g, rot in rows_:
                heads_scale_V(V, row4(t, a, b), n, at, qk_g[:, g * DH:(g + 1) * DH])
                at += n
                if rot:
                    cs, sn = const("cos2", (t - 2) * DH, (t - 1) * DH), const("sin2", (t - 2) * DH, (t - 1) * DH)
                    rope_V(V, row4(t, a, b), n, cs, sn, True)
                if dup:
                    dup_V(V, t, row4(t, a, b))
            V.note(("V", key))

        gk = [(t, 512, 640, 2, 3, t in LAT) for t in ALL]
        gq = [(t, 0, 512, NH, 2, True) for t in LAT]
        nq = [(t, 768, 1280, NH, 4, False) for t in LAT]
        nk = [(t, 1280, 1792, NH, 5, False) for t in ALL]
        ODD_T = lambda c: LAT if c in (1, 2) else ALL
        oo = turns_o()
        o_turn = lambda g, *needs: turn_step("2.1 turn", oo, g, LAST, *needs)
        o_evac = lambda which: evac_step("2.1 turn", oo, which, LAST)
        proj_phase("2.1 in", ODD_CUTS, ODD_T, plain(0, S4),
                   between={(2, 0, 1): [o_turn(0, ("V", ("V", "odd gk")))], (2, 1, 0): [o_turn(1)],
                            (3, 0, 1): [o_turn(2, ("V", ("V", "odd gq")))], (3, 0, 3): [o_turn(3)],
                            (4, 0, 0): [o_turn(4, ("V", ("V", "odd nq")))], (4, 0, 1): [o_turn(5)],
                            (4, 1, 0): [o_turn(6, ("V", ("V", "odd nk")))], (4, 1, 1): [o_turn(7)], (4, 1, 2): [o_turn(8)], (4, 1, 3): [o_turn(9)]},
                   after_V={0: [lambda V: odd_prep(V, "odd gk", gk, True)],
                            1: [o_evac((0, 1)), lambda V: odd_prep(V, "odd gq", gq, False)],
                            2: [lambda V: odd_prep(V, "odd nq", nq, False), o_evac((2, 3))],
                            3: [o_evac((4, 5)), lambda V: odd_prep(V, "odd nk", nk, False), o_evac(range(6, 10))]},
                   after_A={0: [lambda A: heads_rms_A(A, "odd gk", 8)], 1: [o_evac((0, 1)), lambda A: heads_rms_A(A, "odd gq", 16)],
                            2: [lambda A: heads_rms_A(A, "odd nq", 16), o_evac((2, 3))],
                            3: [o_evac((4, 5)), lambda A: heads_rms_A(A, "odd nk", 32), o_evac(range(6, 10))]},
                   G=bias_load)
        jg = jobs_o("global")
        jn = jobs_o("near")
        for j in jn:
            j["group"] += 4

        def odd_att_T(T):
            T.eng.wait_ge(bias_in, 16 * 4 * NH)
            att_T(T, "2.1 attention", jg + jn)
        phase("2.1 attention", odd_att_T, lambda V: att_V(V, "2.1 attention", jg + jn), lambda A: att_A(A, "2.1 attention", jg + jn))
        out_phase("2.1 out", LAT, 2, 1)
        norm_phase("2.1 norm2", LAT, shift_scale(1, 1))
        ffn_phases("2.1 ffn", LAT, 1, 2, 5)

        def bcast(v, n):
            return bass.AP(tensor=v.tensor, offset=v.offset, ap=[[0, P], [1, n]])

        rows = lambda a: a.rearrange("(r n) -> r n", n=P)
        loads = [
            (con[:, :], io["const"]),
            (xt[:, 2:4, :], io["x"][0].rearrange("(t p) d -> p t d", p=P)),
            (xt[:, 0:2, :], io["ctx_2"][0].rearrange("(t p) d -> p t d", p=P)),
            (vrows[0:16, :], rows(io["attn_norm"].rearrange("a n -> (a n)"))),
            (vrows[16:32, :], rows(io["ffn_norm"].rearrange("a n -> (a n)"))),
            (vrows[32:64, :], rows(io["norm_g_2"].rearrange("a b n -> (a b n)"))),
            (vrows[64:72, :], rows(io["c_ctx_2"])),
            (vrows[72:80, :], rows(io["c_2"][0])),
            (final_g[:, :], bcast(io["final_norm"], D)),
            (head_g[:, :], bcast(io["mlstm_head_g_2"], 512)),
            (sub_g[:, :], bcast(io["diff_subln"], P)),
            (qk_g[:, 0:P], bcast(io["swa_qk_g_2"], P)),
            (qk_g[:, P:2 * P], bcast(io["gqa_qk_g_2"], P)),
            (qk_g[:, 2 * P:3 * P], bcast(io["na_qk_g_2"], P)),
            (sink[:, :], bcast(io["swa_sink_2"], NH)),
            (lam_in[:, :], bcast(io["diff_lambda"], 256)),
            (gbias[0:MH, :], io["mlstm_gate_b_2"][0].rearrange("(g h) -> h g", h=MH)),
            (fbias[0:NH, :], io["hyb_b_f"][0].rearrange("(h o) -> h o", o=1)),
        ]
        for l in range(2):
            loads.append((crow[l][0:66, :], rows(io["ffn_conv_w"][l].rearrange("a n -> (a n)"))))
            loads.append((crow[l][66:88, :], rows(io["ffn_conv_b"][l])))
            w2 = rows(io["ffn_conv_w_2"][l].rearrange("a n -> (a n)"))
            loads.append((crow[2 + 2 * l][0:88, :], w2[0:88, :]))
            loads.append((crow[3 + 2 * l][0:44, :], w2[88:132, :]))
            loads.append((crow[3 + 2 * l][44:88, :], rows(io["ffn_conv_b_2"][l])))
        N_LOADS = len(loads)

        block = ctx.enter_context(nc.Block())

        def run(E):
            before = None
            for name, parts in phases:
                if before is not None:
                    fence(E, before)
                if parts[E.name] is not None:
                    parts[E.name](E)
                E.note((E.name, "end", name))
                before = name
            return before

        @block.sync
        def _(sp):
            for u, (src, view) in enumerate(stream):
                if u >= SLOTS:
                    sp.wait_ge(tensor_done, done("T", "slot", u - SLOTS))
                sp.dma_start(view(wslot[:, u % SLOTS, :]), src).then_inc(slot_full[u % SLOTS], 16)
            last = phases[-1][0]
            sp.wait_ge(vector_done, done("V", "end", last))
            sp.dma_start(out[0].rearrange("(t p) d -> p t d", p=P), xt[:, 2:4, :]).then_inc(stored, 16)
            sp.wait_ge(stored, 16)

        @block.scalar
        def _(act):
            for dst, src in loads:
                act.dma_start(dst, src).then_inc(loaded, 16)
            run(Progress("A", act, scalar_done, noted))

        @block.gpsimd
        def _(pool):
            run(Progress("G", pool, gpsimd_done, noted))

        @block.tensor
        def _(pe):
            run(Progress("T", pe, tensor_done, noted))
            assert Taken.n == len(stream), (Taken.n, len(stream))

        @block.vector
        def _(dve):
            run(Progress("V", dve, vector_done, noted))


_INS = ["x", "attn_norm", "ffn_norm", "final_norm", "hyb_w_in", "hyb_b_f", "hyb_w_out", "diff_w_qkv", "diff_lambda",
        "diff_subln", "diff_w_out", "ffn_w_up", "ffn_conv_w", "ffn_conv_b", "ffn_w_down", "c_2", "ctx_2", "c_ctx_2",
        "ada_w_2", "ada_b_2", "norm_g_2", "w_out_2", "ffn_up_2", "ffn_conv_w_2", "ffn_conv_b_2", "ffn_down_2",
        "even_w_in_2", "mlstm_gate_b_2", "mlstm_head_g_2", "swa_qk_g_2", "swa_sink_2", "odd_w_in_2", "gqa_qk_g_2",
        "na_qk_g_2", "na_rpb_2"]


def kernel(**inputs):
    import concourse.bacc as bacc
    from concourse.bass_utils import run_bass_kernel_spmd

    known, noted = {}, {}
    for _ in range(2):
        nc = bacc.Bacc("TRN2", target_bir_lowering=False, num_devices=1)
        arrays, io = {}, {}
        for name in _INS + ["const"]:
            a = constants() if name == "const" else np.ascontiguousarray(inputs[name])
            arrays[f"in_{name}"] = a
            io[name] = nc.dram_tensor(f"in_{name}", a.shape, F32, kind="ExternalInput").ap()
        out = nc.dram_tensor("out_0", (1, SEQ, D), F32, kind="ExternalOutput").ap()
        noted = {}
        with nc.allow_non_contiguous_dma(reason="columns of weights, and a few small vectors"):
            program(nc, io, out, known, noted)
        known = noted
    r = run_bass_kernel_spmd(nc, [arrays], core_ids=[0])
    return r.results[0]["out_0"]
```

```python
import math
from contextlib import ExitStack

import numpy as np
import concourse.bass as bass
from concourse import mybir

ALU = mybir.AluOpType
ACT = mybir.ActivationFunctionType
F32 = mybir.dt.float32
F32R = mybir.dt.float32r
AX_X = mybir.AxisListType.X

P = 128
D = 1024
KT = D // P
DH = 64
NH = 8
FF = 2816
FC = FF // P
SEQ = 256
TT = 4
CTX, LAT, ALL = (0, 1), (2, 3), (0, 1, 2, 3)
MH, MD = 4, 128
SLOTS = 3
SLOT = 2048
HALF = SLOT // 2
HIGHS = 4
BIG_N = 4 * 2836
BIG_NEG = 1e30
LAM_INIT = 0.8 - 0.6 * math.exp(-0.3 * 1)
EPS, SUB_EPS = 1e-6, 1e-5

WIDTHS = dict(ident=128, negflip=128, dilated=512, causal=256, window=1024, nbhood=512, later=128, earlier=128,
              cos1=128, sin1=128, cos2=128, sin2=128)
AT = {}
_n = 0
for _k, _w in WIDTHS.items():
    AT[_k] = (_n, _w)
    _n += _w
NCONST = _n


def constants():
    c = {k: np.zeros((P, w), np.float32) for k, w in WIDTHS.items()}
    c["ident"][:] = np.eye(P)
    c["negflip"][:] = -np.eye(P)[::-1]
    t = np.arange(SEQ)
    delta = t[:, None] - t[None, :]
    count = ((delta >= 0) & (delta <= 128)).astype(int) + ((delta >= 0) & (delta % 4 == 0)) + ((delta >= 0) & (delta % 16 == 0))
    dil = np.where(count > 0, -np.log(np.maximum(count, 1)), BIG_NEG).astype(np.float32)
    c["dilated"][:] = dil.reshape(2, P, SEQ).transpose(1, 0, 2).reshape(P, -1)
    p = np.arange(P)
    c["causal"][:, P:] = np.where(p[None, :] > p[:, None], BIG_NEG, 0)
    win = np.where(np.abs(delta) <= 128, 0, BIG_NEG).astype(np.float32).reshape(2, P, SEQ)
    w = c["window"].reshape(P, 2, 512)
    w[:, :, SEQ:] = win.transpose(1, 0, 2)
    col = np.arange(64)
    first = np.clip(col - 8, 0, 48)
    ok = (col[None, :] >= first[:, None]) & (col[None, :] < first[:, None] + 16)
    c["nbhood"][:, SEQ:] = np.tile(np.where(ok, 0, BIG_NEG), (2, 4))
    c["later"][:] = np.where(p[:, None] > p[None, :], -BIG_NEG, 0)
    c["earlier"][:] = np.where(p[:, None] < p[None, :], -BIG_NEG, 0)
    f = np.float32
    inv = (1.0 / (f(10000.0) ** (np.arange(0, DH, 2, dtype=f) / f(DH)))).astype(f)
    ang = np.arange(SEQ, dtype=f)[:, None] * inv[None, :]
    ang = np.concatenate([ang, ang], -1)
    sgn = np.where(np.arange(DH) < DH // 2, -1, 1).astype(f)
    tile = lambda a: a.astype(f).reshape(2, P, DH).transpose(1, 0, 2).reshape(P, -1)
    c["cos1"][:], c["sin1"][:] = tile(np.cos(ang)), tile(np.sin(ang) * sgn)
    freq = (f(10000.0) ** (-np.arange(0, 32, 2, dtype=f) / f(32))).astype(f)
    r = (t // 64).astype(f)[:, None] * freq[None, :]
    k = (t % 64).astype(f)[:, None] * freq[None, :]
    ang = np.concatenate([r, r, k, k], -1)
    sgn = np.where(np.arange(DH) % 32 < 16, -1, 1).astype(f)
    c["cos2"][:], c["sin2"][:] = tile(np.cos(ang)), tile(np.sin(ang) * sgn)
    return np.ascontiguousarray(np.concatenate([c[k] for k in WIDTHS], 1))



class Progress:

    def __init__(self, name, eng, sem, noted):
        self.name, self.eng, self.sem, self.noted, self.n = name, eng, sem, noted, 0

    def one(self, step=None):
        self.n += 1
        if step is not None:
            self.note(step)
        return 1

    def note(self, step):
        self.noted[step] = self.n


def program(nc, io, out, known, noted, debug=None):
    with ExitStack() as ctx:
        base = -(-nc.sbuf_base // 32) * 32
        used = [0]

        def sb(name, width, dtype=F32, over=None):
            at = used[0] if over is None else over
            if over is None:
                used[0] += -(-width // 8) * 8
            return nc.alloc_sbuf_tensor_at(name, [P, width], dtype, offset=base + 4 * at)

        ring_at = used[0]
        ring = sb("weights", SLOTS * SLOT)
        ring_low = sb("weights_low", SLOTS * SLOT, F32R, ring_at)
        ring_high = sb("weights_high", HIGHS * HALF, F32R)
        x_t = sb("x_tokens", TT * D)
        nt_at = used[0]
        nt_high = sb("normed_features_high", KT * 512, F32R)
        nt_low = sb("normed_features_low", KT * 512, F32R)
        m_rows = sb("minus_M_rows", 1024, F32, nt_at)
        big_at = used[0]
        big = sb("big", BIG_N)
        hid_high = sb("hidden_high", FC * 512, F32R, big_at)
        hid_low_narrow = sb("hidden_low_narrow", FC * 256, F32R, big_at + FC * 256)
        qkt_at = used[0]
        qkt = sb("qk_features", 7168)
        work = sb("work", 4608)
        hid_low_wide = sb("hidden_low_wide", FC * 512, F32R, qkt_at)
        gate = sb("gate_rows", 2048)
        con = sb("con", NCONST)
        final_g = sb("final_g", D)
        head_g = sb("head_g", 512)
        sub_g = sb("sub_g", P)
        qk_g = sb("qk_g", 3 * P)
        sink = sb("sink", NH)
        nsink = sb("nsink", NH)
        lam = sb("lam", 8)
        veccol = sb("veccol", 80)
        convcol = sb("convcol", 6 * 88)
        mod = sb("mod", 3 * 512)
        modcol = sb("modcol", 2 * 64)
        acol = sb("acol", 2 * 2 * 16)
        gbias = sb("gbias", 4)
        fbias = sb("fbias", 1)
        stat = sb("stat", 64)
        mxs = sb("mxs", 4 * 4)
        mcol = sb("mcol", 64)
        st2 = sb("st2", 128)
        rms = sb("rms", 96)
        lam_in = work[:, 1024:1280]
        psum = [ctx.enter_context(nc.psum_tensor(f"bank{i}", [P, 512], F32)) for i in range(8)]

        def sem(name):
            return ctx.enter_context(nc.semaphore(name))

        tensor_done, vector_done, scalar_done, gpsimd_done = sem("tensor_done"), sem("vector_done"), sem("scalar_done"), sem("gpsimd_done")
        slot_full = [sem(f"slot{i}_full") for i in range(SLOTS)]
        ada_full = [sem(f"ada_tile{i}_full") for i in range(2)]
        loaded = sem("small_inputs_loaded")
        x_in = sem("tokens_loaded")
        bias_in = sem("neighbour_bias_loaded")
        adab_in = sem("ada_bias_loaded")
        stored = sem("output_stored")
        SEM = {"T": tensor_done, "V": vector_done, "A": scalar_done, "G": gpsimd_done}

        def done(*step):
            return known.get(step, 0)

        def const(name, a=0, b=None, rows=slice(0, P)):
            o, w = AT[name]
            return con[rows, o + a:o + (w if b is None else b)]

        ident = const("ident")
        xt = x_t[:, :].rearrange("p (t d) -> p t d", t=TT)
        nTh = nt_high[:, :].rearrange("p (k t) -> p k t", k=KT)
        nTl = nt_low[:, :].rearrange("p (k t) -> p k t", k=KT)
        wslot = ring[:, :].rearrange("p (s n) -> p s n", s=SLOTS)
        wlow = ring_low[:, :].rearrange("p (s n) -> p s n", s=SLOTS)
        whigh = ring_high[:, :].rearrange("p (s n) -> p s n", s=HIGHS)

        def pick(n, row, rows=slice(0, P)):
            return const("ident", row, row + 1, rows).to_broadcast([n, P])

        stream, halves, first_half, first_slot = [], [], {}, {}

        def begin(ph):
            first_half[ph], first_slot[ph] = len(halves), len(stream)

        def add_proj(ph, w, cuts):
            begin(ph)
            for a, b in cuts:
                for half in range(2):
                    src = w[half * 512:half * 512 + 512, a:b].rearrange("(k p) n -> p k n", p=P)
                    for q in range(2):
                        halves.append((len(stream), lambda s, n=b - a, q=q: s.rearrange("p (k n) -> p k n", k=4)[:, 2 * q:2 * q + 2, 0:n],
                                       lambda s, n=b - a: s.rearrange("p (k n) -> p k n", k=2)[:, :, 0:n]))
                    stream.append((src, lambda s, n=b - a: s.rearrange("p (k n) -> p k n", k=4)[:, :, 0:n]))
                    issue.append(("weights", len(stream) - 1))

        def cuts_of(n):
            return [(a, min(a + 512, n)) for a in range(0, n, 512)]

        HYB_CUTS = [(2824, 3080), (0, 512), (512, 1024), (1536, 2048), (2048, 2560), (1024, 1536), (2560, 2824)]
        QKV_CUTS = cuts_of(3072)
        OUT_CUTS = cuts_of(1024)
        EVEN_CUTS = [(2048, 2448), (2448, 2832), (0, 512), (512, 1024), (1536, 2048), (1024, 1536)]
        ODD_CUTS = [(512, 768), (0, 512), (768, 1280), (1280, 1792), (1792, 2304)]

        ADA_AFTER = [2 if f >= FC - 2 else 1 for f in range(FC)]
        ADA_N = KT * 3
        ada_slot = [work[:, 0:SLOT], work[:, SLOT:2 * SLOT]]
        ada_stream, issue = [], []

        def add_up(ph, w, ada=None):
            begin(ph)
            first = len(ada_stream)
            if ada is not None:
                ada_stream.extend(ada[k * P:(k + 1) * P, g * 2048:(g + 1) * 2048] for g in range(3) for k in range(KT))
            for f in range(FC):
                src = w.rearrange("(k p) (u f c) -> p u k f c", p=P, u=2, c=P)[:, :, :, f, :]
                for u in range(2):
                    halves.append((len(stream), lambda s, u=u: s.rearrange("p (u k c) -> p u k c", u=2, c=P)[:, u, :, :],
                                   lambda s: s.rearrange("p (k c) -> p k c", c=P)))
                stream.append((src, lambda s: s.rearrange("p (u k c) -> p u k c", u=2, c=P)))
                issue.append(("weights", len(stream) - 1))
                if ada is not None and f >= 2:
                    issue.extend(("ada", first + n) for n in ([0, 1] if f == 2 else [f - 1] if f < FC - 1 else range(f - 1, ADA_N)))

        def add_down_rows(ph, w):
            begin(ph)
            for f in range(0, FC, 2):
                for c in range(2):
                    halves.append((len(stream), lambda s, c=c: s[:, c * D:(c + 1) * D], lambda s: s))
                stream.append((w[f * P:(f + 2) * P, :].rearrange("(c p) n -> p c n", p=P),
                               lambda s: s.rearrange("p (c n) -> p c n", c=2)))
                issue.append(("weights", len(stream) - 1))

        def add_down_halves(ph, w):
            begin(ph)
            for half in range(2):
                for f in range(0, FC, 4):
                    m = min(4, FC - f)
                    for q in range(m // 2):
                        halves.append((len(stream), lambda s, q=q: s.rearrange("p (c n) -> p c n", c=4)[:, 2 * q:2 * q + 2, :],
                                       lambda s: s.rearrange("p (c n) -> p c n", c=2)))
                    stream.append((w[f * P:(f + m) * P, half * 512:half * 512 + 512].rearrange("(c p) n -> p c n", p=P),
                                   lambda s, m=m: s.rearrange("p (c n) -> p c n", c=4)[:, 0:m, :]))
                    issue.append(("weights", len(stream) - 1))

        add_proj("1.0 in", io["hyb_w_in"][0], HYB_CUTS)
        add_proj("1.0 out", io["hyb_w_out"][0], OUT_CUTS)
        add_up("1.0 ffn up", io["ffn_w_up"][0], io["ada_w_2"][0])
        add_down_rows("1.0 ffn down", io["ffn_w_down"][0])
        add_proj("1.1 in", io["diff_w_qkv"][0], QKV_CUTS)
        add_proj("1.1 out", io["diff_w_out"][0], OUT_CUTS)
        add_up("1.1 ffn up", io["ffn_w_up"][1], io["ada_w_2"][1])
        add_down_rows("1.1 ffn down", io["ffn_w_down"][1])
        add_proj("2.0 in", io["even_w_in_2"][0], EVEN_CUTS)
        add_proj("2.0 out", io["w_out_2"][0], OUT_CUTS)
        add_up("2.0 ffn up", io["ffn_up_2"][0])
        add_down_halves("2.0 ffn down", io["ffn_down_2"][0])
        add_proj("2.1 in", io["odd_w_in_2"][0], ODD_CUTS)
        add_proj("2.1 out", io["w_out_2"][1], OUT_CUTS)
        add_up("2.1 ffn up", io["ffn_up_2"][1])
        add_down_rows("2.1 ffn down", io["ffn_down_2"][1])


        class Count:
            half = high = 0

        def take_half(T):
            m = Count.half
            Count.half += 1
            u, raw, high = halves[m]
            T.eng.wait_ge(gpsimd_done, done("G", "low", m))
            return high(whigh[:, m % HIGHS, :]), raw(wlow[:, u % SLOTS, :]), m

        def half_read(T, i, m):
            i.then_inc(tensor_done, T.one(("T", "half", m)))
            u = halves[m][0]
            if m + 1 == len(halves) or halves[m + 1][0] != u:
                T.note(("T", "slot", u))

        def ahead(A, upto):
            while Count.high < min(upto, len(halves)):
                m = Count.high
                Count.high += 1
                u, raw, high = halves[m]
                A.eng.wait_ge(slot_full[u % SLOTS], 16 * (u // SLOTS + 1))
                if m >= HIGHS:
                    A.eng.wait_ge(tensor_done, done("T", "half", m - HIGHS))
                A.eng.activation(high(whigh[:, m % HIGHS, :]), raw(wslot[:, u % SLOTS, :]), ACT.Copy).then_inc(scalar_done, A.one(("A", "high", m)))

        def lows_G(G, first, end):
            for m in range(first, end):
                u, raw, high = halves[m]
                G.eng.wait_ge(scalar_done, done("A", "high", m))
                G.eng.tensor_tensor(raw(wlow[:, u % SLOTS, :]), raw(wslot[:, u % SLOTS, :]), high(whigh[:, m % HIGHS, :]).bitcast(F32),
                                    ALU.subtract).then_inc(gpsimd_done, G.one(("G", "low", m)))

        def product(T, out_, left, right, first, last):
            (lh, ll), (rh, rl) = left, right
            T.eng.matmul(out_, lh, rh, start=first, stop=False)
            T.eng.matmul(out_, ll, rh, start=False, stop=False)
            return T.eng.matmul(out_, lh, rl, start=False, stop=last)

        def fence(E, phase):
            for o in "TVA":
                if o != E.name:
                    E.eng.wait_ge(SEM[o], done(o, "end", phase))

        XN = [work[:, 0:1024], work[:, 1024:2048], work[:, 2048:3072], work[:, 3072:4096]]

        def squares_A(A, ph, parts):
            for step, bank, t, a, b in parts:
                A.eng.wait_ge(SEM[step[0]], done(*step))
                for c in range(a, b, 512):
                    A.eng.activation(psum[bank][:, 0:512], xt[:, t, c:c + 512], ACT.Square, scale=D ** -0.5,
                                     accum_out=stat[:, 2 * t + c // 512:2 * t + c // 512 + 1]).then_inc(scalar_done, A.one())
                    A.eng.wait_ge(scalar_done, A.n)

        def rstd_V(V, ph, tiles):
            t0, n = tiles[0], len(tiles)
            s2 = stat[:, 2 * t0:2 * t0 + 2 * n].rearrange("p (t h) -> p t h", h=2)
            V.eng.wait_ge(vector_done, V.n)
            V.eng.scalar_tensor_tensor(out=stat[:, 16:16 + n], in0=s2[:, :, 0], scalar=EPS, in1=s2[:, :, 1], op0=ALU.add, op1=ALU.add).then_inc(vector_done, V.one())
            V.eng.wait_ge(vector_done, V.n)
            V.eng.reciprocal(stat[:, 16:16 + n], stat[:, 16:16 + n]).then_inc(vector_done, V.one(("V", ph, "inverse")))
            V.eng.wait_ge(scalar_done, done("A", ph, "rstd"))

        def rstd_A(A, ph, tiles):
            n = len(tiles)
            A.eng.wait_ge(vector_done, done("V", ph, "inverse"))
            A.eng.activation(stat[:, 24:24 + n], stat[:, 16:16 + n], ACT.Sqrt).then_inc(scalar_done, A.one(("A", ph, "rstd")))

        def norm_A(A, ph, tiles):
            rstd_A(A, ph, tiles)
            A.eng.wait_ge(scalar_done, A.n)
            for j in range(1, len(tiles), 2):
                A.eng.activation(XN[j], xt[:, tiles[j], :], ACT.Copy, scale=stat[:, 24 + j:25 + j]).then_inc(scalar_done, A.one(("A", ph, "xn", j)))

        def norm_V(V, ph, tiles):
            rstd_V(V, ph, tiles)
            for j in range(0, len(tiles), 2):
                V.eng.tensor_scalar(XN[j], xt[:, tiles[j], :], stat[:, 24 + j:25 + j], None, ALU.mult).then_inc(vector_done, V.one(("V", ph, "xn", j)))

        def norm_T(T, ph, tiles):
            for j in range(len(tiles)):
                e = "VA"[j % 2]
                T.eng.wait_ge(SEM[e], done(e, ph, "xn", j))
                for k in range(KT):
                    i = T.eng.transpose(psum[k][:, j * P:(j + 1) * P], XN[j][:, k * P:(k + 1) * P], ident)
                    if j == len(tiles) - 1:
                        i.then_inc(tensor_done, T.one(("T", ph, "k", k)))

        TMP = [gate[:, 1024:1536], gate[:, 1536:2048]]

        def span(tiles):
            return slice(tiles[0] * P, (tiles[-1] + 1) * P)

        def norm_evac_V(V, ph, tiles, which):
            n = len(tiles) * P
            for k in range(KT + 1):
                if k < KT:
                    V.eng.wait_ge(tensor_done, done("T", ph, "k", k))
                    for s in sorted({t // 2 for t in tiles}):
                        lo = [j for j, t in enumerate(tiles) if t // 2 == s][0] * P
                        dst, src = TMP[k % 2][:, lo:lo + SEQ], psum[k][:, lo:lo + SEQ]
                        a, b = which(k, s)
                        V.eng.wait_ge(vector_done, V.n)
                        if b is None:
                            V.eng.tensor_scalar(dst, src, a, None, ALU.mult).then_inc(vector_done, V.one(("V", ph, "features", k)))
                        else:
                            V.eng.tensor_scalar(dst, src, a, b, ALU.mult, ALU.add).then_inc(vector_done, V.one(("V", ph, "features", k)))
                if k >= 1:
                    q = k - 1
                    V.eng.wait_ge(scalar_done, done("A", ph, "high", q))
                    V.eng.wait_ge(vector_done, done("V", ph, "features", q))
                    V.eng.tensor_tensor(nTl[:, q, span(tiles)], TMP[q % 2][:, 0:n], nTh[:, q, span(tiles)].bitcast(F32),
                                        ALU.subtract).then_inc(vector_done, V.one(("V", ph, "low", q)))

        def norm_evac_A(A, ph, tiles):
            for k in range(KT):
                A.eng.wait_ge(vector_done, done("V", ph, "features", k))
                A.eng.activation(nTh[:, k, span(tiles)], TMP[k % 2][:, 0:len(tiles) * P], ACT.Copy).then_inc(scalar_done, A.one(("A", ph, "high", k)))

        def pieces_of(cuts, tiles_of, reader):
            out_ = []
            for c, (a, b) in enumerate(cuts):
                for j, t in enumerate(tiles_of(c)):
                    out_.append(dict(n=len(out_), c=c, j=j, t=t, a=a, b=b, reader=reader(c, j)))
            return out_

        def proj_T(T, ph, cuts, pieces, banks, between, normed=None, gates=None):
            for c, (a, b) in enumerate(cuts):
                mine = [p for p in pieces if p["c"] == c]
                for h4 in range(4):
                    wh, wl, m = take_half(T)
                    half, q = h4 // 2, h4 % 2
                    for p in mine:
                        bank = p["n"] % banks
                        if h4 == 0 and p["n"] >= banks:
                            o = pieces[p["n"] - banks]
                            T.eng.wait_ge(SEM[o["reader"]], done(o["reader"], ph, "piece", o["n"]))
                        elif h4 == 0 and bank == 4 and gates is not None:
                            T.eng.wait_ge(scalar_done, done("A", gates, "gates"))
                        elif h4 == 0 and normed is not None:
                            T.eng.wait_ge(vector_done, done("V", normed, "features", bank))
                        for kk in range(2):
                            k = 2 * h4 + kk
                            if c == 0 and p is mine[0] and normed is not None:
                                T.eng.wait_ge(vector_done, done("V", normed, "low", k))
                            tok = slice(p["t"] * P, (p["t"] + 1) * P)
                            i = product(T, psum[bank][:, 0:b - a], (nTh[:, k, tok], nTl[:, k, tok]), (wh[:, kk, :], wl[:, kk, :]), k == 0, k == KT - 1)
                        if p is mine[-1]:
                            half_read(T, i, m)
                            if h4 == 3:
                                T.note(("T", ph, "piece", p["n"]))
                        elif h4 == 3:
                            i.then_inc(tensor_done, T.one(("T", ph, "piece", p["n"])))
                        if q == 1:
                            for step in between.get((c, half, p["j"]), []):
                                step(T)

        def proj_read(E, ph, cuts, pieces, banks, dst, after):
            for c in range(len(cuts)):
                if E.name == "A":
                    ahead(E, first_half[ph] + 4 * (c + 1) + HIGHS)
                for p in pieces:
                    if p["c"] != c or p["reader"] != E.name:
                        continue
                    E.eng.wait_ge(tensor_done, done("T", ph, "piece", p["n"]))
                    src = psum[p["n"] % banks][:, 0:p["b"] - p["a"]]
                    to, view, func = dst(c, p["t"], p["a"], p["b"])
                    if E.name == "V":
                        E.eng.wait_ge(E.sem, E.n)
                        E.eng.tensor_copy(to, view(src)).then_inc(E.sem, E.one(("V", ph, "piece", p["n"])))
                    else:
                        E.eng.wait_ge(E.sem, E.n)
                        E.eng.activation(to, view(src), func).then_inc(E.sem, E.one(("A", ph, "piece", p["n"])))
                if E.name == "V" and c in after:
                    E.eng.wait_ge(scalar_done, done("A", ph, "piece", [p["n"] for p in pieces if p["c"] == c and p["reader"] == "A"][-1]))
                if E.name == "A" and c in after and c + 1 < len(cuts):
                    ahead(E, first_half[ph] + 4 * (c + 2))
                for step in after.get(c, []):
                    step(E)

        def residual_V(V, ph, parts, gated):
            for n, (step, bank, t, a, b) in enumerate(parts):
                V.eng.wait_ge(tensor_done, done(*step))
                src = psum[bank][:, 0:b - a]
                if gated:
                    s = t // 2
                    tmp = work[:, 4096:4096 + b - a]
                    V.eng.wait_ge(vector_done, V.n)
                    V.eng.tensor_tensor(tmp, src, gate[:, s * D + a:s * D + b], ALU.mult).then_inc(vector_done, V.one())
                    src = tmp
                V.eng.wait_ge(vector_done, V.n)
                V.eng.tensor_tensor(xt[:, t, a:b], xt[:, t, a:b], src, ALU.add).then_inc(vector_done, V.one(("V", ph, "x", n)))

        def rope_V(V, rows, n, tables, axial):
            m = 4 if axial else 2
            q = DH // m
            start = V.n
            sums = []
            for x, (row, (cos, sin)) in enumerate(zip(rows, tables)):
                src = row.rearrange("p (h m q) -> p h m q", m=m, q=q)
                o = work[:, 640 * (x % 2):640 * (x % 2) + n * DH]
                r = work[:, 1280 + 640 * (x % 2):1280 + 640 * (x % 2) + n * DH]
                c3 = cos.rearrange("p (o e) -> p o e", o=1).to_broadcast([P, n, DH])
                s4 = sin.rearrange("p (o m q) -> p o m q", o=1, m=m)
                r4 = r.rearrange("p (h m q) -> p h m q", m=m, q=q)
                V.eng.wait_ge(vector_done, sums[x - 2] if x >= 2 else start)
                V.eng.tensor_tensor(o.rearrange("p (h e) -> p h e", e=DH), row.rearrange("p (h e) -> p h e", e=DH), c3, ALU.mult).then_inc(vector_done, V.one())
                for a in range(m):
                    b = a ^ 1
                    V.eng.tensor_tensor(r4[:, :, a, :], src[:, :, b, :], s4[:, :, a, :].to_broadcast([P, n, q]), ALU.mult).then_inc(vector_done, V.one())
                V.eng.wait_ge(vector_done, V.n)
                V.eng.tensor_tensor(row, o, r, ALU.add).then_inc(vector_done, V.one())
                sums.append(V.n)

        hv = lambda a, e: a.rearrange("p (h e) -> p h e", e=e)
        over = lambda col, n, e: col.rearrange("p (h o) -> p h o", o=1).to_broadcast([P, n, e])
        under = lambda row, n, e: row.rearrange("p (o e) -> p o e", o=1).to_broadcast([P, n, e])

        def heads_rms_V(V, ph, rows, width, eps):
            at, reduced, begin_ = 0, [], V.n
            for x, (row, n) in enumerate(rows):
                sq = work[:, 640 * (x % 2):640 * (x % 2) + n * width]
                V.eng.wait_ge(vector_done, reduced[x - 2] if x >= 2 else begin_)
                V.eng.tensor_tensor(sq, row, row, ALU.mult).then_inc(vector_done, V.one())
                V.eng.wait_ge(vector_done, V.n)
                V.eng.tensor_reduce(rms[:, at:at + n], hv(sq, width), AX_X, ALU.add).then_inc(vector_done, V.one())
                reduced.append(V.n)
                at += n
            V.eng.wait_ge(vector_done, V.n)
            V.eng.tensor_scalar(rms[:, 0:at], rms[:, 0:at], 1.0 / width, eps, ALU.mult, ALU.add).then_inc(vector_done, V.one())
            V.eng.wait_ge(vector_done, V.n)
            V.eng.reciprocal(rms[:, 0:at], rms[:, 0:at]).then_inc(vector_done, V.one(("V", ph, "inverse")))
            V.eng.wait_ge(scalar_done, done("A", ph, "rstd"))

        def heads_rms_A(A, ph, n):
            A.eng.wait_ge(vector_done, done("V", ph, "inverse"))
            A.eng.wait_ge(scalar_done, A.n)
            A.eng.activation(rms[:, 0:n], rms[:, 0:n], ACT.Sqrt).then_inc(scalar_done, A.one(("A", ph, "rstd")))

        def heads_scale_V(V, parts):
            scaled = []
            for row, n, at, g in parts:
                V.eng.tensor_tensor(hv(row, DH), hv(row, DH), over(rms[:, at:at + n], n, DH), ALU.mult).then_inc(vector_done, V.one())
                scaled.append(V.n)
            for (row, n, at, g), first in zip(parts, scaled):
                V.eng.wait_ge(vector_done, first)
                V.eng.tensor_tensor(hv(row, DH), hv(row, DH), under(g, n, DH), ALU.mult).then_inc(vector_done, V.one())

        def turn_T(T, ph, groups, g, banks, needs):
            srcs = groups[g][0]
            for e, step in needs:
                T.eng.wait_ge(SEM[e], done(*step))
            if g >= len(banks):
                e = "VA"[(g - len(banks)) % 2]
                T.eng.wait_ge(SEM[e], done(e, ph, "turn", g - len(banks)))
            for j, s in enumerate(srcs):
                i = T.eng.transpose(psum[banks[g % len(banks)]][:, j * P:(j + 1) * P], s, ident)
            i.then_inc(tensor_done, T.one(("T", ph, "turn", g)))

        def turns_T(T, ph, groups, banks=tuple(range(8)), needs=()):
            for g in range(len(groups)):
                turn_T(T, ph, groups, g, banks, needs if g == 0 else ())

        def turns_evac(E, ph, groups, which, banks=tuple(range(8))):
            for g in which:
                srcs, dst, scale = groups[g]
                if "VA"[g % 2] != E.name:
                    continue
                E.eng.wait_ge(tensor_done, done("T", ph, "turn", g))
                src = psum[banks[g % len(banks)]][:, 0:len(srcs) * P]
                if E.name == "V":
                    if scale == 1.0:
                        E.eng.wait_ge(E.sem, E.n)
                        E.eng.tensor_copy(dst, src).then_inc(E.sem, E.one(("V", ph, "turn", g)))
                    else:
                        E.eng.wait_ge(E.sem, E.n)
                        E.eng.tensor_scalar(dst, src, scale, None, ALU.mult).then_inc(E.sem, E.one(("V", ph, "turn", g)))
                else:
                    E.eng.wait_ge(E.sem, E.n)
                    E.eng.activation(dst, src, ACT.Copy, scale=scale).then_inc(E.sem, E.one(("A", ph, "turn", g)))

        NB, PROBS, TURN, OUT, CLOSE, LOW = 4, 2, 3, 4, 5, 7
        PB = [work[:, 512 * i:512 * i + 512] for i in range(NB)]
        PTB = [work[:, 2048 + 512 * i:2560 + 512 * i] for i in range(NB)]

        def att_T(T, ph, jobs):
            n = len(jobs)
            for s in range(n + OUT):
                if s < n:
                    j = jobs[s]
                    if s >= 3:
                        e = "V" if jobs[s - 3]["mask"] is not None else "A"
                        T.eng.wait_ge(SEM[e], done(e, ph, "read", s - 3))
                    bank = psum[s % 3]
                    for (a, b, terms) in j["scores"]:
                        for m, (l, r) in enumerate(terms):
                            i = T.eng.matmul(bank[:, a:b], l, r, start=(m == 0), stop=(m == len(terms) - 1))
                    i.then_inc(tensor_done, T.one(("T", ph, "scores", s)))
                if 0 <= s - TURN < n:
                    q = s - TURN
                    T.eng.wait_ge(vector_done, done("V", ph, "probs", q))
                    if q >= 2:
                        T.eng.wait_ge(scalar_done, done("A", ph, "turned", q - 2))
                    for c in range(jobs[q]["n"] // P):
                        i = T.eng.transpose(psum[3 + q % 2][:, c * P:(c + 1) * P], PB[q % NB][:, c * P:(c + 1) * P], ident)
                    i.then_inc(tensor_done, T.one(("T", ph, "turn", q)))
                if 0 <= s - OUT < n:
                    q = s - OUT
                    j = jobs[q]
                    T.eng.wait_ge(scalar_done, done("A", ph, "turned", q))
                    ob, oa, ob_cols, first, last, tok = j["out"]
                    if j["open"] and j["group"] >= 2:
                        T.eng.wait_ge(scalar_done, done("A", ph, "group", j["group"] - 2))
                        T.eng.wait_ge(vector_done, done("V", ph, "group", j["group"] - 2))
                    nc_ = j["n"] // P
                    for c in range(nc_):
                        pt = PTB[q % NB][:, c * P:(c + 1) * P]
                        o = psum[5 + j["group"] % 2][oa, ob_cols]
                        l, r = (pt, j["v"][c]) if tok else (j["v"][c], pt)
                        i = T.eng.matmul(o, l, r, start=(first and c == 0), stop=(last and c == nc_ - 1))
                    i.then_inc(tensor_done, T.one(("T", ph, "out", q)))

        def att_V(V, ph, jobs, aside={}):
            n = len(jobs)
            for s in range(n + LOW):
                for step in aside.get(s, []):
                    step(V)
                if s < n:
                    j = jobs[s]
                    V.eng.wait_ge(tensor_done, done("T", ph, "scores", s))
                    mn = mxs[:, s % NB:s % NB + 1]
                    if s >= NB:
                        V.eng.wait_ge(tensor_done, done("T", ph, "turn", s - NB))
                    init = j["sink"] if j["sink"] is not None else None
                    if j["mask"] is not None:
                        V.eng.tensor_tensor_reduce(out=PB[s % NB][:, 0:j["n"]], in0=psum[s % 3][:, 0:j["n"]], in1=j["mask"],
                                                          scale=1.0, scalar=(3e38 if init is None else init), op0=ALU.add, op1=ALU.min,
                                                          accum_out=mn).then_inc(vector_done, V.one(("V", ph, "read", s)))
                    else:
                        V.eng.tensor_reduce(mn, psum[s % 3][:, 0:j["n"]], AX_X, ALU.min).then_inc(vector_done, V.one())
                        if init is not None:
                            V.eng.wait_ge(vector_done, V.n)
                            V.eng.tensor_tensor(mn, mn, init, ALU.min).then_inc(vector_done, V.one())
                    V.note(("V", ph, "max", s))
                if 0 <= s - PROBS < n:
                    q = s - PROBS
                    j = jobs[q]
                    den, r = mxs[:, 4 + q % NB:5 + q % NB], mxs[:, 12 + q % NB:13 + q % NB]
                    V.eng.wait_ge(scalar_done, done("A", ph, "exp", q))
                    if j["sink"] is not None:
                        V.eng.tensor_tensor(den, den, mxs[:, 8 + q % NB:9 + q % NB], ALU.add).then_inc(vector_done, V.one())
                    if j["sink"] is not None:
                        V.eng.wait_ge(vector_done, V.n)
                    V.eng.reciprocal(r, den).then_inc(vector_done, V.one())
                    if j["factor"] is None:
                        V.eng.wait_ge(vector_done, V.n)
                        V.eng.tensor_scalar(PB[q % NB][:, 0:j["n"]], PB[q % NB][:, 0:j["n"]], r, None, ALU.mult).then_inc(vector_done, V.one(("V", ph, "probs", q)))
                    else:
                        V.eng.wait_ge(vector_done, V.n)
                        V.eng.tensor_scalar(PB[q % NB][:, 0:j["n"]], PB[q % NB][:, 0:j["n"]], r, j["factor"], ALU.mult, ALU.mult).then_inc(vector_done, V.one(("V", ph, "probs", q)))
                if s >= LOW and jobs[s - LOW]["close"] is not None:
                    j = jobs[s - LOW]
                    src_cols, high, low = j["close"]
                    if low is not None:
                        V.eng.wait_ge(scalar_done, done("A", ph, "group", j["group"]))
                        V.eng.tensor_tensor(low, psum[5 + j["group"] % 2][:, src_cols], high.bitcast(F32), ALU.subtract).then_inc(vector_done, V.one(("V", ph, "group", j["group"])))

        def att_A(A, ph, jobs, aside={}):
            n = len(jobs)
            for s in range(n + CLOSE):
                for step in aside.get(s, []):
                    step(A)
                if s < n:
                    j = jobs[s]
                    A.eng.wait_ge(vector_done, done("V", ph, "max", s))
                    if s >= NB:
                        A.eng.wait_ge(vector_done, done("V", ph, "probs", s - NB))
                    src = PB[s % NB] if j["mask"] is not None else psum[s % 3]
                    mn = mxs[:, s % NB:s % NB + 1]
                    A.eng.activation(PB[s % NB][:, 0:j["n"]], src[:, 0:j["n"]], ACT.Exp, bias=mn, scale=-1.0,
                                            accum_out=mxs[:, 4 + s % NB:5 + s % NB]).then_inc(scalar_done, A.one(("A", ph, "read", s)))
                    if j["sink"] is not None:
                            A.eng.activation(mxs[:, 8 + s % NB:9 + s % NB], j["sink"], ACT.Exp, bias=mn, scale=-1.0).then_inc(scalar_done, A.one())
                    A.note(("A", ph, "exp", s))
                if 0 <= s - TURN < n:
                    q = s - TURN
                    A.eng.wait_ge(tensor_done, done("T", ph, "turn", q))
                    if q >= NB:
                        A.eng.wait_ge(tensor_done, done("T", ph, "out", q - NB))
                    m = jobs[q]["n"]
                    A.eng.activation(PTB[q % NB][:, 0:m], psum[3 + q % 2][:, 0:m], ACT.Copy).then_inc(scalar_done, A.one(("A", ph, "turned", q)))
                if 0 <= s - CLOSE < n and jobs[s - CLOSE]["close"] is not None:
                    q = s - CLOSE
                    src_cols, dst, _ = jobs[q]["close"]
                    A.eng.wait_ge(tensor_done, done("T", ph, "out", q))
                    A.eng.activation(dst, psum[5 + jobs[q]["group"] % 2][:, src_cols], ACT.Copy).then_inc(scalar_done, A.one(("A", ph, "group", jobs[q]["group"])))

        def jobs_of_pairs(heads, tiles, tile0, scores, n, mask, sink_of, values, dst):
            jobs = []
            group = 0
            for pair in range(heads // 2):
                for ti, t in enumerate(tiles):
                    for par in range(2):
                        h = 2 * pair + par
                        lastj = ti == len(tiles) - 1 and par == 1
                        jobs.append(dict(
                            n=n(t), scores=scores(h, t), mask=mask(t), sink=sink_of(h), factor=None, v=values(h, t),
                            out=(None, slice(64 * par, 64 * par + 64), slice(ti * P, (ti + 1) * P), True, True, False),
                            open=(ti == 0 and par == 0), group=group,
                            close=((slice(0, len(tiles) * P),) + dst(pair)) if lastj else None))
                group += 1
            return jobs

        WITH_ADA = ("1.0 ffn up", "1.1 ffn up")

        def up_bank(ph, f, u, n):
            return psum[f % 4][:, u * n:(u + 1) * n] if ph in WITH_ADA else psum[2 * (f % 4) + u][:, 0:n]

        def up_T(T, ph, lo, n, ada, normed):
            tile = 0
            T.eng.wait_ge(vector_done, done("V", normed, "features", 0))
            for f in range(FC):
                if f >= 4:
                    T.eng.wait_ge(vector_done, done("V", ph, "product", f - 4))
                for u in range(2):
                    wh, wl, m = take_half(T)
                    for k in range(KT):
                        if f == 0 and u == 0:
                            T.eng.wait_ge(vector_done, done("V", normed, "low", k))
                        i = product(T, up_bank(ph, f, u, n), (wh[:, k, :], wl[:, k, :]), (nTh[:, k, lo:lo + n], nTl[:, k, lo:lo + n]), k == 0, k == KT - 1)
                    half_read(T, i, m)
                T.note(("T", ph, "up", f))
                for _ in range(ADA_AFTER[f] if ada else 0):
                    ada_tile_T(T, ph, tile, 1 if ph == WITH_ADA[1] else 0)
                    tile += 1

        def cbuf(f, i, n):
            b = (f % 2) * 3 + i
            if n == SEQ:
                return qkt[:, b * 512:b * 512 + n]
            return gate[:, b * 512:b * 512 + n] if b < 4 else final_g[:, (b - 4) * 512:(b - 4) * 512 + n]

        hidh = lambda f, n: hid_high[:, f * n:(f + 1) * n]
        hidl = lambda f, n: (hid_low_narrow if n == SEQ else hid_low_wide)[:, f * n:(f + 1) * n]

        def up_A(A, ph, n, taps, both):
            mid, bias = taps
            m0 = first_half[ph]
            ahead(A, m0 + HIGHS)
            for f in range(FC):
                ahead(A, m0 + 2 * f + 1 + HIGHS)
                A.eng.wait_ge(tensor_done, done("T", ph, "up", f))
                if f >= 2:
                    A.eng.wait_ge(vector_done, done("V", ph, "low", f - 2))
                for u in range(2 if both else 1):
                    A.eng.activation(cbuf(f, u, n), up_bank(ph, f, u, n), ACT.Identity,
                                     scale=mid(u, f), bias=bias(u, f)).then_inc(scalar_done, A.one(("A", ph, "mid", f, u)))
                ahead(A, m0 + 2 * f + 2 + HIGHS)
                A.eng.wait_ge(vector_done, done("V", ph, "conv", f))
                A.eng.activation(cbuf(f, 2, n), cbuf(f, 0, n), ACT.Silu).then_inc(scalar_done, A.one(("A", ph, "silu", f)))
                A.eng.wait_ge(vector_done, done("V", ph, "product", f))
                A.eng.activation(hidh(f, n), cbuf(f, 1, n), ACT.Copy).then_inc(scalar_done, A.one(("A", ph, "high", f)))

        def up_low_V(V, ph, f, n):
            V.eng.wait_ge(scalar_done, done("A", ph, "high", f))
            V.eng.tensor_tensor(hidl(f, n), cbuf(f, 1, n), hidh(f, n).bitcast(F32), ALU.subtract).then_inc(vector_done, V.one(("V", ph, "low", f)))

        def up_V_causal(V, ph, n, tap):
            for f in range(FC):
                g = up_bank(ph, f, 0, n)
                c = cbuf(f, 0, n)
                V.eng.wait_ge(scalar_done, done("A", ph, "mid", f, 0))
                for back in (1, 2):
                    V.eng.wait_ge(vector_done, V.n)
                    V.eng.scalar_tensor_tensor(out=c[:, back:n], in0=g[:, 0:n - back], scalar=tap(2 - back, f),
                                                      in1=c[:, back:n], op0=ALU.mult, op1=ALU.add).then_inc(vector_done, V.one(("V", ph, "conv", f)))
                if f >= 1:
                    up_low_V(V, ph, f - 1, n)
                if f in (KT + 1, 2 * KT + 1):
                    ada_rows_V(V, ph, WITH_ADA.index(ph), (f // KT - 1,))
                V.eng.wait_ge(scalar_done, done("A", ph, "silu", f))
                V.eng.tensor_tensor(cbuf(f, 1, n), up_bank(ph, f, 1, n), cbuf(f, 2, n), ALU.mult).then_inc(vector_done, V.one(("V", ph, "product", f)))
            V.eng.wait_ge(vector_done, V.n)
            up_low_V(V, ph, FC - 1, n)

        def up_V_both(V, ph, n, tap):
            for f in range(FC):
                for u in range(2):
                    V.eng.wait_ge(scalar_done, done("A", ph, "mid", f, u))
                    g = up_bank(ph, f, u, n).rearrange("p (s t) -> p s t", t=SEQ)
                    c = cbuf(f, u, n).rearrange("p (s t) -> p s t", t=SEQ)
                    V.eng.wait_ge(vector_done, V.n)
                    V.eng.scalar_tensor_tensor(out=c[:, :, 1:], in0=g[:, :, 0:SEQ - 1], scalar=tap(u, 0, f),
                                                      in1=c[:, :, 1:], op0=ALU.mult, op1=ALU.add).then_inc(vector_done, V.one())
                    V.eng.wait_ge(vector_done, V.n)
                    V.eng.scalar_tensor_tensor(out=c[:, :, 0:SEQ - 1], in0=g[:, :, 1:], scalar=tap(u, 2, f),
                                                      in1=c[:, :, 0:SEQ - 1], op0=ALU.mult, op1=ALU.add).then_inc(vector_done, V.one())
                    if u == 0:
                        V.note(("V", ph, "conv", f))
                if f >= 1:
                    up_low_V(V, ph, f - 1, n)
                V.eng.wait_ge(scalar_done, done("A", ph, "silu", f))
                V.eng.wait_ge(vector_done, V.n)
                V.eng.tensor_tensor(cbuf(f, 1, n), cbuf(f, 1, n), cbuf(f, 2, n), ALU.mult).then_inc(vector_done, V.one(("V", ph, "product", f)))
            V.eng.wait_ge(vector_done, V.n)
            up_low_V(V, ph, FC - 1, n)

        DOWN_BANKS = {"1.0 ffn down": (2, 3, 4, 5), "1.1 ffn down": (2, 3, 4, 5), "2.0 ffn down": tuple(range(8)), "2.1 ffn down": (0, 1, 6, 7)}

        def down_T(T, ph, up, tiles):
            n = len(tiles) * P
            banks = DOWN_BANKS[ph]
            last = FC - 1 if n > SEQ else FC - 2 if up not in WITH_ADA else FC - 3
            T.eng.wait_ge(vector_done, done("V", up, "product", last))
            tok = lambda j: slice(j * P, (j + 1) * P)
            if len(tiles) == 2:
                for f in range(FC):
                    T.eng.wait_ge(vector_done, done("V", up, "low", f))
                    wh, wl, m = take_half(T)
                    for j in range(2):
                        for half in range(2):
                            cols = slice(half * 512, half * 512 + 512)
                            i = product(T, psum[banks[2 * half + j]][:, :], (hidh(f, n)[:, tok(j)], hidl(f, n)[:, tok(j)]), (wh[:, cols], wl[:, cols]),
                                        f == 0, f == FC - 1)
                    half_read(T, i, m)
                T.note(("T", ph, "out", 0))
                T.note(("T", ph, "out", 1))
            else:
                for half in range(2):
                    for f0 in range(0, FC, 2):
                        wh, wl, m = take_half(T)
                        for c in range(2):
                            f = f0 + c
                            if half == 0:
                                T.eng.wait_ge(vector_done, done("V", up, "low", f))
                            elif f == 0:
                                T.eng.wait_ge(scalar_done, done("A", ph, "gates"))
                            for j in range(4):
                                i = product(T, psum[4 * half + j][:, :], (hidh(f, n)[:, tok(j)], hidl(f, n)[:, tok(j)]), (wh[:, c, :], wl[:, c, :]),
                                            f == 0, f == FC - 1)
                        half_read(T, i, m)
                    T.note(("T", ph, "out", half))

        def ahead_and_squares(A, ph, parts, steps, count):
            A.eng.wait_ge(scalar_done, A.n)
            A.eng.activation(stat[:, 32:33], const("ident", 0, 1), ACT.Sqrt).then_inc(scalar_done, A.one())
            per = len(parts) * steps // count
            for c in range(count // steps):
                ahead(A, first_half[ph] + steps * (c + 1) + HIGHS)
                squares_A(A, ph, [(("V", ph, "x", n), bank, t, a, b) for n, (_, bank, t, a, b) in enumerate(parts)][c * per:(c + 1) * per])

        silu_c = st2[:, 64:80].rearrange("p (k s) -> p k s", s=2)
        silu_below = st2[:, 80:112].rearrange("p (k s) -> p k s", s=4)

        def ada_tile_T(T, ph, tile, layer):
            g, k = tile // KT, tile % KT
            n = ADA_N * layer + tile
            T.eng.wait_ge(ada_full[n % 2], 16 * (n // 2 + 1))
            w = ada_slot[n % 2]
            for j in range(4):
                i = T.eng.matmul(psum[4 + g][32 * j:32 * j + 2 + 2 * layer, :], (silu_below if layer else silu_c)[:, k, :],
                                 w[:, j * 512:(j + 1) * 512], start=(k == 0), stop=(k == KT - 1))
            i.then_inc(tensor_done, T.one(("T", "ada", n)))
            if k == KT - 1:
                T.note(("T", ph, "rows", g))

        def ada_rows_V(V, ph, layer, groups):
            V.eng.wait_ge(adab_in, 16 * 8 * 2)
            for g in groups:
                V.eng.wait_ge(tensor_done, done("T", ph, "rows", g))
                for j in range(4):
                    r = slice(32 * j, 32 * j + 2 + 2 * layer)
                    m = mod[r, g * 512:(g + 1) * 512]
                    V.eng.wait_ge(vector_done, V.n)
                    V.eng.tensor_tensor(m, psum[4 + g][r, :], m, ALU.add).then_inc(vector_done, V.one())
                V.note(("V", ph, "rows", g))

        def ada_cols_T(T, ph, layer):
            T.eng.wait_ge(vector_done, done("V", WITH_ADA[layer], "rows", 2))
            n = 0
            for w, idx in enumerate((0, 1, 3, 4)):
                for k in range(KT):
                    g, j = idx // 2, (idx % 2) * 2 + k // 4
                    r = slice(32 * j, 32 * j + 4)
                    at = g * 512 + (k % 4) * P
                    i = T.eng.matmul(psum[(0, 1, 6, 7)[j]][:, 2 * n:2 * n + 2], mod[r, at:at + P],
                                     const("ident", 32 * j + 2 * layer, 32 * j + 2 * layer + 2, r), start=True, stop=True, tile_position=(32 * j, 0))
                    n += 1
            i.then_inc(tensor_done, T.one(("T", ph, "cols")))

        def ada_cols_V(V, ph, layer):
            V.eng.wait_ge(tensor_done, done("T", ph, "cols"))
            for w, idx in enumerate((0, 1, 3, 4)):
                for half in range(2):
                    a = w * 16 + half * 8
                    V.eng.wait_ge(vector_done, V.n)
                    V.eng.tensor_copy(modcol[:, layer * 64 + a:layer * 64 + a + 8],
                                      psum[(0, 1, 6, 7)[(idx % 2) * 2 + half]][:, a:a + 8]).then_inc(vector_done, V.one())
            for m, w in enumerate((1, 3)):
                g3 = veccol[:, 32 + layer * 16 + m * 8:32 + layer * 16 + m * 8 + 8].rearrange("p (k o) -> p k o", o=1).to_broadcast([P, KT, 2])
                V.eng.wait_ge(vector_done, V.n)
                V.eng.scalar_tensor_tensor(
                    out=acol[:, layer * 32 + m * 16:layer * 32 + (m + 1) * 16].rearrange("p (k s) -> p k s", s=2),
                    in0=modcol[:, layer * 64 + w * 16:layer * 64 + (w + 1) * 16].rearrange("p (k s) -> p k s", s=2),
                    scalar=1.0, in1=g3, op0=ALU.add, op1=ALU.mult).then_inc(vector_done, V.one())

        def gates_T(T, ph, idx, streams, layer):
            n = 0
            for s in streams:
                for half in range(2):
                    g, j = idx // 2, (idx % 2) * 2 + half
                    r = slice(32 * j, 32 * j + 4)
                    i = T.eng.matmul(psum[4 + 2 * streams.index(s) + half][:, :], pick(4, 32 * j + 2 * layer + s, r), mod[r, g * 512:(g + 1) * 512],
                                     start=True, stop=True, tile_position=(32 * j, 0))
                    n += 1
            i.then_inc(tensor_done, T.one(("T", ph, "gates")))

        def gates_A(A, ph, streams, up=None):
            if up is not None:
                A.eng.wait_ge(vector_done, done("V", up, "low", FC - 1))
            A.eng.wait_ge(tensor_done, done("T", ph, "gates"))
            for s in streams:
                for half in range(2):
                    A.eng.wait_ge(scalar_done, A.n)
                    A.eng.activation(gate[:, s * D + half * 512:s * D + half * 512 + 512], psum[4 + 2 * streams.index(s) + half][:, :], ACT.Copy).then_inc(scalar_done, A.one(("A", ph, "gates")))

        S1 = 3080
        tok1 = lambda t: big[:, (t - 2) * S1:(t - 1) * S1]
        f256 = lambda i: qkt[:, i * SEQ:(i + 1) * SEQ]
        frow = gate[0:NH, :]

        def turns_l0():
            return [([big[:, j * S1 + kind * 512 + pr * P:j * S1 + kind * 512 + (pr + 1) * P] for pr in (p2, p2 + 1) for j in range(2)],
                     qkt[:, (base + p2) * SEQ:(base + p2 + 2) * SEQ], scale)
                    for base, kind, scale in ((0, 0, -0.125), (4, 1, 1.0), (8, 3, -0.125), (12, 4, 1.0)) for p2 in (0, 2)]

        def jobs_l0(which):
            base = 0 if which == "dilated" else 8
            vcol = 1024 if which == "dilated" else 2560
            def scores(h, t):
                r = slice(64 * (h % 2), 64 * (h % 2) + 64)
                n = (t + 1) * P
                terms = [(f256(base + h // 2)[r, t * P:(t + 1) * P], f256(base + 4 + h // 2)[r, 0:n])]
                if which == "forget":
                    terms.append((pick(NH, h, slice(0, NH)), frow[:, 512:512 + n]))
                return [(0, n, terms)]
            mask = (lambda t: const("dilated", t * SEQ, t * SEQ + (t + 1) * P)) if which == "dilated" else \
                   (lambda t: const("causal", P - t * P, 2 * P))
            vals = lambda h, t: [big[:, c * S1 + vcol + h * DH:c * S1 + vcol + (h + 1) * DH] for c in range(t + 1)]
            off = 0 if which == "dilated" else 4
            return jobs_of_pairs(NH, (0, 1), 0, scores, lambda t: (t + 1) * P, mask, lambda h: None, vals,
                                 lambda pair: (nTh[:, off + pair, SEQ:2 * SEQ], nTl[:, off + pair, SEQ:2 * SEQ]))

        S2 = 3072
        def turns_l1():
            return [([big[:, j * S2 + kind * 1024 + pr * P:j * S2 + kind * 1024 + (pr + 1) * P] for pr in (p2, p2 + 1) for j in range(2)],
                     qkt[:, (kind * 8 + p2) * SEQ:(kind * 8 + p2 + 2) * SEQ], scale)
                    for kind, scale in ((0, -0.125), (1, 1.0)) for p2 in (0, 2, 4, 6)]

        def jobs_l1():
            jobs = []
            group = 0
            for t in range(2):
                for h0 in range(0, NH, 4):
                    for h in range(h0, h0 + 4):
                        for m in range(2):
                            r = slice(64 * m, 64 * m + 64)
                            n = (t + 1) * P
                            jobs.append(dict(
                                n=n, scores=[(0, n, [(f256(h)[r, t * P:(t + 1) * P], f256(8 + h)[r, 0:n])])],
                                mask=const("causal", P - t * P, 2 * P), sink=None, factor=(lam[:, 4:5] if m else None),
                                v=[big[:, c * S2 + 2048 + h * P:c * S2 + 2048 + (h + 1) * P] for c in range(t + 1)],
                                out=(None, slice(0, P), slice((h - h0) * P, (h - h0 + 1) * P), m == 0, m == 1, True),
                                open=(h == h0 and m == 0), group=group,
                                close=(slice(0, 512), big[:, t * S2 + h0 * P:t * S2 + (h0 + 4) * P], None) if (h == h0 + 3 and m) else None))
                    group += 1
            return jobs

        S3 = 2832 + MH

        def row3(t, a, b):
            o = t * S3 + (MH if a >= 1536 else 0)
            return big[:, o + a:o + b]

        vals3 = lambda t: big[:, t * S3 + 1024:t * S3 + 1536 + MH].rearrange("p (h e) -> p h e", e=MD + 1)
        f512 = lambda i: qkt[:, i * 512:(i + 1) * 512]
        kdup = lambda t: final_g[:, t * 256:(t + 1) * 256]

        def turns_e(part):
            g = []
            if part == 0:
                for h in range(MH):
                    g.append(([row3(t, h * P, (h + 1) * P) for t in ALL], f512(h), 1.0))
                    g.append(([row3(t, 512 + h * P, 512 + (h + 1) * P) for t in ALL], f512(4 + h), MD ** -0.5))
            else:
                for pr in range(4):
                    g.append(([row3(t, 2064 + pr * P, 2064 + (pr + 1) * P) for t in ALL], f512(8 + pr), -0.125))
                for kv in range(2):
                    g.append(([kdup(t)[:, kv * P:(kv + 1) * P] for t in ALL], f512(12 + kv), 1.0))
            return g

        def jobs_e(stream):
            def scores(h, t):
                r = slice(64 * (h % 2), 64 * (h % 2) + 64)
                return [(0, 512 if stream else 256, [(f512(8 + h // 2)[r, t * P:(t + 1) * P], f512(12 + h // 4)[r, 0:(512 if stream else 256)])])]
            n = 512 if stream else 256
            vals = lambda h, t: [row3(c, 2704 + (h // 4) * DH, 2704 + (h // 4 + 1) * DH) for c in range(n // P)]
            mask = (lambda t: const("window", (t - 2) * 512, (t - 1) * 512)) if stream else (lambda t: None)
            return jobs_of_pairs(NH, LAT if stream else CTX, 0, scores, lambda t: n, mask, lambda h: nsink[:, h:h + 1], vals,
                                 lambda pair: (nTh[:, 4 + pair, stream * SEQ:(stream + 1) * SEQ], nTl[:, 4 + pair, stream * SEQ:(stream + 1) * SEQ]))

        S4 = 2304
        row4 = lambda t, a, b: big[:, t * S4 + a:t * S4 + b]
        OQ, OK_, NQ, NK = 0, 1024, 2048, 3072

        def turns_o():
            g = [([kdup(t)[:, kv * P:(kv + 1) * P] for t in ALL], qkt[:, OK_ + kv * 512:OK_ + (kv + 1) * 512], 1.0) for kv in range(2)]
            for at, col in ((OQ, 0), (NQ, 768)):
                for p2 in (0, 2):
                    g.append(([row4(t, col + pr * P, col + (pr + 1) * P) for pr in (p2, p2 + 1) for t in LAT],
                              qkt[:, at + p2 * SEQ:at + (p2 + 2) * SEQ], -0.125))
            for pr in range(4):
                g.append(([row4(t, 1280 + pr * P, 1280 + (pr + 1) * P) for t in ALL], qkt[:, NK + pr * 512:NK + (pr + 1) * 512], 1.0))
            return g

        def nbias(h, t):
            o = (h % 4) * 512 + t * SEQ
            return qkt[:, 5120 + o:5120 + o + SEQ] if h < 4 else big[:, 4 * S4 + o:4 * S4 + o + SEQ]

        def jobs_o(which):
            def scores(h, t):
                r = slice(64 * (h % 2), 64 * (h % 2) + 64)
                if which == "global":
                    q = qkt[r, OQ + (h // 2) * SEQ + (t - 2) * P:OQ + (h // 2) * SEQ + (t - 1) * P]
                    return [(0, 512, [(q, qkt[r, OK_ + (h // 4) * 512:OK_ + (h // 4 + 1) * 512])])]
                q = qkt[r, NQ + (h // 2) * SEQ + (t - 2) * P:NQ + (h // 2) * SEQ + (t - 1) * P]
                k = NK + (h // 2) * 512
                return [(0, SEQ, [(q, qkt[r, k:k + SEQ])]),
                        (SEQ, 512, [(q, qkt[r, k + SEQ:k + 512]), (const("negflip"), nbias(h, t - 2))])]
            if which == "global":
                vals = lambda h, t: [row4(c, 640 + (h // 4) * DH, 640 + (h // 4 + 1) * DH) for c in ALL]
                mask = lambda t: None
            else:
                vals = lambda h, t: [row4(c, 1792 + h * DH, 1792 + (h + 1) * DH) for c in ALL]
                mask = lambda t: const("nbhood")
            off = 0 if which == "global" else 4
            return jobs_of_pairs(NH, LAT, 0, scores, lambda t: 512, mask, lambda h: None, vals,
                                 lambda pair: (nTh[:, off + pair, SEQ:2 * SEQ], nTl[:, off + pair, SEQ:2 * SEQ]))

        mrow = lambda d, i: (gate[0:MH, i * 512:(i + 1) * 512] if d == 0 else work[0:MH, 2560 + i * 512:3072 + i * 512])
        negM = lambda d: m_rows[0:MH, d * 512:(d + 1) * 512]
        PT = lambda d, s: work[:, d * 2048 + s * 512:d * 2048 + (s + 1) * 512]
        WT = lambda i: gate[:, (i % 4) * 512:(i % 4 + 1) * 512]
        REACH = [{s: [t for t in range(4) if t >= s] for s in range(4)}, {0: [0, 2, 3], 1: [0, 1, 2, 3], 2: [2], 3: [2, 3]}]

        def runs(tiles):
            out_, a = [], tiles[0]
            for x, y in zip(tiles, tiles[1:] + [99]):
                if y != x + 1:
                    out_.append((a * P, (x + 1) * P))
                    a = y
            return out_

        def mgate_rows_T(T, ph):
            for q in (2, 3):
                e = "VA"[q % 2]
                T.eng.wait_ge(SEM[e], done(e, "2.0 in", "piece", q))
            for g in range(4):
                for t in ALL:
                    i = T.eng.matmul(psum[7][32 * g:32 * g + MH, t * P:(t + 1) * P], row3(t, 2048 + 4 * g, 2052 + 4 * g), ident, start=True, stop=True)
            i.then_inc(tensor_done, T.one(("T", ph, "gates")))

        def mgate_cols_T(T, ph):
            T.eng.wait_ge(vector_done, done("V", ph, "rows"))
            n = 0
            for d in range(2):
                for what in range(2):
                    for t in ALL:
                        i = T.eng.matmul(psum[7][:, 4 * n:4 * n + 4], mrow(d, what)[:, t * P:(t + 1) * P],
                                         const("ident", 0, MH, slice(0, MH)), start=True, stop=True)
                        n += 1
            i.then_inc(tensor_done, T.one(("T", ph, "cols")))

        def log_sigmoid(V, A, ph, key, x, t1, t2):
            if V is not None:
                V.eng.wait_ge(vector_done, V.n)
                V.eng.scalar_tensor_tensor(out=t1, in0=x, scalar=-1.0, in1=x, op0=ALU.mult, op1=ALU.max).then_inc(vector_done, V.one(("V", ph, "abs", key)))
                V.eng.wait_ge(scalar_done, done("A", ph, "log", key))
                V.eng.wait_ge(vector_done, V.n)
                V.eng.scalar_tensor_tensor(out=x, in0=x, scalar=0.0, in1=t2, op0=ALU.min, op1=ALU.subtract).then_inc(vector_done, V.one())
            else:
                A.eng.wait_ge(vector_done, done("V", ph, "abs", key))
                A.eng.wait_ge(scalar_done, A.n)
                A.eng.activation(t1, t1, ACT.Exp, scale=-1.0).then_inc(scalar_done, A.one())
                A.eng.wait_ge(scalar_done, A.n)
                A.eng.activation(t2, t1, ACT.Ln, bias=1.0).then_inc(scalar_done, A.one(("A", ph, "log", key)))

        def mgate_V(V, ph):
            V.eng.wait_ge(tensor_done, done("T", ph, "gates"))
            for g in range(4):
                V.eng.wait_ge(vector_done, V.n)
                V.eng.tensor_scalar(mrow(g // 2, g % 2), psum[7][32 * g:32 * g + MH, :], gbias[0:MH, g:g + 1], None, ALU.add).then_inc(vector_done, V.one())
            for d in range(2):
                a, f, B, M = (mrow(d, i) for i in range(4))
                log_sigmoid(V, None, ph, d, f, B, M)
                zero = work[0:MH, 2048:2560]
                if d == 0:
                    V.eng.wait_ge(vector_done, V.n)
                    V.eng.memset(zero, 0.0).then_inc(vector_done, V.one())
                    V.eng.wait_ge(vector_done, V.n)
                    V.eng.tensor_tensor_scan(B, f, zero, 0.0, ALU.add, ALU.add).then_inc(vector_done, V.one())
                    V.eng.wait_ge(vector_done, V.n)
                    V.eng.tensor_tensor(a, a, B, ALU.subtract).then_inc(vector_done, V.one())
                    V.eng.wait_ge(vector_done, V.n)
                    V.eng.tensor_tensor_scan(M, a, a, 0.0, ALU.max, ALU.max).then_inc(vector_done, V.one())
                else:
                    c, l = (lambda x: x[:, 0:SEQ][:, ::-1]), (lambda x: x[:, SEQ:512][:, ::-1])
                    V.eng.wait_ge(vector_done, V.n)
                    V.eng.tensor_tensor_scan(c(B), c(f), c(zero), 0.0, ALU.add, ALU.add).then_inc(vector_done, V.one())
                    V.eng.wait_ge(vector_done, V.n)
                    V.eng.tensor_tensor_scan(l(B), l(f), l(zero), B[:, 0:1], ALU.add, ALU.add).then_inc(vector_done, V.one())
                    V.eng.wait_ge(vector_done, V.n)
                    V.eng.tensor_tensor(a, a, B, ALU.subtract).then_inc(vector_done, V.one())
                    V.eng.wait_ge(vector_done, V.n)
                    V.eng.tensor_tensor_scan(c(M), c(a), c(a), 0.0, ALU.max, ALU.max).then_inc(vector_done, V.one())
                    V.eng.wait_ge(vector_done, V.n)
                    V.eng.tensor_tensor_scan(l(M), l(a), l(a), M[:, 0:1], ALU.max, ALU.max).then_inc(vector_done, V.one())
                V.eng.wait_ge(vector_done, V.n)
                V.eng.tensor_tensor(f, B, M, ALU.add).then_inc(vector_done, V.one())
            V.note(("V", ph, "rows"))

        def mgate_cols_V(V, ph):
            V.eng.wait_ge(tensor_done, done("T", ph, "cols"))
            V.eng.wait_ge(vector_done, V.n)
            V.eng.tensor_copy(mcol[:, :], psum[7][:, 0:64]).then_inc(vector_done, V.one(("V", ph, "cols")))

        def mgate_A(A, ph):
            for d in range(2):
                log_sigmoid(None, A, ph, d, None, mrow(d, 2), mrow(d, 3))

        def mgate_cols_A(A, ph):
            A.eng.wait_ge(vector_done, done("V", ph, "cols"))
            for d in range(2):
                c = mcol[:, d * 32 + 16:d * 32 + 32]
                A.eng.wait_ge(scalar_done, A.n)
                A.eng.activation(c, c, ACT.Exp, scale=-1.0).then_inc(scalar_done, A.one())

        MASKED = lambda d: work[:, 4096 + d * 512:4608 + d * 512] if d == 0 else final_g[:, 0:512]
        W = MD + 1
        PIECES = [(s, d) for s in range(4) for d in range(2)]

        def mlstm_T(T, ph):
            def spread(h):
                for d in range(2):
                    if h >= 1:
                        T.eng.wait_ge(scalar_done, done("A", ph, "w", 8 * h - 1))
                        T.eng.wait_ge(vector_done, done("V", ph, "masked", 2 * (h - 1) + d))
                    i = T.eng.matmul(psum[2 + d][:, :], pick(MH, h, slice(0, MH)), negM(d), start=True, stop=True)
                    i.then_inc(tensor_done, T.one(("T", ph, "spread", 2 * h + d)))

            T.eng.wait_ge(vector_done, done("V", ph, "-M"))
            spread(0)
            for h in range(MH):
                for s in range(4):
                    n = 4 * h + s
                    if n >= 2:
                        T.eng.wait_ge(vector_done, done("V", ph, "pt", n - 2))
                    i = T.eng.matmul(psum[s % 2][:, :], f512(4 + h)[:, s * P:(s + 1) * P], f512(h), start=True, stop=True)
                    i.then_inc(tensor_done, T.one(("T", ph, "qk", n)))
                if h + 1 < MH:
                    spread(h + 1)
                for d in range(2):
                    g = 2 * h + d
                    T.eng.wait_ge(vector_done, done("V", ph, "pt", 4 * h + 3))
                    if g >= 2:
                        T.eng.wait_ge(vector_done, done("V", ph, "h", g - 2))
                    for t in range(4):
                        srcs = [s for s in range(4) if t in REACH[d][s]]
                        for m, s in enumerate(srcs):
                            i = T.eng.matmul(psum[4 + 2 * (g % 2) + t // 2][:, (t % 2) * W:(t % 2 + 1) * W], PT(d, s)[:, t * P:(t + 1) * P],
                                             vals3(s)[:, h, :], start=(m == 0), stop=(m == len(srcs) - 1))
                    i.then_inc(tensor_done, T.one(("T", ph, "sum", g)))

        def mlstm_A(A, ph):
            for h in range(MH):
                for w8, (s, d) in enumerate(PIECES):
                    w = 8 * h + w8
                    if s == 0:
                        A.eng.wait_ge(tensor_done, done("T", ph, "spread", 2 * h + d))
                        A.eng.wait_ge(vector_done, done("V", ph, "masked", 2 * h + d))
                    if w == 0:
                        A.eng.wait_ge(vector_done, done("V", ph, "-M"))
                    if w >= 4:
                        A.eng.wait_ge(vector_done, done("V", ph, "pt", (w - 4) // 2))
                    col = mcol[:, d * 32 + s * 4 + h:d * 32 + s * 4 + h + 1]
                    A.eng.activation(WT(w)[:, s * P:(s + 1) * P], MASKED(d)[:, s * P:(s + 1) * P], ACT.Exp, bias=col).then_inc(scalar_done, A.one())
                    rest = [t for t in REACH[d][s] if t != s]
                    for a, b in (runs(rest) if rest else []):
                        A.eng.activation(WT(w)[:, a:b], psum[2 + d][:, a:b], ACT.Exp, bias=col).then_inc(scalar_done, A.one())
                    A.note(("A", ph, "w", w))

        def mlstm_V(V, ph):
            def mask(h):
                for d in range(2):
                    V.eng.wait_ge(tensor_done, done("T", ph, "spread", 2 * h + d))
                    if h >= 1:
                        V.eng.wait_ge(scalar_done, done("A", ph, "w", 8 * h - 1))
                    m = const("later" if d == 0 else "earlier").rearrange("p (o n) -> p o n", o=1).to_broadcast([P, 4, P])
                    V.eng.tensor_tensor(MASKED(d).rearrange("p (t n) -> p t n", n=P), psum[2 + d][:, :].rearrange("p (t n) -> p t n", n=P),
                                        m, ALU.add).then_inc(vector_done, V.one(("V", ph, "masked", 2 * h + d)))

            def finish(g):
                h, d = g // 2, g % 2
                V.eng.wait_ge(tensor_done, done("T", ph, "sum", g))
                banks = [psum[4 + 2 * (g % 2) + i][:, 0:2 * W].rearrange("p (t e) -> p t e", e=W) for i in range(2)]
                r = st2[:, 0:4]
                for i in range(2):
                    V.eng.tensor_copy(st2[:, 4 + 2 * i:6 + 2 * i], banks[i][:, :, MD]).then_inc(vector_done, V.one())
                V.eng.wait_ge(vector_done, V.n)
                V.eng.scalar_tensor_tensor(out=r, in0=st2[:, 4:8], scalar=-1.0, in1=st2[:, 4:8], op0=ALU.mult, op1=ALU.max).then_inc(vector_done, V.one())
                e = mcol[:, d * 32 + 16:d * 32 + 32].rearrange("p (t h) -> p t h", h=MH)[:, :, h]
                V.eng.wait_ge(vector_done, V.n)
                V.eng.tensor_tensor(r, r, e, ALU.max).then_inc(vector_done, V.one())
                V.eng.wait_ge(vector_done, V.n)
                V.eng.reciprocal(r, r).then_inc(vector_done, V.one())
                hh = big[:, :].rearrange("p (t e) -> p t e", e=S3)[:, :, h * P:(h + 1) * P]
                rb = r.rearrange("p (t o) -> p t o", o=1).to_broadcast([P, 4, P])
                to = hh if d == 0 else final_g[:, 512:1024].rearrange("p (t e) -> p t e", e=P)
                for i in range(2):
                    V.eng.wait_ge(vector_done, V.n)
                    V.eng.tensor_tensor(to[:, 2 * i:2 * i + 2, :], banks[i][:, :, 0:MD], rb[:, 2 * i:2 * i + 2, :], ALU.mult).then_inc(vector_done, V.one())
                V.note(("V", ph, "h", g))
                if d == 1:
                    V.eng.wait_ge(vector_done, V.n)
                    V.eng.tensor_tensor(hh, hh, to, ALU.add).then_inc(vector_done, V.one())

            for d in range(2):
                V.eng.wait_ge(vector_done, V.n)
                V.eng.tensor_scalar(negM(d), mrow(d, 3), -1.0, None, ALU.mult).then_inc(vector_done, V.one(("V", ph, "-M")))
            mask(0)
            for h in range(MH):
                for s in range(4):
                    n = 4 * h + s
                    V.eng.wait_ge(tensor_done, done("T", ph, "qk", n))
                    if h >= 1 and s == 0:
                        V.eng.wait_ge(tensor_done, done("T", ph, "sum", 2 * h - 1))
                    for d in range(2):
                        V.eng.wait_ge(scalar_done, done("A", ph, "w", 8 * h + 2 * s + d))
                        for a, b in runs(REACH[d][s]):
                            V.eng.tensor_tensor(PT(d, s)[:, a:b], psum[s % 2][:, a:b], WT(2 * s + d)[:, a:b], ALU.mult).then_inc(vector_done, V.one())
                    V.note(("V", ph, "pt", n))
                if h + 1 < MH:
                    mask(h + 1)
                for d in range(2):
                    finish(2 * h + d)

        def mout_G(G, ph):
            G.eng.wait_ge(vector_done, done("V", "end", "2.0 mlstm"))
            G.eng.wait_ge(scalar_done, done("A", "end", "2.0 mlstm"))
            sq = work[:, 4096:4608]
            for t in ALL:
                h = row3(t, 0, 512)
                if t:
                    G.eng.wait_ge(vector_done, done("V", ph, "sum", t - 1))
                G.eng.tensor_tensor(sq, h, h, ALU.mult).then_inc(gpsimd_done, G.one(("G", ph, "squares", t)))
                G.eng.wait_ge(gpsimd_done, G.n)
                G.eng.tensor_tensor(h, h, head_g[:, :], ALU.mult).then_inc(gpsimd_done, G.one())
                G.eng.wait_ge(gpsimd_done, G.n)
                G.eng.tensor_tensor(h, h, row3(t, 1536, 2048), ALU.mult).then_inc(gpsimd_done, G.one(("G", ph, "gated", t)))
            G.eng.wait_ge(scalar_done, done("A", ph, "rstd"))
            for t in ALL:
                h = row3(t, 0, 512)
                G.eng.wait_ge(gpsimd_done, done("G", ph, "gated", t))
                G.eng.tensor_tensor(hv(h, MD), hv(h, MD), over(rms[:, t * MH:(t + 1) * MH], MH, MD), ALU.mult).then_inc(gpsimd_done, G.one(("G", ph, "out", t)))

        def mout_sum_V(V, ph, t):
            V.eng.wait_ge(gpsimd_done, done("G", ph, "squares", t))
            V.eng.tensor_reduce(rms[:, t * MH:(t + 1) * MH], hv(work[:, 4096:4608], MD), AX_X, ALU.add).then_inc(vector_done, V.one(("V", ph, "sum", t)))

        def mout_inverse_V(V, ph):
            at = TT * MH
            V.eng.wait_ge(vector_done, V.n)
            V.eng.tensor_scalar(rms[:, 0:at], rms[:, 0:at], 1.0 / MD, EPS, ALU.mult, ALU.add).then_inc(vector_done, V.one())
            V.eng.wait_ge(vector_done, V.n)
            V.eng.reciprocal(rms[:, 0:at], rms[:, 0:at]).then_inc(vector_done, V.one(("V", ph, "inverse")))

        def turns_mout():
            return [([row3(t, h * P, (h + 1) * P) for t in ALL], (nTh[:, h, :], nTl[:, h, :])) for h in range(MH)]

        def turns_sub():
            return [([big[:, j * S2 + h * P:j * S2 + (h + 1) * P] for j in range(2)], (nTh[:, h, SEQ:512], nTl[:, h, SEQ:512])) for h in range(NH)]


        def lay(kind, layer, k):
            base = {"attn": 0, "ffn": 16}[kind] + layer * 8 + k
            return veccol[:, base:base + 1]

        def tap1(layer):
            c = lambda j, f: convcol[:, layer * 88 + j * 22 + f:layer * 88 + j * 22 + f + 1]
            return c

        def tap2(layer):
            def c(u, j, f):
                o = (2 + 2 * layer) * 88 + 44 * j + 22 * u + f
                return convcol[:, o:o + 1]
            return c

        phases = []

        def phase(name, T=None, V=None, A=None, no_fence=""):
            phases.append((name, {"T": T, "V": V, "A": A}, no_fence))

        vrows, crow = work[0:80, 0:P], [work[0:88, P * (1 + i):P * (2 + i)] for i in range(6)]

        def setup_T(T):
            T.eng.wait_ge(loaded, 16 * N_LOADS)
            T.eng.transpose(psum[0][:, 0:80], vrows, const("ident", 0, 80, slice(0, 80)))
            for i in range(4):
                T.eng.transpose(psum[1][:, i * 88:(i + 1) * 88], crow[i], const("ident", 0, 88, slice(0, 88)))
            for i in range(4, 6):
                m = T.eng.transpose(psum[2][:, (i - 4) * 88:(i - 3) * 88], crow[i], const("ident", 0, 88, slice(0, 88)))
            m.then_inc(tensor_done, T.one(("T", "setup", "cols")))

        def setup_V(V):
            V.eng.wait_ge(loaded, 16 * N_LOADS)
            V.eng.wait_ge(vector_done, V.n)
            V.eng.memset(silu_below[:, :, 0:2], 0.0).then_inc(vector_done, V.one())
            V.eng.wait_ge(tensor_done, done("T", "setup", "cols"))
            V.eng.wait_ge(vector_done, V.n)
            V.eng.tensor_copy(veccol[:, :], psum[0][:, 0:80]).then_inc(vector_done, V.one(("V", "setup", "vec")))
            V.eng.wait_ge(vector_done, V.n)
            V.eng.tensor_copy(convcol[:, 0:352], psum[1][:, 0:352]).then_inc(vector_done, V.one())
            V.eng.wait_ge(vector_done, V.n)
            V.eng.tensor_copy(convcol[:, 352:528], psum[2][:, 0:176]).then_inc(vector_done, V.one())
            V.eng.wait_ge(vector_done, V.n)
            V.eng.tensor_scalar(nsink[:, :], sink[:, :], -1.0, None, ALU.mult).then_inc(vector_done, V.one())
            V.eng.wait_ge(vector_done, V.n)
            V.eng.tensor_scalar(sub_g[:, :], sub_g[:, :], 1.0 - LAM_INIT, None, ALU.mult).then_inc(vector_done, V.one())
            l4 = lam_in.rearrange("p (a b e) -> p a b e", a=2, b=2)
            pr = work[:, 2048:2176].rearrange("p (a e) -> p a e", a=2)
            V.eng.wait_ge(vector_done, V.n)
            V.eng.tensor_tensor(pr, l4[:, :, 0, :], l4[:, :, 1, :], ALU.mult).then_inc(vector_done, V.one())
            V.eng.wait_ge(vector_done, V.n)
            V.eng.tensor_reduce(lam[:, 0:2], pr, AX_X, ALU.add).then_inc(vector_done, V.one(("V", "setup", "dots")))
            V.eng.wait_ge(scalar_done, done("A", "setup", "exps"))
            V.eng.wait_ge(vector_done, V.n)
            V.eng.tensor_tensor(lam[:, 5:6], lam[:, 3:4], lam[:, 2:3], ALU.subtract).then_inc(vector_done, V.one())
            V.eng.wait_ge(vector_done, V.n)
            V.eng.tensor_scalar(lam[:, 4:5], lam[:, 5:6], LAM_INIT, None, ALU.subtract).then_inc(vector_done, V.one())

        def setup_A(A):
            A.eng.wait_ge(x_in, 16 * 2)
            for t in ALL:
                for half in range(2):
                    A.eng.wait_ge(scalar_done, A.n)
                    A.eng.activation(psum[3][:, :], xt[:, t, half * 512:half * 512 + 512], ACT.Square, scale=D ** -0.5,
                                     accum_out=stat[:, 2 * t + half:2 * t + half + 1]).then_inc(scalar_done, A.one())
            A.eng.wait_ge(vector_done, done("V", "setup", "dots"))
            A.eng.wait_ge(scalar_done, A.n)
            A.eng.activation(lam[:, 2:4], lam[:, 0:2], ACT.Exp).then_inc(scalar_done, A.one(("A", "setup", "exps")))
            A.eng.wait_ge(scalar_done, A.n)
            A.eng.activation(st2[:, 64:80].rearrange("p (k s) -> p s k", s=2),
                                    veccol[:, 64:80].rearrange("p (s k) -> p s k", s=2), ACT.Silu).then_inc(scalar_done, A.one())
            A.eng.wait_ge(scalar_done, A.n)
            A.eng.activation(silu_below[:, :, 2:4], silu_c, ACT.Copy).then_inc(scalar_done, A.one())

        def ada_bias_load(act):
            for layer in range(2):
                for j in range(4):
                    for s in range(2):
                        src = io["ada_b_2"][layer:layer + 1, :].rearrange("o (g j n) -> o g j n", g=3, j=4)[:, :, j, :]
                        dst = mod[32 * j + 2 * layer + s:32 * j + 2 * layer + s + 1, :]
                        act.dma_start(dst.rearrange("p (g n) -> p g n", g=3), src).then_inc(adab_in, 16)

        phase("setup", setup_T, setup_V, lambda A: (setup_A(A), ahead(A, HIGHS)))

        def proj_phase(ph, norm, cuts, tiles_of, dst, reader=lambda c, j: "VA"[j % 2], between={}, after_V={}, after_A={}):
            pieces = pieces_of(cuts, tiles_of, reader)
            banks = 7 if len(tiles_of(len(cuts) - 1)) == 4 else 6
            nm, tiles, which = norm
            phase(ph, lambda T: (norm_T(T, nm, tiles), proj_T(T, ph, cuts, pieces, banks, between, nm)),
                  lambda V: (norm_V(V, nm, tiles), norm_evac_V(V, nm, tiles, which), proj_read(V, ph, cuts, pieces, banks, dst, after_V)),
                  lambda A: (norm_A(A, nm, tiles), norm_evac_A(A, nm, tiles), proj_read(A, ph, cuts, pieces, banks, dst, after_A)))

        def out_phase(ph, tiles, gate_idx, layer=0):
            streams = sorted({t // 2 for t in tiles})
            gated = gate_idx is not None

            def gates_then_out_T(T):
                if gated:
                    gates_T(T, ph, gate_idx, streams, layer)
                proj_T(T, ph, OUT_CUTS, pieces, 8, {}, gates=ph if gated else None)

            pieces = pieces_of(OUT_CUTS, lambda c: tiles, lambda c, j: "V")
            parts = [(("T", ph, "piece", p["n"]), p["n"], p["t"], p["a"], p["b"]) for p in pieces]
            phase(ph, gates_then_out_T,
                  lambda V: (V.eng.wait_ge(scalar_done, done("A", ph, "gates")) if gated else None, residual_V(V, ph, parts, gated)),
                  lambda A: (gates_A(A, ph, streams) if gated else None, ahead_and_squares(A, ph, parts, 4, 8)))

        def down_parts(ph, tiles):
            k = len(tiles)
            return [(("T", ph, "out", half), DOWN_BANKS[ph][k * half + j], t, 512 * half, 512 * half + 512) for half in range(2) for j, t in enumerate(tiles)]

        def ffn_phases(ph, norm, tiles, layer, block, gate_idx):
            n = len(tiles) * P
            lo = 512 - n
            up, down = ph + " up", ph + " down"
            nm, _, which = norm
            norm_V_ = lambda V: (norm_V(V, nm, tiles), norm_evac_V(V, nm, tiles, which))
            norm_A_ = lambda A: (norm_A(A, nm, tiles), norm_evac_A(A, nm, tiles))
            if block == 1:
                tap = tap1(layer)
                phase(up, lambda T: (norm_T(T, nm, tiles), up_T(T, up, lo, n, True, nm)),
                      lambda V: (norm_V_(V), up_V_causal(V, up, n, tap)),
                      lambda A: (norm_A_(A), up_A(A, up, n, (lambda u, f: tap(2, f), lambda u, f: tap(3, f)), False)))
                phase(down, lambda T: (down_T(T, down, up, tiles), ada_cols_T(T, down, layer)),
                      lambda V: (ada_rows_V(V, up, layer, (2,)), residual_V(V, down, down_parts(down, tiles), False), ada_cols_V(V, down, layer)),
                      lambda A: ahead_and_squares(A, down, down_parts(down, tiles), FC, FC), no_fence="T")
                return
            tap = tap2(layer)
            phase(up, lambda T: (norm_T(T, nm, tiles), up_T(T, up, lo, n, False, nm)), lambda V: (norm_V_(V), up_V_both(V, up, n, tap)),
                  lambda A: (norm_A_(A), up_A(A, up, n, (lambda u, f: tap(u, 1, f), lambda u, f: tap(u, 3, f)), True)))
            streams = sorted({t // 2 for t in tiles})

            def gates_then_down_T(T):
                T.eng.wait_ge(vector_done, done("V", up, "product", FC - 3))
                gates_T(T, down, gate_idx, streams, layer)
                down_T(T, down, up, tiles)

            phase(down, gates_then_down_T, lambda V: (V.eng.wait_ge(scalar_done, done("A", down, "gates")),
                                                      residual_V(V, down, down_parts(down, tiles), True)),
                  lambda A: (gates_A(A, down, streams, up), ahead_and_squares(A, down, down_parts(down, tiles), FC // len(streams), FC)), no_fence="T")

        def turn_split_V(V, ph, groups, banks):
            for g, (srcs, (high, low)) in enumerate(groups):
                V.eng.wait_ge(scalar_done, done("A", ph, "high", g))
                V.eng.tensor_tensor(low, psum[banks[g]][:, 0:len(srcs) * P], high.bitcast(F32), ALU.subtract).then_inc(vector_done, V.one())

        def turn_split_A(A, ph, groups, banks):
            for g, (srcs, (high, low)) in enumerate(groups):
                A.eng.wait_ge(tensor_done, done("T", ph, "turn", g))
                A.eng.activation(high, psum[banks[g]][:, 0:len(srcs) * P], ACT.Copy).then_inc(scalar_done, A.one(("A", ph, "high", g)))

        def plain(base, stride):
            return lambda c, t, a, b: (big[:, (t - base) * stride + a:(t - base) * stride + b], lambda s: s, ACT.Copy)

        def att_phase(ph, jobs):
            phase(ph, lambda T: att_T(T, ph, jobs), lambda V: att_V(V, ph, jobs), lambda A: att_A(A, ph, jobs))

        l0_turns = turns_l0()

        def rope_1(V, stride, col):
            tables = [(const("cos1", j * DH, (j + 1) * DH), const("sin1", j * DH, (j + 1) * DH)) for j in range(2)]
            rope_V(V, [big[:, j * stride + col:j * stride + col + 512] for j in range(2)], 8, tables, False)
            V.note(("V", "rope", stride, col))

        def fox_T(T):
            for j in range(2):
                e = "VA"[j]
                T.eng.wait_ge(SEM[e], done(e, "1.0 in", "piece", j))
                i = T.eng.matmul(psum[7][0:NH, j * P:(j + 1) * P], big[:, j * S1 + 3072:j * S1 + 3080], ident, start=True, stop=True)
            i.then_inc(tensor_done, T.one(("T", "fox", "rows")))

        def fox_V(V):
            f, t1, c, t2 = (frow[:, i * SEQ:(i + 1) * SEQ] for i in range(4))
            V.eng.wait_ge(tensor_done, done("T", "fox", "rows"))
            V.eng.wait_ge(vector_done, V.n)
            V.eng.tensor_scalar(f, psum[7][0:NH, 0:SEQ], fbias[0:NH, 0:1], None, ALU.add).then_inc(vector_done, V.one(("V", "fox", "rows")))
            log_sigmoid(V, None, "fox", 0, f, t1, t2)
            V.eng.wait_ge(vector_done, V.n)
            V.eng.memset(t1, 0.0).then_inc(vector_done, V.one())
            V.eng.wait_ge(vector_done, V.n)
            V.eng.tensor_tensor_scan(c, f, t1, 0.0, ALU.add, ALU.add).then_inc(vector_done, V.one())

        def fox_A(A):
            log_sigmoid(None, A, "fox", 0, None, frow[:, SEQ:2 * SEQ], frow[:, 3 * SEQ:4 * SEQ])
        def turn_step(ph, groups, g, banks, *needs):
            return lambda T: turn_T(T, ph, groups, g, banks, needs)

        def evac_step(ph, groups, which, banks):
            return lambda E: turns_evac(E, ph, groups, which, banks)

        def ahead_step(ph, count):
            return lambda A: ahead(A, first_half[ph] + count)

        SIDE = (6, 7)
        both_read = lambda ph, n: [("V", ("V", ph, "piece", n)), ("A", ("A", ph, "piece", n + 1))]
        l0 = lambda g, *needs: turn_step("1.0 turn", l0_turns, g, SIDE, *needs)
        l0_evac = lambda *which: evac_step("1.0 turn", l0_turns, which, SIDE)
        proj_phase("1.0 in", ("1.0 norm", LAT, lambda k, s: (lay("attn", 0, k), None)), HYB_CUTS, lambda c: LAT, plain(2, S1),
                   between={(1, 0, 1): [fox_T],
                            (3, 0, 1): [l0(0, ("V", ("V", "rope", S1, 0)), ("V", ("V", "fox", "rows")))], (3, 1, 0): [l0(1)],
                            (4, 0, 1): [l0(2, ("V", ("V", "rope", S1, 512)))], (4, 1, 0): [l0(3)],
                            (5, 0, 1): [l0(4, *both_read("1.0 in", 6))], (5, 1, 0): [l0(5)],
                            (6, 0, 1): [l0(6, *both_read("1.0 in", 8))], (6, 1, 0): [l0(7)]},
                   after_V={0: [fox_V], 1: [lambda V: rope_1(V, S1, 0)], 2: [lambda V: rope_1(V, S1, 512), l0_evac(0, 1)],
                            3: [l0_evac(2, 3)], 4: [l0_evac(4, 5)], 5: [l0_evac(6, 7)]},
                   after_A={0: [ahead_step("1.0 in", 10), fox_A], **{c: [ahead_step("1.0 in", 4 * c + 11), l0_evac(2 * c - 4, 2 * c - 3)] for c in (2, 3, 4, 5)}})
        ja = jobs_l0("dilated")
        jb = jobs_l0("forget")
        for j in jb:
            j["group"] += 4
        att_phase("1.0 attention", ja + jb)
        out_phase("1.0 out", LAT, None)
        ffn_phases("1.0 ffn", ("1.0 norm2", LAT, lambda k, s: (lay("ffn", 0, k), None)), LAT, 0, 1, None)
        l1_turns = turns_l1()
        l1 = lambda g, *needs: turn_step("1.1 turn", l1_turns, g, SIDE, *needs)
        l1_evac = lambda *which: evac_step("1.1 turn", l1_turns, which, SIDE)
        roped = lambda col: ("V", ("V", "rope", S2, col))
        proj_phase("1.1 in", ("1.1 norm", LAT, lambda k, s: (lay("attn", 1, k), None)), QKV_CUTS, lambda c: LAT, plain(2, S2),
                   between={(2, 0, 1): [l1(0, roped(0))], (2, 1, 0): [l1(1)], (3, 0, 1): [l1(2, roped(512))], (3, 1, 0): [l1(3)],
                            (4, 0, 1): [l1(4, roped(1024))], (4, 1, 0): [l1(5)], (5, 0, 1): [l1(6, roped(1536))], (5, 1, 0): [l1(7)]},
                   after_V={0: [lambda V: rope_1(V, S2, 0)], 1: [lambda V: rope_1(V, S2, 512), l1_evac(0, 1)],
                            2: [lambda V: rope_1(V, S2, 1024), l1_evac(2, 3)],
                            3: [lambda V: rope_1(V, S2, 1536), l1_evac(4, 5)], 4: [l1_evac(6, 7)]},
                   after_A={c: [ahead_step("1.1 in", 4 * c + 11), l1_evac(2 * c - 2, 2 * c - 1)] for c in (1, 2, 3, 4)})
        j1 = jobs_l1()

        sub_rows = lambda g: big[:, (g // 2) * S2 + (g % 2) * 512:(g // 2) * S2 + (g % 2) * 512 + 512]

        def subln_sum_V(V, g):
            V.eng.wait_ge(scalar_done, done("A", "1.1 attention", "group", g))
            sq = work[:, 4096:4608]
            V.eng.wait_ge(vector_done, V.n)
            V.eng.tensor_tensor(sq, sub_rows(g), sub_rows(g), ALU.mult).then_inc(vector_done, V.one())
            V.eng.wait_ge(vector_done, V.n)
            V.eng.tensor_reduce(rms[:, 4 * g:4 * g + 4], hv(sq, P), AX_X, ALU.add).then_inc(vector_done, V.one())
            V.eng.tensor_tensor(hv(sub_rows(g), P), hv(sub_rows(g), P), under(sub_g[:, :], 4, P), ALU.mult).then_inc(vector_done, V.one())

        def subln_V(V):
            subln_sum_V(V, 3)
            V.eng.wait_ge(vector_done, V.n)
            V.eng.tensor_scalar(rms[:, 0:16], rms[:, 0:16], 1.0 / P, SUB_EPS, ALU.mult, ALU.add).then_inc(vector_done, V.one())
            V.eng.wait_ge(vector_done, V.n)
            V.eng.reciprocal(rms[:, 0:16], rms[:, 0:16]).then_inc(vector_done, V.one(("V", "subln", "inverse")))
            V.eng.wait_ge(scalar_done, done("A", "subln", "rstd"))
            for g in (0, 2, 1, 3):
                V.eng.tensor_tensor(hv(sub_rows(g), P), hv(sub_rows(g), P), over(rms[:, 4 * g:4 * g + 4], 4, P), ALU.mult).then_inc(vector_done, V.one(("V", "subln", g)))

        turns_s = turns_sub()

        def turns_sub_T(T):
            for g in range(NH):
                if g % 4 == 0:
                    T.eng.wait_ge(vector_done, done("V", "subln", 2 + g // 4))
                turn_T(T, "1.1 turn2", turns_s, g, tuple(range(8)), ())

        sub_banks = tuple(range(8))
        ph11 = "1.1 attention"
        phase(ph11, lambda T: (att_T(T, ph11, j1), turns_sub_T(T)),
              lambda V: (att_V(V, ph11, j1, {8 * g + 14: [lambda V, g=g: subln_sum_V(V, g)] for g in range(3)}), subln_V(V),
                         turn_split_V(V, "1.1 turn2", turns_s, sub_banks)),
              lambda A: (att_A(A, ph11, j1), heads_rms_A(A, "subln", 2 * NH), turn_split_A(A, "1.1 turn2", turns_s, sub_banks)))
        out_phase("1.1 out", LAT, None)
        ffn_phases("1.1 ffn", ("1.1 norm2", LAT, lambda k, s: (lay("ffn", 1, k), None)), LAT, 1, 1, None)

        def final_A(A):
            rstd_A(A, "final", LAT)
            squares_A(A, "final", [(("V", "final", "x", j), j, t, 0, D) for j, t in enumerate(LAT)])

        def final_V(V):
            rstd_V(V, "final", LAT)
            for j, t in enumerate(LAT):
                V.eng.scalar_tensor_tensor(out=xt[:, t, :], in0=xt[:, t, :], scalar=stat[:, 24 + j:25 + j], in1=final_g[:, :],
                                                  op0=ALU.mult, op1=ALU.mult).then_inc(vector_done, V.one(("V", "final", "x", j)))

        phase("1 final", None, final_V, final_A)

        def shift_scale(layer, m):
            a, b = layer * 32 + m * 16, layer * 64 + 2 * m * 16
            return lambda k, s: (acol[:, a + 2 * k + s:a + 2 * k + s + 1], modcol[:, b + 2 * k + s:b + 2 * k + s + 1])

        def dup_V(V, parts):
            V.eng.wait_ge(vector_done, V.n)
            for t, k in parts:
                d = kdup(t).rearrange("p (g two e) -> p g two e", g=2, two=2)
                for m in range(2):
                    V.eng.tensor_copy(d[:, :, m, :], k.rearrange("p (g e) -> p g e", g=2)).then_inc(vector_done, V.one())

        AXIAL = [(const("cos2", j * DH, (j + 1) * DH), const("sin2", j * DH, (j + 1) * DH)) for j in range(2)]

        def swa_prep(V):
            rows_ = [(row3(t, 2064, 2704), NH + 2) for t in ALL]
            heads_rms_V(V, "swa", rows_, DH, EPS)
            heads_scale_V(V, [part for t in ALL for part in ((row3(t, 2064, 2576), NH, 10 * t, qk_g[:, 0:DH]),
                                                             (row3(t, 2576, 2704), 2, 10 * t + NH, qk_g[:, DH:2 * DH]))])
            rope_V(V, [row3(t, 2064, 2704) for t in LAT], NH + 2, AXIAL, True)
            dup_V(V, [(t, row3(t, 2576, 2704)) for t in ALL])
            V.note(("V", "swa prep"))

        def even_dst(c, t, a, b):
            if (a, b) == (1024, 1536):
                return vals3(t)[:, :, 0:MD], lambda s: s.rearrange("p (h e) -> p h e", e=MD), ACT.Copy
            return row3(t, a, b), lambda s: s, (ACT.Sigmoid if (a, b) == (1536, 2048) else ACT.Copy)

        def value_ones(V):
            for t in ALL:
                V.eng.wait_ge(vector_done, V.n)
                V.eng.memset(vals3(t)[:, :, MD:MD + 1], 1.0).then_inc(vector_done, V.one())

        e0, e1 = turns_e(0), turns_e(1)
        LAST = (7,)
        e0_turn = lambda g, *needs: turn_step("2.0 turn", e0, g, LAST, *needs)
        e1_turn = lambda g, *needs: turn_step("2.0 turn3", e1, g, LAST, *needs)
        e0_evac, e1_evac = evac_step("2.0 turn", e0, range(8), LAST), evac_step("2.0 turn3", e1, range(6), LAST)
        proj_phase("2.0 in", ("2.0 norm", ALL, shift_scale(0, 0)), EVEN_CUTS, lambda c: ALL, even_dst, lambda c, j: "A" if c == 4 else "VA"[j % 2],
                   between={(1, 0, 1): [lambda T: mgate_rows_T(T, "mg")], (3, 1, 0): [lambda T: mgate_cols_T(T, "mg")],
                            (4, 0, 1): [e1_turn(0, ("V", ("V", "swa prep")), ("V", ("V", "mg", "cols")))], (4, 0, 2): [e1_turn(1)], (4, 0, 3): [e1_turn(2)],
                            (4, 1, 0): [e1_turn(3)], (4, 1, 1): [e1_turn(4)], (4, 1, 2): [e1_turn(5)],
                            (5, 0, 0): [e0_turn(0, ("V", ("V", "2.0 turn3", "turn", 4)), ("A", ("A", "2.0 turn3", "turn", 5)), *both_read("2.0 in", 14), *both_read("2.0 in", 10))],
                            (5, 0, 1): [e0_turn(1)], (5, 0, 2): [e0_turn(2)], (5, 0, 3): [e0_turn(3)],
                            (5, 1, 0): [e0_turn(4)], (5, 1, 1): [e0_turn(5)], (5, 1, 2): [e0_turn(6)], (5, 1, 3): [e0_turn(7)]},
                   after_V={0: [value_ones], 1: [lambda V: mgate_V(V, "mg")], 2: [swa_prep],
                            3: [lambda V: mgate_cols_V(V, "mg"), e1_evac], 4: [e0_evac]},
                   after_A={1: [lambda A: mgate_A(A, "mg")], 2: [lambda A: heads_rms_A(A, "swa", 40)],
                            3: [lambda A: mgate_cols_A(A, "mg"), ahead_step("2.0 in", 21), evac_step("2.0 turn3", e1, range(2), LAST),
                                ahead_step("2.0 in", 23), evac_step("2.0 turn3", e1, range(2, 6), LAST)],
                            4: [evac_step("2.0 turn", e0, range(2), LAST), ahead_step("2.0 in", 25), evac_step("2.0 turn", e0, range(2, 8), LAST)]})
        phase("2.0 mlstm", lambda T: mlstm_T(T, "ml"), lambda V: mlstm_V(V, "ml"), lambda A: mlstm_A(A, "ml"))

        js = jobs_e(0)
        jl = jobs_e(1)
        for j in jl:
            j["group"] += 4
        turns_m = turns_mout()
        out_done = [("G", ("G", "mo", "out", t)) for t in ALL]
        phase("2.0 attention",
              lambda T: (att_T(T, "2.0 attention", js + jl), turns_T(T, "2.0 turn2", turns_m, (7, 0, 1, 2), out_done)),
              lambda V: (att_V(V, "2.0 attention", js + jl, {**{5 + 3 * t: [lambda V, t=t: mout_sum_V(V, "mo", t)] for t in ALL},
                                                             15: [lambda V: mout_inverse_V(V, "mo")]}),
                         turn_split_V(V, "2.0 turn2", turns_m, (7, 0, 1, 2))),
              lambda A: (att_A(A, "2.0 attention", js + jl, {17: [lambda A: heads_rms_A(A, "mo", TT * MH)]}),
                         turn_split_A(A, "2.0 turn2", turns_m, (7, 0, 1, 2))))
        out_phase("2.0 out", ALL, 2)
        ffn_phases("2.0 ffn", ("2.0 norm2", ALL, shift_scale(0, 1)), ALL, 0, 2, 5)

        def bias_load(sp, n):
            rpb = io["na_rpb_2"]
            h0, t, r = 4 * (n // 4), n // 2 % 2, n % 2
            for h in range(h0, h0 + 4):
                off = h * 465 + (r - 2 * t - 1 + 7) * 31 - 63 + 15
                src = bass.AP(tensor=rpb.tensor, offset=off, ap=[[1, 64], [31, 4], [1, 64]])
                sp.dma_start(nbias(h, t)[64 * r:64 * r + 64, :].rearrange("p (a b) -> p a b", a=4), src).then_inc(bias_in, 16)

        def odd_prep(V, key, rows_, dup):
            heads_rms_V(V, key, [(row4(t, a, b), n) for t, a, b, n, g, rot in rows_], DH, EPS)
            at, parts = 0, []
            for t, a, b, n, g, rot in rows_:
                parts.append((row4(t, a, b), n, at, qk_g[:, g * DH:(g + 1) * DH]))
                at += n
            heads_scale_V(V, parts)
            turned = [(t, a, b, n) for t, a, b, n, g, rot in rows_ if rot]
            if turned:
                rope_V(V, [row4(t, a, b) for t, a, b, n in turned], turned[0][3], AXIAL, True)
            if dup:
                dup_V(V, [(t, row4(t, a, b)) for t, a, b, n, g, rot in rows_])
            V.note(("V", key))

        gk = [(t, 512, 640, 2, 3, t in LAT) for t in ALL]
        gq = [(t, 0, 512, NH, 2, True) for t in LAT]
        nq = [(t, 768, 1280, NH, 4, False) for t in LAT]
        nk = [(t, 1280, 1792, NH, 5, False) for t in ALL]
        ODD_T = lambda c: LAT if c in (1, 2) else ALL
        oo, FREE = turns_o(), (7, 2, 3, 4)
        o_turn = lambda g, *needs: turn_step("2.1 turn", oo[:4], g, LAST, *needs)
        o_evac = lambda which: evac_step("2.1 turn", oo[:4], which, LAST)
        p_turn = lambda g, *needs: turn_step("2.1 turn b", oo[4:], g, FREE, *needs)
        p_evac = evac_step("2.1 turn b", oo[4:], range(6), FREE)
        free_now = [("A", ("A", "2.1 turn", "turn", 3)), ("V", ("V", "2.1 in", "piece", 10)), ("A", ("A", "2.1 in", "piece", 11))]
        proj_phase("2.1 in", ("2.1 norm", ALL, shift_scale(1, 0)), ODD_CUTS, ODD_T, plain(0, S4),
                   between={(3, 0, 1): [o_turn(0, ("V", ("V", "odd gk")))], (3, 0, 3): [o_turn(1)],
                            (3, 1, 1): [o_turn(2, ("V", ("V", "odd gq")))], (3, 1, 3): [o_turn(3)],
                            (4, 0, 2): [p_turn(0, ("V", ("V", "odd nq")), *free_now)], (4, 0, 3): [p_turn(1)],
                            (4, 1, 2): [p_turn(2, ("V", ("V", "odd nk"))), p_turn(3)], (4, 1, 3): [p_turn(4), p_turn(5)]},
                   after_V={0: [lambda V: odd_prep(V, "odd gk", gk, True)], 1: [lambda V: odd_prep(V, "odd gq", gq, False)],
                            2: [lambda V: odd_prep(V, "odd nq", nq, False), o_evac(range(4))],
                            3: [lambda V: odd_prep(V, "odd nk", nk, False), p_evac]},
                   after_A={0: [lambda A: heads_rms_A(A, "odd gk", 8)], 1: [lambda A: heads_rms_A(A, "odd gq", 16)],
                            2: [lambda A: heads_rms_A(A, "odd nq", 16), ahead_step("2.1 in", 17), o_evac(range(2)),
                                ahead_step("2.1 in", 19), o_evac(range(2, 4))],
                            3: [lambda A: heads_rms_A(A, "odd nk", 32), p_evac]})

        jg = jobs_o("global")
        jn = jobs_o("near")
        for j in jn:
            j["group"] += 4

        def odd_att_T(T):
            T.eng.wait_ge(bias_in, 16 * 4 * NH)
            att_T(T, "2.1 attention", jg + jn)
        phase("2.1 attention", odd_att_T, lambda V: att_V(V, "2.1 attention", jg + jn), lambda A: att_A(A, "2.1 attention", jg + jn))
        out_phase("2.1 out", LAT, 2, 1)
        ffn_phases("2.1 ffn", ("2.1 norm2", LAT, shift_scale(1, 1)), LAT, 1, 2, 5)

        def bcast(v, n):
            return bass.AP(tensor=v.tensor, offset=v.offset, ap=[[0, P], [1, n]])

        rows = lambda a: a.rearrange("(r n) -> r n", n=P)
        loads = [
            (con[:, :], io["const"]),
            (vrows[0:16, :], rows(io["attn_norm"].rearrange("a n -> (a n)"))),
            (vrows[16:32, :], rows(io["ffn_norm"].rearrange("a n -> (a n)"))),
            (vrows[32:64, :], rows(io["norm_g_2"].rearrange("a b n -> (a b n)"))),
            (vrows[64:72, :], rows(io["c_ctx_2"])),
            (vrows[72:80, :], rows(io["c_2"][0])),
            (final_g[:, :], bcast(io["final_norm"], D)),
            (head_g[:, :], bcast(io["mlstm_head_g_2"], 512)),
            (sub_g[:, :], bcast(io["diff_subln"], P)),
            (qk_g[:, 0:P], bcast(io["swa_qk_g_2"], P)),
            (qk_g[:, P:2 * P], bcast(io["gqa_qk_g_2"], P)),
            (qk_g[:, 2 * P:3 * P], bcast(io["na_qk_g_2"], P)),
            (sink[:, :], bcast(io["swa_sink_2"], NH)),
            (lam_in, bcast(io["diff_lambda"], 256)),
            (gbias[0:MH, :], io["mlstm_gate_b_2"][0].rearrange("(g h) -> h g", h=MH)),
            (fbias[0:NH, :], io["hyb_b_f"][0].rearrange("(h o) -> h o", o=1)),
        ]
        for l in range(2):
            loads.append((crow[l][0:66, :], rows(io["ffn_conv_w"][l].rearrange("a n -> (a n)"))))
            loads.append((crow[l][66:88, :], rows(io["ffn_conv_b"][l])))
            w2 = rows(io["ffn_conv_w_2"][l].rearrange("a n -> (a n)"))
            loads.append((crow[2 + 2 * l][0:88, :], w2[0:88, :]))
            loads.append((crow[3 + 2 * l][0:44, :], w2[88:132, :]))
            loads.append((crow[3 + 2 * l][44:88, :], rows(io["ffn_conv_b_2"][l])))
        N_LOADS = len(loads)

        block = ctx.enter_context(nc.Block())

        def run(E):
            before = None
            for name, parts, no_fence in phases:
                if before is not None and E.name not in no_fence:
                    fence(E, before)
                if parts[E.name] is not None:
                    parts[E.name](E)
                E.note((E.name, "end", name))
                before = name
            return before

        @block.sync
        def _(sp):
            for what, u in issue:
                if what == "weights" and u == 2:
                    for dst, src in loads[N_LOADS // 3:]:
                        sp.dma_start(dst, src).then_inc(loaded, 16)
                if what == "weights" and u == SLOTS + 1:
                    ada_bias_load(sp)
                if what == "ada":
                    if u % ADA_N < 2:
                        sp.wait_ge(tensor_done, done("T", ("1.0 norm2", "1.1 norm2")[u // ADA_N], "k", KT - 1))
                    else:
                        sp.wait_ge(tensor_done, done("T", "ada", u - 2))
                    sp.dma_start(ada_slot[u % 2], ada_stream[u]).then_inc(ada_full[u % 2], 16)
                    continue
                src, view = stream[u]
                if u >= SLOTS:
                    sp.wait_ge(tensor_done, done("T", "slot", u - SLOTS))
                if 0 <= u - first_slot["2.1 in"] - SLOTS < 8:
                    bias_load(sp, u - first_slot["2.1 in"] - SLOTS)
                sp.dma_start(view(wslot[:, u % SLOTS, :]), src).then_inc(slot_full[u % SLOTS], 16)
            last = phases[-1][0]
            sp.wait_ge(vector_done, done("V", "end", last))
            sp.dma_start(out[0].rearrange("(t p) d -> p t d", p=P), xt[:, 2:4, :]).then_inc(stored, 16)
            sp.wait_ge(stored, 16)

        @block.scalar
        def _(act):
            act.dma_start(xt[:, 2:4, :], io["x"][0].rearrange("(t p) d -> p t d", p=P)).then_inc(x_in, 16)
            act.dma_start(xt[:, 0:2, :], io["ctx_2"][0].rearrange("(t p) d -> p t d", p=P)).then_inc(x_in, 16)
            for dst, src in loads[:N_LOADS // 3]:
                act.dma_start(dst, src).then_inc(loaded, 16)
            run(Progress("A", act, scalar_done, noted))

        @block.gpsimd
        def _(pool):
            G = Progress("G", pool, gpsimd_done, noted)
            before = first_half["2.0 out"] + HIGHS
            lows_G(G, 0, before)
            mout_G(G, "mo")
            lows_G(G, before, len(halves))

        @block.tensor
        def _(pe):
            run(Progress("T", pe, tensor_done, noted))
            assert Count.half == Count.high == len(halves)

        @block.vector
        def _(dve):
            run(Progress("V", dve, vector_done, noted))


_INS = ["x", "attn_norm", "ffn_norm", "final_norm", "hyb_w_in", "hyb_b_f", "hyb_w_out", "diff_w_qkv", "diff_lambda",
        "diff_subln", "diff_w_out", "ffn_w_up", "ffn_conv_w", "ffn_conv_b", "ffn_w_down", "c_2", "ctx_2", "c_ctx_2",
        "ada_w_2", "ada_b_2", "norm_g_2", "w_out_2", "ffn_up_2", "ffn_conv_w_2", "ffn_conv_b_2", "ffn_down_2",
        "even_w_in_2", "mlstm_gate_b_2", "mlstm_head_g_2", "swa_qk_g_2", "swa_sink_2", "odd_w_in_2", "gqa_qk_g_2",
        "na_qk_g_2", "na_rpb_2"]


def kernel(**inputs):
    import concourse.bacc as bacc
    from concourse.bass_utils import run_bass_kernel_spmd

    known, noted = {}, {}
    for _ in range(2):
        nc = bacc.Bacc("TRN2", target_bir_lowering=False, num_devices=1, dynamic_dma_scratch_size=1024)
        arrays, io = {}, {}
        for name in _INS + ["const"]:
            a = constants() if name == "const" else np.ascontiguousarray(inputs[name])
            arrays[f"in_{name}"] = a
            io[name] = nc.dram_tensor(f"in_{name}", a.shape, F32, kind="ExternalInput").ap()
        out = nc.dram_tensor("out_0", (1, SEQ, D), F32, kind="ExternalOutput").ap()
        noted = {}
        with nc.allow_non_contiguous_dma(reason="columns of weights, and a few small vectors"):
            program(nc, io, out, known, noted)
        known = noted
    r = run_bass_kernel_spmd(nc, [arrays], core_ids=[0])
    return r.results[0]["out_0"]
```
